# Optimizing a Trainium2 kernel written in Bass

```python
import math
import functools
import jax
import jax.numpy as jnp
from jax import lax
import numpy as np

D_MODEL = 1024
BATCH = 1
SEQ = 1024
DEPTH = 2
DEC_BATCH = 8
DEC_SEQ = 4
PAST_LEN = 1024
PAGE_SIZE = 128

HEAD_DIM = 128
N_MEM = 256
ML_HEADS = 4
ML_W = ML_HEADS * HEAD_DIM
ML_CHUNK = 128
GM_GROUPS = 4
GM_GW = 128
GM_W = GM_GROUPS * GM_GW
GM_CHUNK = 128
AT_HEADS = 8
AT_KV_HEADS = 2
AT_W = AT_HEADS * HEAD_DIM
KV_W = AT_KV_HEADS * HEAD_DIM
IDX_HEADS = 8
IDX_DIM = 64
TOPK_MAX = 256
Q_BLOCK = 128
XA_HEADS = 4
XA_W = XA_HEADS * HEAD_DIM
ROPE_THETA = 500000.0
ROPE_FRAC = 4
NORM_EPS = 1e-6
N_EVEN = (DEPTH + 1) // 2
N_ODD = DEPTH // 2

EVEN_SPLITS = (ML_W, ML_W, ML_W, ML_W, ML_HEADS, ML_HEADS, ML_W,
               GM_W, GM_W, GM_W,
               XA_W, XA_W)
ODD_SPLITS = (AT_W, KV_W, KV_W, AT_W,
              IDX_HEADS * IDX_DIM, IDX_HEADS, IDX_DIM,
              XA_W, XA_W)
EVEN_IN = sum(EVEN_SPLITS)
ODD_IN = sum(ODD_SPLITS)
EVEN_OUT = ML_W + GM_W + XA_W
ODD_OUT = AT_W + XA_W

kernel_name = 'hybrid_mlstm_gmlp_dsa_decoder_step'

def _rms(x, g):
    xf = x.astype(jnp.float32)
    y = xf * lax.rsqrt(jnp.mean(xf * xf, axis=-1, keepdims=True) + NORM_EPS)
    return (y * g.astype(jnp.float32)).astype(x.dtype)

def _layernorm(x, g, b):
    xf = x.astype(jnp.float32)
    xc = xf - jnp.mean(xf, axis=-1, keepdims=True)
    var = jnp.mean(xc * xc, axis=-1, keepdims=True)
    y = xc * lax.rsqrt(var + NORM_EPS) * g.astype(jnp.float32) + b.astype(jnp.float32)
    return y.astype(x.dtype)

def _split(h, sizes):
    cuts = np.cumsum(np.asarray(sizes))[:-1].tolist()
    return jnp.split(h, cuts, axis=-1)

def _rope(x, pos):
    rd = x.shape[-1] // ROPE_FRAC
    half = rd // 2
    inv = ROPE_THETA ** (-jnp.arange(half, dtype=jnp.float32) / half)
    ang = pos.astype(jnp.float32)[:, None] * inv[None, :]
    cos = jnp.cos(ang)[:, None, :]
    sin = jnp.sin(ang)[:, None, :]
    xf = x.astype(jnp.float32)
    x1, x2 = xf[..., :half], xf[..., half:rd]
    out = jnp.concatenate([x1 * cos - x2 * sin, x2 * cos + x1 * sin, xf[..., rd:]], axis=-1)
    return out.astype(x.dtype)

def _mlstm(q, k, v, log_i, log_f, C0, n0, m0):
    B, T, H, Dh = q.shape
    L = math.gcd(T, ML_CHUNK)
    nc = T // L

    def to_chunks(a):
        return jnp.moveaxis(a.reshape((B, nc, L) + a.shape[2:]), 1, 0)

    causal = jnp.tril(jnp.ones((L, L), dtype=bool))

    def step(carry, inp):
        C, n, m = carry
        qc, kc, vc, li, lf = inp
        b = jnp.cumsum(lf, axis=1)
        dlog = b[:, :, None, :] - b[:, None, :, :] + li[:, None, :, :]
        dlog = jnp.where(causal[None, :, :, None], dlog, -jnp.inf)
        inter = b + m[:, None, :]
        m_t = jnp.maximum(inter, jnp.max(dlog, axis=2))
        w_intra = jnp.exp(dlog - m_t[:, :, None, :])
        w_inter = jnp.exp(inter - m_t)
        qk = jnp.einsum('bjhd,bshd->bjsh', qc, kc) * w_intra
        num = jnp.einsum('bjsh,bshd->bjhd', qk, vc) + w_inter[..., None] * jnp.einsum('bjhd,bhde->bjhe', qc, C)
        den = jnp.sum(qk, axis=2) + w_inter * jnp.einsum('bjhd,bhd->bjh', qc, n)
        h = num / jnp.maximum(jnp.abs(den), jnp.exp(-m_t))[..., None]
        b_end = b[:, -1, :]
        g = b_end[:, None, :] - b + li
        m_new = jnp.maximum(b_end + m, jnp.max(g, axis=1))
        a_prev = jnp.exp(b_end + m - m_new)
        a_tok = jnp.exp(g - m_new[:, None, :])
        C_new = a_prev[..., None, None] * C + jnp.einsum('bsh,bshd,bshe->bhde', a_tok, kc, vc)
        n_new = a_prev[..., None] * n + jnp.einsum('bsh,bshd->bhd', a_tok, kc)
        return (C_new, n_new, m_new), h

    init = (C0.astype(jnp.float32), n0.astype(jnp.float32), m0.astype(jnp.float32))
    (C, n, m), hs = lax.scan(step, init, tuple(map(to_chunks, (q, k, v, log_i, log_f))))
    return jnp.moveaxis(hs, 0, 1).reshape(B, T, H, Dh), C, n, m

def _gmlp(u, v, w_s, b_s):
    B, T, _ = v.shape
    nck = max(T // GM_CHUNK, 1)
    c = T // nck
    w = jnp.where(jnp.tril(jnp.ones((c, c), dtype=bool))[None], w_s[:, :c, :c], 0.0)
    vg = v.reshape(B, nck, c, GM_GROUPS, GM_GW)
    mixed = jnp.einsum('gts,bnsgc->bntgc', w, vg) + b_s[:, :c].T[None, None, :, :, None]
    return u * mixed.reshape(B, T, GM_W).astype(u.dtype)

def _mem_kv(mem, w_kv, kn):
    B, M, _ = mem.shape
    mk, mv = _split(mem @ w_kv, (XA_W, XA_W))
    mk = _rms(mk.reshape(B, M, XA_HEADS, HEAD_DIM), kn)
    return mk, mv.reshape(B, M, XA_HEADS, HEAD_DIM)

def _mem_attn(xq, mk, mv, qn):
    q = _rms(xq, qn)
    s = jnp.einsum('bthd,bmhd->bhtm', q, mk).astype(jnp.float32) * HEAD_DIM ** -0.5
    p = jax.nn.softmax(s, axis=-1).astype(mv.dtype)
    return jnp.einsum('bhtm,bmhd->bthd', p, mv)

def _index_select(qi, wi, ki, qpos, topk):
    s = jnp.einsum('bqhd,bld->bqhl', qi.astype(jnp.float32), ki.astype(jnp.float32)) * IDX_DIM ** -0.5
    s = jnp.einsum('bqhl,bqh->bql', jax.nn.relu(s), wi.astype(jnp.float32))
    kpos = jnp.arange(ki.shape[1])
    s = jnp.where((kpos[None, :] <= qpos[:, None])[None], s, -jnp.inf)
    _, idx = lax.top_k(s, topk)
    return idx, idx <= qpos[None, :, None]

def _sparse_attend(q, kg, vg, valid):
    B, Q, H, Dh = q.shape
    qg = q.reshape(B, Q, AT_KV_HEADS, H // AT_KV_HEADS, Dh)
    s = jnp.einsum('bqngd,bqknd->bqngk', qg, kg).astype(jnp.float32) * Dh ** -0.5
    s = jnp.where(valid[:, :, None, None, :], s, -jnp.inf)
    p = jax.nn.softmax(s, axis=-1).astype(vg.dtype)
    return jnp.einsum('bqngk,bqknd->bqngd', p, vg).reshape(B, Q, H, Dh)

def _dsa_prompt(q, k, v, qi, wi, ki):
    B, S = q.shape[:2]
    topk = min(TOPK_MAX, S // 4)
    take = jax.vmap(lambda rows, idx: rows[idx])

    def block(i):
        s0 = i * Q_BLOCK
        sl = lambda a: lax.dynamic_slice_in_dim(a, s0, Q_BLOCK, axis=1)
        qpos = s0 + jnp.arange(Q_BLOCK)
        idx, valid = _index_select(sl(qi), sl(wi), ki, qpos, topk)
        return _sparse_attend(sl(q), take(k, idx), take(v, idx), valid)

    out = lax.map(block, jnp.arange(S // Q_BLOCK))
    return jnp.moveaxis(out, 0, 1).reshape(B, S, AT_HEADS, HEAD_DIM)

def _paged_take(pool, layer, page_table, idx, new_rows):
    past = page_table.shape[1] * PAGE_SIZE
    pidx = jnp.minimum(idx, past - 1)
    phys = jax.vmap(lambda pt, pi: pt[pi])(page_table, pidx // PAGE_SIZE)
    rows_past = pool[layer, phys, pidx % PAGE_SIZE].astype(new_rows.dtype)
    nidx = jnp.clip(idx - past, 0, new_rows.shape[1] - 1)
    rows_new = jax.vmap(lambda r, i: r[i])(new_rows, nidx)
    in_past = idx < past
    mask = in_past.reshape(in_past.shape + (1,) * (rows_new.ndim - in_past.ndim))
    return jnp.where(mask, rows_past, rows_new)

def _dsa_sample(q, k, v, qi, wi, ki, layer, cache_k, cache_v, cache_ik, page_table):
    Bd, T = q.shape[:2]
    past = page_table.shape[1] * PAGE_SIZE
    topk = min(TOPK_MAX, (past + T) // 4)
    ki_past = cache_ik[layer, page_table].reshape(Bd, past, IDX_DIM).astype(ki.dtype)
    ki_all = jnp.concatenate([ki_past, ki], axis=1)
    qpos = past + jnp.arange(T)
    idx, valid = _index_select(qi, wi, ki_all, qpos, topk)
    kg = _paged_take(cache_k, layer, page_table, idx, k)
    vg = _paged_take(cache_v, layer, page_table, idx, v)
    return _sparse_attend(q, kg, vg, valid)

def _even_layer(x, mk, mv, C0, n0, m0, norm_g, w_in, b_if, h_g, ln_g, ln_b, w_s, b_s, w_out, mem_qn):
    B, T, _ = x.shape
    xn = _rms(x, norm_g)
    q, k, v, o, ig, fg, g_a, u, vb, g_b, xq, g_x = _split(xn @ w_in, EVEN_SPLITS)
    heads = lambda a, n: a.reshape(B, T, n, HEAD_DIM)
    f32 = jnp.float32
    log_i = (ig + b_if[:ML_HEADS]).astype(f32)
    log_f = jax.nn.log_sigmoid((fg + b_if[ML_HEADS:]).astype(f32))
    hA, C, n, m = _mlstm(heads(q, ML_HEADS).astype(f32),
                         heads(k, ML_HEADS).astype(f32) * HEAD_DIM ** -0.5,
                         heads(v, ML_HEADS).astype(f32), log_i, log_f, C0, n0, m0)
    hA = _rms(hA, h_g.reshape(ML_HEADS, HEAD_DIM)).reshape(B, T, ML_W).astype(x.dtype)
    yA = hA * jax.nn.sigmoid(o) * jax.nn.silu(g_a)
    vbn = _layernorm(vb, ln_g, ln_b)
    yB = _gmlp(u, vbn, w_s, b_s) * jax.nn.silu(g_b)
    yX = _mem_attn(heads(xq, XA_HEADS), mk, mv, mem_qn).reshape(B, T, XA_W) * jax.nn.silu(g_x)
    y = jnp.concatenate([yA, yB, yX.astype(yA.dtype)], axis=-1) @ w_out
    return x + y.astype(x.dtype), (C, n, m), vbn

def _odd_layer(x, pos, mk, mv, attend, norm_g, w_in, qn, kn, w_out, mem_qn):
    B, T, _ = x.shape
    xn = _rms(x, norm_g)
    q, k, v, g_c, qi, wi, ki, xq, g_x = _split(xn @ w_in, ODD_SPLITS)
    heads = lambda a, n: a.reshape(B, T, n, HEAD_DIM)
    q = _rope(_rms(heads(q, AT_HEADS), qn), pos)
    k = _rope(_rms(heads(k, AT_KV_HEADS), kn), pos)
    v = heads(v, AT_KV_HEADS)
    qi = _rope(qi.reshape(B, T, IDX_HEADS, IDX_DIM), pos)
    ki = _rope(ki[:, :, None, :], pos)[:, :, 0, :]
    wi = wi * IDX_HEADS ** -0.5
    yC = attend(q, k, v, qi, wi, ki).reshape(B, T, AT_W) * jax.nn.silu(g_c)
    yX = _mem_attn(heads(xq, XA_HEADS), mk, mv, mem_qn).reshape(B, T, XA_W) * jax.nn.silu(g_x)
    y = jnp.concatenate([yC, yX.astype(yC.dtype)], axis=-1) @ w_out
    return x + y.astype(x.dtype), (k, v, ki)

def setup_inputs(seed: int = 0) -> dict:
    key = jax.random.key(seed)
    keys = jax.random.split(key, 32)

    def nrm(i, shape, scale=1.0):
        return scale * jax.random.normal(keys[i], shape, jnp.float32)

    n_pages = PAST_LEN // PAGE_SIZE
    n_used = DEC_BATCH * n_pages
    n_pool = n_used + max(1, n_used // 4)
    page_table = jax.random.permutation(keys[10], n_pool)[:n_used].reshape(DEC_BATCH, n_pages).astype(jnp.int32)
    b_if = jnp.concatenate([nrm(14, (N_EVEN, ML_HEADS), 0.1),
                            3.0 + nrm(15, (N_EVEN, ML_HEADS), 0.5)], axis=-1)
    return {
        'x_prompt': nrm(0, (BATCH, SEQ, D_MODEL)),
        'x_sample': nrm(1, (DEC_BATCH, DEC_SEQ, D_MODEL)),
        'state_mlstm_C': nrm(2, (N_EVEN, DEC_BATCH, ML_HEADS, HEAD_DIM, HEAD_DIM), 0.05),
        'state_mlstm_n': nrm(3, (N_EVEN, DEC_BATCH, ML_HEADS, HEAD_DIM), 0.05),
        'state_mlstm_m': nrm(4, (N_EVEN, DEC_BATCH, ML_HEADS), 0.5),
        'cache_attn_k': nrm(5, (N_ODD, n_pool, PAGE_SIZE, AT_KV_HEADS, HEAD_DIM)),
        'cache_attn_v': nrm(6, (N_ODD, n_pool, PAGE_SIZE, AT_KV_HEADS, HEAD_DIM)),
        'cache_idx_k': nrm(7, (N_ODD, n_pool, PAGE_SIZE, IDX_DIM)),
        'cache_mem_k': nrm(8, (DEPTH, DEC_BATCH, N_MEM, XA_HEADS, HEAD_DIM)),
        'cache_mem_v': nrm(9, (DEPTH, DEC_BATCH, N_MEM, XA_HEADS, HEAD_DIM)),
        'page_table': page_table,
        'mem_prompt': nrm(11, (BATCH, N_MEM, D_MODEL)),
        'norm_even': 1.0 + nrm(12, (N_EVEN, D_MODEL), 0.02),
        'w_in_even': nrm(13, (N_EVEN, D_MODEL, EVEN_IN), D_MODEL ** -0.5),
        'b_if_even': b_if,
        'mlstm_hnorm': 1.0 + nrm(16, (N_EVEN, ML_W), 0.02),
        'gmlp_ln_g': 1.0 + nrm(17, (N_EVEN, GM_W), 0.02),
        'gmlp_ln_b': nrm(18, (N_EVEN, GM_W), 0.02),
        'gmlp_w': nrm(19, (N_EVEN, GM_GROUPS, GM_CHUNK, GM_CHUNK), GM_CHUNK ** -0.5),
        'gmlp_b': nrm(20, (N_EVEN, GM_GROUPS, GM_CHUNK), 0.1),
        'w_out_even': nrm(21, (N_EVEN, EVEN_OUT, D_MODEL), EVEN_OUT ** -0.5),
        'norm_odd': 1.0 + nrm(22, (N_ODD, D_MODEL), 0.02),
        'w_in_odd': nrm(23, (N_ODD, D_MODEL, ODD_IN), D_MODEL ** -0.5),
        'attn_qn': 1.0 + nrm(24, (N_ODD, HEAD_DIM), 0.02),
        'attn_kn': 1.0 + nrm(25, (N_ODD, HEAD_DIM), 0.02),
        'w_out_odd': nrm(26, (N_ODD, ODD_OUT, D_MODEL), ODD_OUT ** -0.5),
        'w_mem_kv': nrm(27, (DEPTH, D_MODEL, 2 * XA_W), D_MODEL ** -0.5),
        'mem_qn': 1.0 + nrm(28, (DEPTH, HEAD_DIM), 0.02),
        'mem_kn': 1.0 + nrm(29, (DEPTH, HEAD_DIM), 0.02),
    }

def reference(x_prompt, x_sample, state_mlstm_C, state_mlstm_n, state_mlstm_m,
              cache_attn_k, cache_attn_v, cache_idx_k, cache_mem_k, cache_mem_v,
              page_table, mem_prompt,
              norm_even, w_in_even, b_if_even, mlstm_hnorm, gmlp_ln_g, gmlp_ln_b,
              gmlp_w, gmlp_b, w_out_even,
              norm_odd, w_in_odd, attn_qn, attn_kn, w_out_odd,
              w_mem_kv, mem_qn, mem_kn):
    B, S, _ = x_prompt.shape
    Bd, T, _ = x_sample.shape
    past = page_table.shape[1] * PAGE_SIZE
    pos_p = jnp.arange(S)
    pos_s = past + jnp.arange(T)
    zero_C = jnp.zeros((B, ML_HEADS, HEAD_DIM, HEAD_DIM), jnp.float32)
    zero_n = jnp.zeros((B, ML_HEADS, HEAD_DIM), jnp.float32)
    zero_m = jnp.zeros((B, ML_HEADS), jnp.float32)
    xp, xs = x_prompt, x_sample
    mlC_p, mln_p, mlm_p, mlC_s, mln_s, mlm_s, gv_s = [], [], [], [], [], [], []
    ak_p, av_p, ik_p, ak_s, av_s, ik_s, memk_p, memv_p = [], [], [], [], [], [], [], []
    for l in range(DEPTH):
        mk_p, mv_p = _mem_kv(mem_prompt, w_mem_kv[l], mem_kn[l])
        memk_p.append(mk_p)
        memv_p.append(mv_p)
        if l % 2 == 0:
            e = l // 2
            prm = (norm_even[e], w_in_even[e], b_if_even[e], mlstm_hnorm[e], gmlp_ln_g[e], gmlp_ln_b[e],
                   gmlp_w[e], gmlp_b[e], w_out_even[e], mem_qn[l])
            xp, (c, n, m), _ = _even_layer(xp, mk_p, mv_p, zero_C, zero_n, zero_m, *prm)
            mlC_p.append(c)
            mln_p.append(n)
            mlm_p.append(m)
            xs, (c, n, m), vrows = _even_layer(xs, cache_mem_k[l], cache_mem_v[l], state_mlstm_C[e],
                                               state_mlstm_n[e], state_mlstm_m[e], *prm)
            mlC_s.append(c)
            mln_s.append(n)
            mlm_s.append(m)
            gv_s.append(vrows)
        else:
            o = l // 2
            prm = (norm_odd[o], w_in_odd[o], attn_qn[o], attn_kn[o], w_out_odd[o], mem_qn[l])
            xp, (k, v, ki) = _odd_layer(xp, pos_p, mk_p, mv_p, _dsa_prompt, *prm)
            ak_p.append(k)
            av_p.append(v)
            ik_p.append(ki)
            attend_s = functools.partial(_dsa_sample, layer=o, cache_k=cache_attn_k, cache_v=cache_attn_v,
                                         cache_ik=cache_idx_k, page_table=page_table)
            xs, (k, v, ki) = _odd_layer(xs, pos_s, cache_mem_k[l], cache_mem_v[l], attend_s, *prm)
            ak_s.append(k)
            av_s.append(v)
            ik_s.append(ki)
    return (xp, xs,
            jnp.stack(mlC_p), jnp.stack(mln_p), jnp.stack(mlm_p),
            jnp.stack(mlC_s), jnp.stack(mln_s), jnp.stack(mlm_s),
            jnp.stack(gv_s),
            jnp.stack(ak_p), jnp.stack(av_p), jnp.stack(ik_p),
            jnp.stack(ak_s), jnp.stack(av_s), jnp.stack(ik_s),
            jnp.stack(memk_p), jnp.stack(memv_p))


_drawn_inputs = setup_inputs


def setup_inputs(seed=0):
    import zlib

    import numpy as np

    out = dict(_drawn_inputs(seed))
    spreads = {}
    factors = {'mlstm_hnorm': 8.0,
     'gmlp_ln_g': 3.0,
     'gmlp_ln_b': 2.991,
     'norm_odd': 2.785,
     'attn_qn': 8.0,
     'attn_kn': 3.022,
     'mem_qn': 8.0,
     'mem_kn': 3.18}
    for name, (base, spread) in spreads.items():
        noise = np.random.default_rng([zlib.crc32(name.encode()), seed]).standard_normal(out[name].shape)
        drawn = base * np.exp(spread * noise) if base else spread * noise
        out[name] = jnp.asarray(drawn.astype(out[name].dtype))
    for name, factor in factors.items():
        out[name] = (out[name] * factor).astype(out[name].dtype)
    return out
```

```python
import concourse.bass as bass
from concourse import mybir
from contextlib import ExitStack
import numpy as np

F32 = mybir.dt.float32
F32R = mybir.dt.float32r
ALU = mybir.AluOpType
ACT = mybir.ActivationFunctionType
AX = mybir.AxisListType

P = 128
D = 1024
KC = D // P
SEQ = 1024
NB, NT = 8, 4
SMP = NB * NT
TOK = SEQ + SMP
TILES = SEQ // P
HD = 128
NH = 4
MEM = 256
MC = MEM // P
QH, KVH = 8, 2
IH, ID = 8, 64
PAGES = 8
PAST = PAGES * P
TOPK = 256
EPS = 1e-6
NEG = -1e30
CUT = -3.0e38
TAKEN = -3.4e38
CW = 512
OUT_CHUNKS = 12
OUT_PIECES = 4
OUT_ROWS = OUT_CHUNKS // OUT_PIECES
W_EVEN = 10 * CW
W_ODD = 8 * CW + 72

E_Q, E_K, E_V, E_U, E_VB, E_XQ, E_GA, E_GB, E_GX, E_O = (CW * n for n in range(10))
O_Q, O_KV, O_QI, O_XQ, O_GC, O_GX, O_WK = 0, 1024, 1536, 2048, 2560, 3584, 4096


class Stage:

    def __init__(self, nc, name):
        self.nc, self.name, self.ctx, self.nums = nc, name, ExitStack(), []

    def __enter__(self):
        return self

    def __exit__(self, *e):
        return self.ctx.__exit__(*e)

    def sb(self, name, shape, dt=F32):
        return self.ctx.enter_context(self.nc.sbuf_tensor(f"{self.name}_{name}", shape, dt))

    def ps(self, name, cols=512):
        return self.ctx.enter_context(self.nc.psum_tensor(f"{self.name}_{name}", [P, cols], F32))

    def sem(self, name, n=None):
        if n is not None:
            return [self.sem(f"{name}{i}") for i in range(n)]
        sem = self.ctx.enter_context(self.nc.semaphore(f"{self.name}_{name}"))
        self.nums.append(sem.num)
        return sem

    def pool_sem(self, name, n=None):
        if n is not None:
            return [self.pool_sem(f"{name}{i}") for i in range(n)]
        return self.nc.alloc_semaphore(f"{self.name}_{name}")

    def clear(self):
        runs = []
        for n in sorted(self.nums):
            if runs and runs[-1][1] == n:
                runs[-1][1] = n + 1
            else:
                runs.append([n, n + 1])
        for lo, hi in runs:
            self.nc.all_engine_barrier(sems_to_clear=range(lo, hi))

    def block(self):
        self.ctx.callback(self.clear)
        return self.ctx.enter_context(self.nc.Block())


def each_tile(eng, body):
    with eng.Fori(0, TILES // 2) as i:
        for u in range(2):
            body(i * 2 + u, u, i + 1, P)
    body(TILES, 0, TILES // 2 + 1, SMP)


def rows_of(t, rows):
    return slice(SEQ, TOK) if rows == SMP else bass.ts(t, P)


class Link:

    def __init__(self, eng, sem):
        self.eng, self.sem, self.base, self.n, self.per = eng, sem, 0, 0, 0

    def __call__(self, ins):
        self.n += 1
        ins.then_inc(self.sem, 1)
        self.eng.wait_ge(self.sem, self.base + self.n)

    def at(self, base):
        self.base, self.n = base, 0


def split(dve, link, x, hi, lo):
    link(dve.tensor_copy(hi, x))
    return dve.tensor_tensor(lo, x, hi, ALU.subtract)


def products(pe, out, terms):
    last = len(terms) - 1
    for k, ((xh, xl), (wh, wl)) in enumerate(terms):
        pe.matmul(out, xh, wh, start=(k == 0), stop=False)
        pe.matmul(out, xh, wl, start=False, stop=False)
        ins = pe.matmul(out, xl, wh, start=False, stop=(k == last))
    return ins


def constants(nc, c, st):
    done = st.sem("made")
    with Stage(nc, "const") as s:
        block = s.block()

        @block.gpsimd
        def _(pool):
            n = [0]

            def link(ins):
                n[0] += 1
                ins.then_inc(done, 1)
                pool.wait_ge(done, n[0])

            def select(t, pattern, base, mult, op, fill):
                link(nc.gpsimd.affine_select(out=t, in_=t, compare_op=op, fill=fill, base=base,
                                             pattern=pattern, channel_multiplier=mult))

            link(nc.gpsimd.memset(c.ident[:, :], 0.0))
            select(c.ident[:, :], [[-1, P]], 0, 1, ALU.not_equal, 1.0)
            link(nc.gpsimd.memset(c.neg_sj[:, :], 0.0))
            select(c.neg_sj[:, :], [[1, P]], 0, -1, ALU.is_ge, NEG)
            link(nc.gpsimd.memset(c.causal[:, :], 1.0))
            select(c.causal[:, :], [[1, P]], 0, -1, ALU.is_ge, 0.0)
            link(nc.gpsimd.memset(c.neg_qk[:, :], 0.0))
            select(c.neg_qk[:, :], [[-1, P]], 0, 1, ALU.is_ge, NEG)
            link(nc.gpsimd.memset(c.lid_qk[:, :], 3.0e38))
            select(c.lid_qk[:, :], [[-1, P]], 0, 1, ALU.is_ge, CUT)
            link(nc.gpsimd.memset(c.neg_smp[:, :], 0.0))
            select(c.neg_smp[:, :], [[1, SMP]], 0, -1, ALU.is_ge, NEG)
            v = c.neg_smp[:, :].rearrange("p (b t) -> p b t", t=NT)
            select(v, [[-NT, NB], [0, NT]], 0, 1, ALU.is_ge, NEG)
            link(nc.gpsimd.memset(c.causal_smp[:, :], 1.0))
            select(c.causal_smp[:, :], [[-1, SMP]], 0, 1, ALU.is_ge, 0.0)
            v = c.causal_smp[:, :].rearrange("p (b t) -> p b t", t=NT)
            select(v, [[NT, NB], [0, NT]], NT - 1, -1, ALU.is_ge, 0.0)
            link(nc.gpsimd.memset(c.of_seq[0:SMP, :], 1.0))
            select(c.of_seq[0:SMP, :], [[-NT, NB]], 0, 1, ALU.is_ge, 0.0)
            select(c.of_seq[0:SMP, :], [[NT, NB]], NT - 1, -1, ALU.is_ge, 0.0)
            for g in range(1, 4):
                link(nc.gpsimd.tensor_copy(c.of_seq[32 * g:32 * g + 32, :], c.of_seq[0:SMP, :]))
            link(nc.gpsimd.memset(c.seq_cols[:, :, :], 1.0))
            select(c.seq_cols[:, :, :], [[-NT, NB], [1, SMP]], 0, 0, ALU.is_ge, 0.0)
            select(c.seq_cols[:, :, :], [[NT, NB], [-1, SMP]], NT - 1, 0, ALU.is_ge, 0.0)
            link(nc.gpsimd.memset(c.head_row[:, :, :], 1.0))
            select(c.head_row[:, :, :], [[1, NH], [0, P]], 0, -1, ALU.is_equal, 0.0)
            for g in range(4):
                link(nc.gpsimd.tensor_copy(c.tok_of[32 * g:32 * g + 32, :],
                                           c.ident[32 * g:32 * g + 32, 32 * g:32 * g + 32]))
                link(nc.gpsimd.tensor_copy(c.tok_to[:, 32 * g:32 * g + 32], c.ident[0:32, 0:32]))
            link(nc.gpsimd.memset(c.half[:, :], -0.5))
            link(nc.gpsimd.memset(c.eps[:, :], EPS))
            link(nc.gpsimd.memset(c.one[:, :], 1.0))
            link(nc.gpsimd.memset(c.inv_d[:, :], 1.0 / D))
            link(nc.gpsimd.memset(c.inv_hd[:, :], 1.0 / HD))


def normed_transpose(nc, c, name, x_of, gamma):
    with Stage(nc, name) as s:
        x = [s.sb(f"x{u}", [P, D]) for u in range(2)]
        gam = s.sb("gamma", [P, D])
        junk = s.sb("squares", [P, D])
        ssq = s.sb("ssq", [P, 2])
        rstd = s.sb("rstd", [P, 2])
        ps = [s.ps(f"t{u}", 1024) for u in range(2)]
        x_in, gam_in = s.sem("x_in", 2), s.sem("gamma_in")
        sq, var, rs, xn = (s.sem(n) for n in ("ssq", "var", "rstd", "xn"))
        xt, ev, dc = s.sem("transposed"), s.sem("evacuated"), s.sem("dve_chain")
        block = s.block()

        @block.sync
        def _(sp):
            sp.dma_start(gam[:, :], gamma.to_broadcast([P, D])).then_inc(gam_in, 16)

            def load(t, u, n, rows):
                sp.wait_ge(xt, t + 1)
                sp.dma_start(x[u][0:rows, :], x_of(t, rows)).then_inc(x_in[u], 16)
            each_tile(sp, load)

        @block.scalar
        def _(act):
            def squares(t, u, n, rows):
                act.wait_ge(x_in[u], n * 16)
                nc.scalar.activation(junk[0:rows, :], x[u][0:rows, :], ACT.Square,
                                     accum_out=ssq[0:rows, u:u + 1]).then_inc(sq, 1)
                act.wait_ge(sq, t + 1)
            each_tile(act, squares)

        @block.gpsimd
        def _(pool):
            link = Link(pool, var)
            for u in range(2):
                load_weights(pool, c, u, u)

            def rstds(t, u, n, rows):
                v, r = ssq[0:rows, u:u + 1], rstd[0:rows, u:u + 1]
                pool.wait_ge(sq, t + 1)
                link.at(t * 2)
                link(nc.gpsimd.tensor_tensor(v, v, c.inv_d[0:rows, 0:1], ALU.mult))
                link(nc.gpsimd.tensor_tensor(v, v, c.eps[0:rows, 0:1], ALU.add))
                nc.gpsimd.tensor_tensor(r, v, c.half[0:rows, 0:1], ALU.pow).then_inc(rs, 1)
            each_tile(pool, rstds)

        @block.vector
        def _(dve):
            dve.sem_inc(ev, 4)
            dve.wait_ge(gam_in, 16)
            link = Link(dve, dc)

            def scale_and_keep(t, u, n, rows):
                dve.wait_ge(rs, t + 1)
                nc.vector.scalar_tensor_tensor(x[u][0:rows, :], x[u][0:rows, :], rstd[0:rows, u:u + 1],
                                               gam[0:rows, :], ALU.mult, ALU.mult).then_inc(xn, 1)
                dve.wait_ge(xt, t + 3)
                to = slice(SEQ, TOK) if rows == SMP else bass.ts(t, P)
                link.at(t * 2)
                for h in range(2):
                    k4 = slice(4 * h, 4 * h + 4)
                    split(nc.vector, link,
                          ps[u][:, 512 * h:512 * h + 512].rearrange("p (k t) -> p k t", k=4)[:, :, 0:rows],
                          c.xh[:, k4, to], c.xl[:, k4, to]).then_inc(ev, 1)
            each_tile(dve, scale_and_keep)

        @block.tensor
        def _(pe):
            pe.sem_inc(xt, 2)

            def transposes(t, u, n, rows):
                pe.wait_ge(xn, t + 1)
                pe.wait_ge(ev, t * 2 + 2)
                for k in range(KC):
                    ins = nc.tensor.transpose(ps[u][:, P * k:P * k + rows], x[u][0:rows, P * k:P * k + P],
                                              c.ident[0:rows, 0:rows])
                ins.then_inc(xt, 1)
            each_tile(pe, transposes)


def projection_memory(c, L, w):
    c.xh, c.xl = (L.sb(n, [P, KC, TOK], F32R) for n in ("xT_hi", "xT_lo"))
    c.w, c.wraw, c.w_in = w, [L.sb(f"w{u}", [P, KC, CW]) for u in range(2)], L.pool_sem("w_in", 2)


def load_weights(pool, c, u, chunk):
    pool.dma_start(c.wraw[u][:, :, :].rearrange("p k n -> p (k n)"),
                   c.w[bass.ds(chunk, 1), :, :].rearrange("o p n -> (o p) n")).then_inc(c.w_in[u], 16)


def project(nc, c, name, h, runs):
    RING, PER = 6, 2 * (TILES + 1)
    with Stage(nc, name) as s:
        wh = [s.sb(f"w_hi{u}", [P, KC, CW], F32R) for u in range(2)]
        wl = [s.sb(f"w_lo{u}", [P, KC, CW], F32R) for u in range(2)]
        st = [s.sb(f"st{r}", [P, CW]) for r in range(RING)]
        ps = [s.ps(f"acc{r}") for r in range(RING)]
        mm, ev = s.sem("products"), s.sem("evacuated")
        halves, chain = s.sem("weights_split"), s.sem("dve_chain")
        stored = s.sem("stored", RING)
        block = s.block()
        CHUNKS = 2 * sum(n for n, _ in runs)

        def pairs(eng, body):
            at = 0
            for n, funcs in runs:
                with eng.Fori(at, at + n) as i:
                    body(i, funcs)
                at += n

        def order():
            for u in range(2):
                for t in range(TILES + 1):
                    r = u * (TILES + 1) + t
                    yield u, t, r, r % RING, P if t < TILES else SMP

        @block.gpsimd
        def _(pool):
            with pool.Fori(0, CHUNKS // 2 - 1) as i:
                for u in range(2):
                    pool.wait_ge(halves, i * 4 + 2 * u + 2)
                    load_weights(pool, c, u, i * 2 + 2 + u)

        @block.vector
        def _(dve):
            link = Link(dve, chain)
            with dve.Fori(0, CHUNKS // 2) as i:
                for u in range(2):
                    dve.wait_ge(c.w_in[u], i * 16 + 16)
                    dve.wait_ge(mm, i * PER + (u + 1) * (TILES + 1))
                    link.at(i * 4 + u * 2)
                    for k in (0, KC // 2):
                        k4 = slice(k, k + KC // 2)
                        split(nc.vector, link, c.wraw[u][:, k4, :], wh[u][:, k4, :], wl[u][:, k4, :])\
                            .then_inc(halves, 1)

        @block.tensor
        def _(pe):
            pe.sem_inc(mm, PER)

            def tiles(i, funcs):
                for u, t, r, b, rows in order():
                    if t == 0:
                        pe.wait_ge(halves, i * 4 + 2 * u + 2)
                    pe.wait_ge(ev, i * PER + r + 1)
                    to = slice(P * t, P * t + rows)
                    products(nc.tensor, ps[b][0:rows, :],
                             [((c.xh[:, k, to], c.xl[:, k, to]), (wh[u][:, k, :], wl[u][:, k, :]))
                              for k in range(KC)]).then_inc(mm, 1)
            pairs(pe, tiles)

        @block.scalar
        def _(act):
            act.sem_inc(ev, RING)
            for r in range(RING):
                act.sem_inc(stored[r], 16)

            def evacuate(i, funcs):
                for u, t, r, b, rows in order():
                    act.wait_ge(mm, i * PER + PER + r + 1)
                    act.wait_ge(stored[b], (i * (PER // RING) + r // RING + 1) * 16)
                    nc.scalar.activation(st[b][0:rows, :], ps[b][0:rows, :], funcs[u]).then_inc(ev, 1)
            pairs(act, evacuate)

        @block.sync
        def _(sp):
            def store(i, funcs):
                for u, t, r, b, rows in order():
                    sp.wait_ge(ev, i * PER + RING + r + 1)
                    sp.dma_start(h[P * t:P * t + rows, bass.ds(i * (2 * CW) + u * CW, CW)],
                                 st[b][0:rows, :]).then_inc(stored[b], 16)
            pairs(sp, store)
            for r in range(RING):
                sp.wait_ge(stored[r], (sum(n for n, _ in runs) * (PER // RING) + 1) * 16)


def project_gates(nc, c, a):
    with Stage(nc, "gates") as s:
        w = s.sb("w", [P, KC, 36])
        wh, wl = (s.sb(n, [P, KC, 36], F32R) for n in ("w_hi", "w_lo"))
        raw = s.sb("raw", [P, KC, 2 * NH])
        ps = [s.ps(f"acc{j}") for j in range(3)]
        N = TOK // 3
        w_in, laid, mm, ev = s.sem("w_in"), s.sem("laid"), s.sem("products"), s.sem("evacuated")
        chain = s.sem("dve_chain")
        block = s.block()

        @block.sync
        def _(sp):
            sp.dma_start(raw[:, :, :], a["w_if"]).then_inc(w_in, 16)

        @block.vector
        def _(dve):
            nc.vector.memset(w[:, :, :], 0.0).then_inc(laid, 1)
            dve.wait_ge(laid, 1)
            dve.wait_ge(w_in, 16)
            nc.vector.tensor_copy(w[:, :, 0:NH], raw[:, :, 0:NH]).then_inc(laid, 1)
            nc.vector.tensor_copy(w[:, :, 32:32 + NH], raw[:, :, NH:2 * NH]).then_inc(laid, 1)
            dve.wait_ge(laid, 3)
            split(nc.vector, Link(dve, chain), w[:, :, :], wh[:, :, :], wl[:, :, :]).then_inc(laid, 1)
            for j in range(3):
                dve.wait_ge(mm, j + 1)
                nc.vector.tensor_copy(c.gates[0:36, j * N:j * N + N], ps[j][0:36, 0:N]).then_inc(ev, 1)
            dve.wait_ge(ev, 3)

        @block.tensor
        def _(pe):
            pe.wait_ge(laid, 4)
            for j in range(3):
                to = slice(j * N, j * N + N)
                products(nc.tensor, ps[j][0:36, 0:N],
                         [((wh[:, k, :], wl[:, k, :]), (c.xh[:, k, to], c.xl[:, k, to]))
                          for k in range(KC)]).then_inc(mm, 1)


def bc(ap, axis, n):
    ap = ap.unsqueeze(axis)
    return ap.broadcast_to([n if i == axis else x for i, x in enumerate(ap.shape)])


def heads(ap, n=NH):
    return ap.rearrange("p (h d) -> p h d", h=n)


def two_ahead(eng, first, second):
    first(0, 0, 1)
    with eng.Fori(0, TILES // 2 - 1) as i:
        first(i * 2 + 1, 1, i + 1)
        second(i * 2, 0, i + 1)
        first(i * 2 + 2, 0, i + 2)
        second(i * 2 + 1, 1, i + 1)
    first(TILES - 1, 1, TILES // 2)
    second(TILES - 2, 0, TILES // 2)
    second(TILES - 1, 1, TILES // 2)


def memory_keys(nc, c, a, o):
    with Stage(nc, "memkv") as s:
        mem = s.sb("mem", [P, MC, D])
        memT = s.sb("memT", [P, KC, MEM])
        w = [s.sb(f"w{j}", [P, KC, CW]) for j in range(4)]
        kn = s.sb("kn", [P, 2, HD])
        qn = s.sb("qn", [P, 2])
        k = [s.sb(f"k{j}", [P, CW]) for j in range(4)]
        sq = [s.sb(f"sq{j}", [P, CW]) for j in range(4)]
        ssq = s.sb("ssq", [P, 4, NH])
        pt = [s.ps(f"t{j}") for j in range(4)]
        pm = [s.ps(f"m{j}") for j in range(4)]
        mem_in, gam_in, w_in = s.sem("mem_in"), s.sem("gamma_in"), s.sem("w_in", 4)
        mt, mte, kmm, vmm, kraw, vcp, squ, red, rs, kno, kt, kte, chain = (s.sem(n) for n in (
            "memT", "memT_copied", "key_products", "value_products", "keys_copied", "values_copied",
            "squares", "sums", "rstd", "keys_normed", "keys_transposed", "keysT_copied", "pool_chain"))
        dchain, out = s.sem("dve_chain"), s.sem("stored")
        block = s.block()

        @block.sync
        def _(sp):
            sp.dma_start(mem[:, :, :], a["mem_prompt"][0].rearrange("(m p) d -> p m d", p=P)).then_inc(mem_in, 16)
            for j in range(4):
                sp.dma_start(w[j][:, :, :].rearrange("p k n -> p (k n)"), a["w_mem"][j // 2, j % 2])\
                    .then_inc(w_in[j], 16)
            sp.dma_start(kn[:, :, :], a["mem_kn"].unsqueeze(0).broadcast_to([P, 2, HD])).then_inc(gam_in, 16)
            sp.dma_start(qn[:, :], a["mem_qn"].rearrange("l d -> d l")).then_inc(gam_in, 16)
            for l in range(2):
                for m in range(MC):
                    sp.wait_ge(kno, 2 * l + m + 1)
                    sp.dma_start(o[15][l, 0, P * m:P * m + P].rearrange("m h d -> m (h d)"), k[2 * l + m][:, :])\
                        .then_inc(out, 16)
                    sp.wait_ge(vcp, 2 * l + m + 1)
                    sp.dma_start(o[16][l, 0, P * m:P * m + P].rearrange("m h d -> m (h d)"), c.vals[:, l, m, :])\
                        .then_inc(out, 16)
            sp.wait_ge(out, 8 * 16)

        @block.tensor
        def _(pe):
            pe.wait_ge(mem_in, 16)
            for j in range(4):
                for i in range(4):
                    m, kk = j // 2, (j % 2) * 4 + i
                    ins = nc.tensor.transpose(pt[j][:, P * i:P * i + P], mem[:, m, P * kk:P * kk + P], c.ident[:, :])
                ins.then_inc(mt, 1)
            pe.wait_ge(mte, 4)
            for l in range(2):
                for m in range(MC):
                    for v in range(2):
                        pe.wait_ge(w_in[2 * l + v], 16)
                        if l:
                            pe.wait_ge(vcp if v else kraw, m + 1)
                        for kk in range(KC):
                            ins = nc.tensor.matmul(pm[2 * m + v][:, :], memT[:, kk, P * m:P * m + P],
                                                   w[2 * l + v][:, kk, :], start=(kk == 0), stop=(kk == KC - 1))
                        ins.then_inc(vmm if v else kmm, 1)
            for j in range(4):
                pe.wait_ge(kno, j + 1)
                for h in range(NH):
                    ins = nc.tensor.transpose(pt[j][:, P * h:P * h + P], k[j][:, P * h:P * h + P], c.ident[:, :])
                ins.then_inc(kt, 1)

        @block.scalar
        def _(act):
            for j in range(4):
                act.wait_ge(mt, j + 1)
                m, half = j // 2, j % 2
                nc.scalar.activation(memT[:, 4 * half:4 * half + 4, P * m:P * m + P],
                                     heads(pt[j][:, :]), ACT.Copy).then_inc(mte, 1)
            for l in range(2):
                for m in range(MC):
                    act.wait_ge(kmm, 2 * l + m + 1)
                    nc.scalar.activation(k[2 * l + m][:, :], pm[2 * m][:, :], ACT.Copy).then_inc(kraw, 1)
                    act.wait_ge(vmm, 2 * l + m + 1)
                    nc.scalar.activation(c.vals[:, l, m, :], pm[2 * m + 1][:, :], ACT.Copy).then_inc(vcp, 1)
            act.wait_ge(gam_in, 32)
            for j in range(4):
                l, m = j // 2, j % 2
                act.wait_ge(kt, j + 1)
                nc.scalar.activation(c.keysT[:, l, :, P * m:P * m + P], heads(pt[j][:, :]), ACT.Copy,
                                     scale=qn[:, l:l + 1]).then_inc(kte, 1)
            act.wait_ge(kte, 4)

        @block.gpsimd
        def _(pool):
            link = Link(pool, chain)
            for j in range(4):
                pool.wait_ge(kraw, j + 1)
                nc.gpsimd.tensor_tensor(sq[j][:, :], k[j][:, :], k[j][:, :], ALU.mult).then_inc(squ, 1)
            for j in range(4):
                pool.wait_ge(red, j + 1)
                v = ssq[:, j, :]
                link(nc.gpsimd.tensor_tensor(v, v, c.inv_hd[:, 0:NH], ALU.mult))
                link(nc.gpsimd.tensor_tensor(v, v, c.eps[:, 0:NH], ALU.add))
                nc.gpsimd.tensor_tensor(v, v, c.half[:, 0:NH], ALU.pow).then_inc(rs, 1)

        @block.vector
        def _(dve):
            link = Link(dve, dchain)
            for j in range(4):
                dve.wait_ge(squ, j + 1)
                nc.vector.tensor_reduce(ssq[:, j, :], heads(sq[j][:, :]), AX.X, ALU.add).then_inc(red, 1)
            dve.wait_ge(gam_in, 32)
            for j in range(4):
                dve.wait_ge(rs, j + 1)
                kh = heads(k[j][:, :])
                link(nc.vector.tensor_tensor(kh, kh, bc(ssq[:, j, :], 2, HD), ALU.mult))
                nc.vector.tensor_tensor(kh, kh, bc(kn[:, j // 2, :], 1, NH), ALU.mult).then_inc(kno, 1)


def memory_attention(nc, c, a, layer, h, cq, cg, y, cy):
    with Stage(nc, f"memattn{layer}") as s:
        xq = [s.sb(f"q{u}", [P, CW]) for u in range(2)]
        gx = [s.sb(f"gate{u}", [P, CW]) for u in range(2)]
        sq = s.sb("squares", [P, CW])
        qT = [s.sb(f"qT{u}", [P, NH, P]) for u in range(2)]
        pr = [s.sb(f"p{u}", [P, NH * MEM]) for u in range(2)]
        prT = [s.sb(f"pT{u}", [P, NH * MC, P]) for u in range(2)]
        yb = [s.sb(f"y{u}", [P, CW]) for u in range(2)]
        ssq = [s.sb(f"rstd{u}", [P, NH]) for u in range(2)]
        mx = [s.sb(f"max{u}", [P, NH]) for u in range(2)]
        tot = [s.sb(f"total{u}", [P, NH]) for u in range(2)]
        ck = s.sb("ck", [P, NB, MC, CW])
        cv = s.sb("cv", [P, NB, MC, CW])
        ckT = s.sb("ckT", [P, NB, NH, MEM])
        qn = s.sb("qn", [P, 1])
        eps = s.sb("eps", [P, NH])
        qTm = s.sb("qTm", [P, NH, NB, SMP])
        oT = s.sb("oT", [P, NH, SMP])
        psT = s.ps("qT_ps")
        psS = [s.ps(f"s{u}", 1024) for u in range(2)]
        psP = s.ps("pT_ps", 1024)
        psO = s.ps("o_ps")
        q_in, g_in, stored = s.sem("q_in", 2), s.sem("gate_in", 2), s.sem("stored", 2)
        k_in, v_in, n_in = s.pool_sem("ck_in"), s.pool_sem("cv_in"), s.pool_sem("qn_in")
        squ, red, rs, qt, qe, sc, nm, ex, pt, pa, pd, od, yd = (s.sem(n) for n in (
            "squares", "sums", "rstd", "queries_transposed", "queriesT_copied", "scores", "neg_max",
            "exps", "p_transposed", "pT_by_act", "pT_by_dve", "mixed", "y"))
        pc, dc, rcp = s.sem("pool_chain"), s.sem("dve_chain"), s.sem("reciprocals")
        ktr, kca, kcd, masked, pn, oc, ot = (s.sem(n) for n in (
            "ck_transposed", "ckT_by_act", "ckT_by_dve", "masked", "p_normed", "oT_copied", "o_transposed"))
        block = s.block()
        L = TILES

        @block.sync
        def _(sp):
            for r in stored:
                sp.sem_inc(r, 16)

            def load(t, u, n, rows=P):
                sp.wait_ge(yd, t + 1)
                sp.dma_start(xq[u][0:rows, :], h[rows_of(t, rows), cq:cq + CW]).then_inc(q_in[u], 16)
                sp.dma_start(gx[u][0:rows, :], h[rows_of(t, rows), cg:cg + CW]).then_inc(g_in[u], 16)

            def store(t, u, n, rows=P):
                sp.wait_ge(yd, t + 3)
                sp.dma_start(y[rows_of(t, rows), cy:cy + CW], yb[u][0:rows, :]).then_inc(stored[u], 16)
            load(0, 0, 1)
            load(1, 1, 1)
            with sp.Fori(0, TILES // 2 - 1) as i:
                store(i * 2, 0, i + 1)
                load(i * 2 + 2, 0, i + 2)
                store(i * 2 + 1, 1, i + 1)
                load(i * 2 + 3, 1, i + 2)
            store(L - 2, 0, 4)
            load(L, 0, 5, SMP)
            store(L - 1, 1, 4)
            store(L, 0, 5, SMP)
            sp.wait_ge(stored[0], 16 * 6)
            sp.wait_ge(stored[1], 16 * 5)

        @block.gpsimd
        def _(pool):
            pool.dma_start(qn[:, :], a["mem_qn"][layer].unsqueeze(1)).then_inc(n_in, 16)
            pool.dma_start(ck[:, :, :, :], a["cache_mem_k"][layer].rearrange("b (m p) h d -> p b m (h d)", p=P))\
                .then_inc(k_in, 16)
            pool.dma_start(cv[:, :, :, :], a["cache_mem_v"][layer].rearrange("b (m p) h d -> p b m (h d)", p=P))\
                .then_inc(v_in, 16)
            for j in range(2):
                load_out(pool, c, j)
            link = Link(pool, pc)
            nc.gpsimd.memset(eps[:, :], EPS * HD)

            def rstds(t, u, n, rows=P):
                link.at(t)
                pool.wait_ge(q_in[u], n * 16)
                pool.wait_ge(red, t + 1)
                nc.gpsimd.tensor_tensor(sq[0:rows, :], xq[u][0:rows, :], xq[u][0:rows, :], ALU.mult)\
                    .then_inc(squ, 1)
                pool.wait_ge(red, t + 2)
                v = ssq[u][0:rows, :]
                link(nc.gpsimd.tensor_tensor(v, v, eps[0:rows, :], ALU.add))
                nc.gpsimd.tensor_tensor(v, v, c.half[0:rows, 0:NH], ALU.pow).then_inc(rs, 1)
            with pool.Fori(0, TILES // 2) as i:
                for u in range(2):
                    rstds(i * 2 + u, u, i + 1)
            rstds(L, 0, 5, SMP)

        @block.tensor
        def _(pe):
            def front(t, u, n):
                pe.wait_ge(q_in[u], n * 16)
                pe.wait_ge(qe, t + 1)
                for g in range(NH):
                    ins = nc.tensor.transpose(psT[:, P * g:P * g + P], xq[u][:, P * g:P * g + P], c.ident[:, :])
                ins.then_inc(qt, 1)
                pe.wait_ge(qe, t + 2)
                for g in range(NH):
                    ins = nc.tensor.matmul(psS[u][:, MEM * g:MEM * g + MEM], qT[u][:, g, :],
                                           c.keysT[:, layer, g, :], start=True, stop=True)
                ins.then_inc(sc, 1)

            def back(t, u, n):
                pe.wait_ge(ex, t + 1)
                pe.wait_ge(pa, t + 1)
                pe.wait_ge(pd, t + 1)
                for j in range(NH * MC):
                    ins = nc.tensor.transpose(psP[:, P * j:P * j + P], pr[u][:, P * j:P * j + P], c.ident[:, :])
                ins.then_inc(pt, 1)
                pe.wait_ge(pa, t + 2)
                pe.wait_ge(pd, t + 2)
                pe.wait_ge(yd, t + 2)
                for g in range(NH):
                    for m in range(MC):
                        ins = nc.tensor.matmul(psO[:, P * g:P * g + P], prT[u][:, MC * g + m, :],
                                               c.vals[:, layer, m, P * g:P * g + P],
                                               start=(m == 0), stop=(m == MC - 1))
                ins.then_inc(od, 1)
            two_ahead(pe, front, back)

            pe.wait_ge(q_in[0], 5 * 16)
            pe.wait_ge(qe, L + 1)
            for g in range(NH):
                ins = nc.tensor.transpose(psT[:, SMP * g:SMP * g + SMP], xq[0][0:SMP, P * g:P * g + P],
                                          c.ident[0:SMP, 0:SMP])
            ins.then_inc(qt, 1)
            pe.wait_ge(k_in, 16)
            for b in range(NB):
                for m in range(MC):
                    bank = psP[:, 512 * m:512 * m + 512]
                    pe.wait_ge(kcd if m else kca, b + 1)
                    if b == 0:
                        pe.wait_ge(pd if m else pa, L + 1)
                    for g in range(NH):
                        ins = nc.tensor.transpose(bank[:, P * g:P * g + P], ck[:, b, m, P * g:P * g + P], c.ident[:, :])
                    ins.then_inc(ktr, 1)
            pe.wait_ge(masked, 1)
            pe.wait_ge(kca, NB + 1)
            pe.wait_ge(kcd, NB + 1)
            for g in range(NH):
                for b in range(NB):
                    ins = nc.tensor.matmul(psS[0][0:SMP, MEM * g:MEM * g + MEM], qTm[:, g, b, :], ckT[:, b, g, :],
                                           start=(b == 0), stop=(b == NB - 1))
            ins.then_inc(sc, 1)
            pe.wait_ge(pn, 1)
            for j in range(NH * MC):
                ins = nc.tensor.transpose(psP[:, SMP * j:SMP * j + SMP], pr[0][0:SMP, P * j:P * j + P],
                                          c.ident[0:SMP, 0:SMP])
            ins.then_inc(pt, 1)
            pe.wait_ge(pa, L + 2)
            pe.wait_ge(v_in, 16)
            pe.wait_ge(yd, L + 2)
            for b in range(NB):
                for g in range(NH):
                    for m in range(MC):
                        at = SMP * g + NT * b
                        ins = nc.tensor.matmul(psO[:, at:at + NT], cv[:, b, m, P * g:P * g + P],
                                               prT[0][:, MC * g + m, NT * b:NT * b + NT],
                                               start=(m == 0), stop=(m == MC - 1))
            ins.then_inc(od, 1)
            pe.wait_ge(oc, 1)
            for g in range(NH):
                ins = nc.tensor.transpose(psT[0:SMP, P * g:P * g + P], oT[:, g, :], c.ident[:, :])
            ins.then_inc(ot, 1)

        @block.scalar
        def _(act):
            act.sem_inc(qe, 1)
            act.sem_inc(pa, 1)
            act.sem_inc(kca, 1)

            def exps(t, u, rows):
                act.wait_ge(nm, t + 1)
                for g in range(NH):
                    ins = nc.scalar.activation(pr[u][0:rows, MEM * g:MEM * g + MEM], psS[u][0:rows, MEM * g:MEM * g + MEM],
                                               ACT.Exp, bias=mx[u][0:rows, g:g + 1], scale=ssq[u][0:rows, g:g + 1],
                                               accum_out=tot[u][0:rows, g:g + 1])
                ins.then_inc(ex, 1)

            def front(t, u, n):
                act.wait_ge(qt, t + 1)
                nc.scalar.activation(qT[u][:, :, :], heads(psT[:, :]), ACT.Copy).then_inc(qe, 1)
                exps(t, u, P)

            def back(t, u, n):
                act.wait_ge(pt, t + 1)
                nc.scalar.activation(prT[u][:, 0:4, :], heads(psP[:, 0:512]), ACT.Copy).then_inc(pa, 1)
            two_ahead(act, front, back)
            act.wait_ge(qt, L + 1)
            nc.scalar.activation(qT[0][:, :, 0:SMP], heads(psT[:, 0:NH * SMP]), ACT.Copy).then_inc(qe, 1)
            act.wait_ge(n_in, 16)
            for b in range(NB):
                act.wait_ge(ktr, 2 * b + 1)
                nc.scalar.activation(ckT[:, b, :, 0:P], heads(psP[:, 0:512]), ACT.Copy, scale=qn[:, 0:1]).then_inc(kca, 1)
            exps(L, 0, SMP)
            act.wait_ge(pt, L + 1)
            nc.scalar.activation(prT[0][:, :, 0:SMP], psP[:, 0:256].rearrange("p (j t) -> p j t", j=8), ACT.Copy)\
                .then_inc(pa, 1)
            act.wait_ge(od, L + 1)
            nc.scalar.activation(oT[:, :, :], heads(psO[:, 0:NH * SMP]), ACT.Copy).then_inc(oc, 1)

        @block.vector
        def _(dve):
            link = Link(dve, dc)
            dve.sem_inc(red, 1)
            dve.sem_inc(pd, 1)
            dve.sem_inc(yd, 2)
            dve.sem_inc(kcd, 1)

            def front(t, u, n, rows=P):
                link.at(t)
                dve.wait_ge(squ, t + 1)
                nc.vector.tensor_reduce(ssq[u][0:rows, :], heads(sq[0:rows, :]), AX.X, ALU.add).then_inc(red, 1)
                dve.wait_ge(sc, t + 1)
                link(nc.vector.tensor_reduce(mx[u][0:rows, :], psS[u][0:rows, :].rearrange("p (h m) -> p h m", h=NH),
                                             AX.X, ALU.max))
                dve.wait_ge(rs, t + 1)
                nc.vector.scalar_tensor_tensor(mx[u][0:rows, :], mx[u][0:rows, :], -1.0, ssq[u][0:rows, :],
                                               ALU.mult, ALU.mult).then_inc(nm, 1)

            def back(t, u, n):
                dve.wait_ge(pt, t + 1)
                nc.vector.tensor_copy(prT[u][:, 4:8, :], heads(psP[:, 512:1024])).then_inc(pd, 1)
                dve.wait_ge(ex, t + 1)
                nc.vector.reciprocal(tot[u][:, :], tot[u][:, :]).then_inc(rcp, 1)
                dve.wait_ge(rcp, t + 1)
                dve.wait_ge(od, t + 1)
                dve.wait_ge(g_in[u], n * 16)
                dve.wait_ge(stored[u], n * 16)
                for g in range(NH):
                    v = slice(P * g, P * g + P)
                    ins = nc.vector.scalar_tensor_tensor(yb[u][:, v], psO[:, v], tot[u][:, g:g + 1], gx[u][:, v],
                                                         ALU.mult, ALU.mult)
                ins.then_inc(yd, 1)
            two_ahead(dve, front, back)
            dve.wait_ge(qe, L + 2)
            for g in range(NH):
                ins = nc.vector.tensor_tensor(qTm[:, g, :, :], bc(qT[0][:, g, 0:SMP], 1, NB), c.seq_cols[:, :, :], ALU.mult)
            ins.then_inc(masked, 1)
            dve.wait_ge(n_in, 16)
            for b in range(NB):
                dve.wait_ge(ktr, 2 * b + 2)
                nc.vector.tensor_scalar(ckT[:, b, :, P:2 * P], heads(psP[:, 512:1024]), qn[:, 0:1], None, ALU.mult)\
                    .then_inc(kcd, 1)
            front(L, 0, 5, SMP)
            dve.wait_ge(ex, L + 1)
            nc.vector.reciprocal(tot[0][0:SMP, :], tot[0][0:SMP, :]).then_inc(rcp, 1)
            dve.wait_ge(rcp, L + 1)
            p4 = pr[0][0:SMP, :].rearrange("p (h m) -> p h m", h=NH)
            nc.vector.tensor_tensor(p4, p4, bc(tot[0][0:SMP, :], 2, MEM), ALU.mult).then_inc(pn, 1)
            dve.wait_ge(ot, 1)
            dve.wait_ge(g_in[0], 5 * 16)
            dve.wait_ge(stored[0], 5 * 16)
            nc.vector.tensor_tensor(yb[0][0:SMP, :], psT[0:SMP, :], gx[0][0:SMP, :], ALU.mult).then_inc(yd, 1)


def mlstm(nc, c, a, o):
    T = TILES
    with Stage(nc, "mlstm") as s:
        li, lf, f, m, b, av, M, negM = (s.sb(n, [NH, TOK]) for n in ("li", "lf", "f", "m", "b", "a", "M", "negM"))
        keep = s.sb("keep", [NH, SEQ])
        bias = s.sb("bias", [P, 1])
        before, last, fade = (s.sb(n, [NH, 16]) for n in ("m_before", "M_last", "fade"))
        R = s.sb("rows", [P, TOK])
        cols = s.sb("cols", [P, T + 1, P])
        fades = s.sb("fades", [P, NH, 16])
        q, k, og, ga = ([s.sb(f"{n}{u}", [P, CW]) for u in range(2)] for n in ("q", "k", "og", "ga"))
        v = [s.sb(f"v{u}", [P, NH, HD + 1]) for u in range(2)]
        hg = s.sb("hg", [P, CW])
        qT, kT, Z, Pt = ([s.sb(f"{n}{u}", [P, CW]) for u in range(2)] for n in ("qT", "kT", "z", "pt"))
        vw = s.sb("vw", [P, NH, HD + 1])
        inter = s.sb("inter", [P, NH, HD + 1])
        num = s.sb("num", [P, NH, HD + 1])
        hh, sq = s.sb("h", [P, CW]), s.sb("sq", [P, CW])
        den, ssq = s.sb("den", [P, NH]), s.sb("ssq", [P, NH])
        yb = [s.sb(f"y{u}", [P, CW]) for u in range(2)]
        C = s.sb("C", [P, NH, HD + 1])
        C0 = s.sb("C0", [P, NB * NH, HD + 1])
        n0 = s.sb("n0", [NB * NH, HD])
        vwm = s.sb("vwm", [SMP, NB, HD + 1])
        vwm2 = s.sb("vwm2", [SMP, NB, HD + 1])
        psq, psk, psS, psZ = (s.ps(n) for n in ("psq", "psk", "pss", "psz"))
        psN, psI = s.ps("psn", 1024), s.ps("psi", 1024)

        def pair(ps):
            return ps[:, :].rearrange("p (b x) -> p b x", b=2)[:, :, 0:2 * (HD + 1)]\
                .rearrange("p b (h d) -> p b h d", h=2)

        def by2(t):
            return t.rearrange("p (b h) d -> p b h d", b=2)

        def of(ps, h):
            at = 512 * (h // 2) + (HD + 1) * (h % 2)
            return slice(at, at + HD + 1)

        par_in, m0_in, C0_in, hg_in, n0_in = (
            s.sem("bias_in"), s.sem("m0_in"), s.pool_sem("C0_in"), s.sem("hg_in"), s.pool_sem("n0_in"))
        made, zex, qnm = s.sem("rows_made"), s.sem("z_exponentials"), s.sem("smp_qn_masked")
        x_in, gt_in, stored, outs = s.sem("qkv_in", 2), s.sem("gates_in", 2), s.sem("stored", 2), s.sem("outs")
        (vones, rchain, e1, e2, e3, rows, trr, trc, frd, tr, qe, ke, sc, zz, ze, ptd, mm, ie, vwd, up, cd, nd, hd_,
         sqd, gt, ssd, rs, yd, dch, pch) = (s.sem(n) for n in (
            "v_ones", "row_chain", "log_f_exps", "rows_ready", "rows_exp", "rows_done", "rows_transposed",
            "cols_copied", "fades_copied", "qk_transposed", "qT_copied", "kT_copied", "scores", "z", "z_exp",
            "weighted", "num_inter", "inter_copied", "vw", "update", "C_updated", "num", "h", "squares", "gate",
            "sums", "rstd", "y", "dve_chain", "pool_chain"))
        n0t, n0c, lqt, mk, up2, c2, it2, itc, it3, fin, fint = (s.sem(n) for n in (
            "n0_transposed", "n0_copied", "smp_qn", "smp_masked", "smp_update", "smp_C", "smp_inter",
            "smp_inter_copied", "smp_inter_back", "n_final", "n_final_copied"))
        block = s.block()
        ALL = slice(0, SEQ)

        def smp(ap):
            return ap[:, SEQ:TOK].rearrange("p (b t) -> p b t", t=NT)

        def chunks(ap):
            return ap[:, 0:SEQ].rearrange("p (c t) -> p c t", t=P)

        @block.sync
        def _(sp):
            for r in stored:
                sp.sem_inc(r, 16)
            sp.dma_start(bias[0:NH, :], a["b_if_even"][0, 0:NH].unsqueeze(1)).then_inc(par_in, 16)
            sp.dma_start(bias[32:32 + NH, :], a["b_if_even"][0, NH:2 * NH].unsqueeze(1)).then_inc(par_in, 16)
            sp.dma_start(before[:, NB:2 * NB], a["state_mlstm_m"][0].rearrange("b h -> h b")).then_inc(m0_in, 16)
            sp.dma_start(hg[:, :], a["mlstm_hnorm"].broadcast_to([P, CW])).then_inc(hg_in, 16)

            def load(t, u, rows=P):
                sp.wait_ge(yd, t + 1)
                r = rows_of(t, rows)
                sp.dma_start(q[u][0:rows, :], c.h_even[r, E_Q:E_Q + CW]).then_inc(x_in[u], 16)
                sp.dma_start(k[u][0:rows, :], c.h_even[r, E_K:E_K + CW]).then_inc(x_in[u], 16)
                sp.dma_start(v[u][0:rows, :, 0:HD], heads(c.h_even[r, E_V:E_V + CW])).then_inc(x_in[u], 16)
                sp.dma_start(og[u][0:rows, :], c.h_even[r, E_O:E_O + CW]).then_inc(gt_in[u], 16)
                sp.dma_start(ga[u][0:rows, :], c.h_even[r, E_GA:E_GA + CW]).then_inc(gt_in[u], 16)

            def store(t, u, rows=P):
                sp.wait_ge(yd, t + 3)
                sp.dma_start(c.y_even[rows_of(t, rows), 0:CW], yb[u][0:rows, :]).then_inc(stored[u], 16)
            sp.wait_ge(vones, 2)
            load(0, 0)
            load(1, 1)
            with sp.Fori(0, T // 2 - 1) as i:
                store(i * 2, 0)
                load(i * 2 + 2, 0)
                store(i * 2 + 1, 1)
                load(i * 2 + 3, 1)
            store(T - 2, 0)
            load(T, 0, SMP)
            store(T - 1, 1)
            store(T, 0, SMP)
            sp.wait_ge(rows, 1)
            sp.dma_start(o[4][0, 0].unsqueeze(1), m[:, SEQ - 1:SEQ]).then_inc(outs, 16)
            sp.dma_start(o[7][0].rearrange("b h -> h b"), smp(m)[:, :, NT - 1]).then_inc(outs, 16)
            sp.wait_ge(cd, T + 1)
            sp.dma_start(o[2][0, 0].rearrange("h k v -> k h v"), C[:, :, 0:HD]).then_inc(outs, 16)
            sp.dma_start(o[3][0, 0].rearrange("h k -> k h"), C[:, :, HD]).then_inc(outs, 16)
            sp.wait_ge(c2, NH)
            sp.dma_start(o[5][0].rearrange("b h k v -> k (b h) v"), C0[:, :, 0:HD]).then_inc(outs, 16)
            sp.wait_ge(fint, 1)
            sp.dma_start(o[6][0].rearrange("b h k -> (b h) k"), n0[:, :]).then_inc(outs, 16)
            sp.wait_ge(outs, 6 * 16)
            sp.wait_ge(stored[0], 6 * 16)
            sp.wait_ge(stored[1], 5 * 16)

        @block.gpsimd
        def _(pool):
            pool.dma_start(C0[:, :, 0:HD], a["state_mlstm_C"][0].rearrange("b h k v -> k (b h) v")).then_inc(C0_in, 16)
            pool.dma_start(n0[:, :], a["state_mlstm_n"][0].rearrange("b h k -> (b h) k")).then_inc(n0_in, 16)
            for u in range(2):
                nc.gpsimd.memset(v[u][:, :, HD:HD + 1], 1.0).then_inc(vones, 1)
            link = Link(pool, pch)
            link(nc.gpsimd.memset(C[:, :, :], 0.0))
            pool.wait_ge(hg_in, 16)

            def gates(t, u, n, rows=P):
                link.at(1 + t)
                pool.wait_ge(gt_in[u], n * 32)
                g = ga[u][0:rows, :]
                link(nc.gpsimd.tensor_tensor(g, g, og[u][0:rows, :], ALU.mult))
                nc.gpsimd.tensor_tensor(g, g, hg[0:rows, :], ALU.mult).then_inc(gt, 1)
                pool.wait_ge(hd_, t + 1)
                nc.gpsimd.tensor_tensor(sq[0:rows, :], hh[0:rows, :], hh[0:rows, :], ALU.mult).then_inc(sqd, 1)
                pool.wait_ge(ssd, t + 1)
                nc.gpsimd.tensor_tensor(ssq[0:rows, :], ssq[0:rows, :], c.half[0:rows, 0:NH], ALU.pow).then_inc(rs, 1)
            with pool.Fori(0, T // 2) as i:
                for u in range(2):
                    gates(i * 2 + u, u, i + 1)
            gates(T, 0, 5, SMP)

        @block.tensor
        def _(pe):
            pe.sem_inc(mm, 1)
            pe.wait_ge(rows, 1)
            for t in range(T + 1):
                w = P if t < T else SMP
                bank = (psq, psk, psS)[t // 4]
                ins = nc.tensor.transpose(bank[0:w, P * (t % 4):P * (t % 4) + P], R[:, P * t:P * t + w], c.ident[:, :])
            for h in range(NH):
                ins = nc.tensor.matmul(psZ[:, 16 * h:16 * h + 16], c.head_row[:, h, :], fade[:, :], start=True, stop=True)
            ins.then_inc(trr, 1)
            pe.wait_ge(n0_in, 16)
            nc.tensor.transpose(psN[:, 0:32], n0[:, :], c.ident[0:32, 0:32]).then_inc(n0t, 1)

            def front(t, u, n, rows=P):
                pe.wait_ge(x_in[u], n * 48)
                pe.wait_ge(qe, t + 1)
                pe.wait_ge(ke, t + 1)
                for src, ps in ((q, psq), (k, psk)):
                    for h in range(NH):
                        ins = nc.tensor.transpose(ps[:, P * h:P * h + rows], src[u][0:rows, P * h:P * h + P],
                                                  c.ident[0:rows, 0:rows])
                ins.then_inc(tr, 1)
                pe.wait_ge(ze, t + 1)
                for h in range(NH):
                    cut = slice(SEQ, TOK) if rows == SMP else bass.ts(t, P)
                    nc.tensor.matmul(psZ[0:rows, P * h:P * h + rows], c.head_row[:, h, 0:rows], negM[:, cut],
                                     start=True, stop=True)
                pe.wait_ge(qe, t + 2)
                pe.wait_ge(ke, t + 2)
                pe.wait_ge(ptd, t + 1)
                for h in range(NH):
                    ins = nc.tensor.matmul(psS[0:rows, P * h:P * h + rows], kT[u][:, P * h:P * h + rows],
                                           qT[u][:, P * h:P * h + rows], start=True, stop=True)
                ins.then_inc(sc, 1)

            def back(t, u, n):
                pe.wait_ge(ptd, t + 2)
                pe.wait_ge(nd, t + 1)
                for h in range(NH):
                    nc.tensor.matmul(psN[:, of(psN, h)], Pt[u][:, P * h:P * h + P], v[u][:, h, :],
                                     start=True, stop=True)
                pe.wait_ge(cd, t + 1)
                for h in range(NH):
                    ins = nc.tensor.matmul(psI[:, of(psI, h)], qT[u][:, P * h:P * h + P], C[:, h, :],
                                           start=True, stop=True)
                ins.then_inc(mm, 1)
                pe.wait_ge(ie, t + 1)
                pe.wait_ge(vwd, t + 1)
                for h in range(NH):
                    ins = nc.tensor.matmul(psI[:, of(psI, h)], k[u][:, P * h:P * h + P], vw[:, h, :],
                                           start=True, stop=True)
                ins.then_inc(up, 1)
            pe.wait_ge(trc, 1)
            two_ahead(pe, front, back)

            front(T, 0, 5, SMP)
            pe.wait_ge(ptd, T + 2)
            pe.wait_ge(nd, T + 1)
            pe.wait_ge(cd, T + 1)
            for h in range(NH):
                nc.tensor.matmul(psN[0:SMP, of(psN, h)], Pt[0][0:SMP, P * h:P * h + SMP], v[0][0:SMP, h, :],
                                 start=True, stop=True)
            pe.wait_ge(C0_in, 16)
            pe.wait_ge(n0c, 1)
            for h in range(NH):
                for b_ in range(NB):
                    at = SMP * h + NT * b_
                    nc.tensor.matmul(psI[:, at:at + NT], C0[:, NH * b_ + h, 0:HD],
                                     qT[0][:, P * h + NT * b_:P * h + NT * b_ + NT], start=True, stop=True)
            n_of = C0[:, :, HD].rearrange("p (b h) -> p b h", h=NH)
            for h in range(NH):
                ins = nc.tensor.matmul(psI[0:SMP, 512 + NB * h:512 + NB * h + NB], qT[0][:, P * h:P * h + SMP],
                                       n_of[:, :, h], start=True, stop=True)
            ins.then_inc(it2, 1)
            pe.wait_ge(itc, 1)
            for h in range(NH):
                ins = nc.tensor.transpose(psq[0:SMP, P * h:P * h + P], hh[:, SMP * h:SMP * h + SMP], c.ident[:, :])
            ins.then_inc(it3, 1)
            for h in range(NH):
                pe.wait_ge(mk, h + 1)
                if h >= 1:
                    pe.wait_ge(c2, h)
                for j, n in enumerate((3, 3, 2)):
                    bank = (psk, psS, psZ)[j]
                    ins = nc.tensor.matmul(bank[:, 0:n * (HD + 1)], k[0][0:SMP, P * h:P * h + P],
                                           (vwm, vwm2)[h % 2][:, 3 * j:3 * j + n, :].rearrange("p b d -> p (b d)"),
                                           start=True, stop=True)
                ins.then_inc(up2, 1)
            pe.wait_ge(c2, NH)
            nc.tensor.transpose(psI[0:NB * NH, 0:HD], C0[:, :, HD], c.ident[:, :]).then_inc(fin, 1)

        @block.scalar
        def _(act):
            act.sem_inc(qe, 1)
            act.wait_ge(e1, 1)
            nc.scalar.activation(f[:, :], f[:, :], ACT.Exp, scale=-1.0).then_inc(e2, 1)
            act.wait_ge(e2, 1)
            nc.scalar.activation(f[:, :], f[:, :], ACT.Ln, bias=1.0).then_inc(e2, 1)
            act.wait_ge(made, 1)
            nc.scalar.activation(R[32:32 + NH, :], R[32:32 + NH, :], ACT.Exp).then_inc(e3, 1)
            nc.scalar.activation(R[64:64 + NH, :], m[:, :], ACT.Exp, scale=-1.0).then_inc(e3, 1)
            nc.scalar.activation(R[96:96 + NH, :], R[96:96 + NH, :], ACT.Exp).then_inc(e3, 1)
            nc.scalar.activation(fade[:, :], fade[:, :], ACT.Exp).then_inc(e3, 1)
            act.wait_ge(trr, 1)
            nc.scalar.activation(fades[:, :, :], heads(psZ[:, 0:64]), ACT.Copy).then_inc(frd, 1)
            act.wait_ge(frd, 1)

            def front(t, u, n, rows=P):
                act.wait_ge(tr, t + 1)
                nc.scalar.activation(heads(qT[u][:, :])[:, :, 0:rows], heads(psq[:, :])[:, :, 0:rows], ACT.Copy)\
                    .then_inc(qe, 1)
                act.wait_ge(zz, t + 1)
                z = heads(Z[u][0:rows, :])[:, :, 0:rows]
                nc.scalar.activation(z, z, ACT.Exp).then_inc(zex, 1)

            def back(t, u, n):
                act.wait_ge(mm, t + 2)
                act.wait_ge(nd, t + 1)
                for h in range(NH):
                    ins = nc.scalar.activation(inter[:, h, :], psI[:, of(psI, h)], ACT.Copy,
                                               scale=cols[:, bass.ds(t, 1), 32 + h:33 + h].rearrange("p a b -> p (a b)"))
                ins.then_inc(ie, 1)
            two_ahead(act, front, back)
            front(T, 0, 5, SMP)
            act.wait_ge(it2, 1)
            nc.scalar.activation(hh[:, 0:NH * SMP], psI[:, 0:NH * SMP], ACT.Copy).then_inc(itc, 1)
            act.wait_ge(it3, 1)
            act.wait_ge(qnm, 1)
            for h in range(NH):
                ins = nc.scalar.activation(inter[0:SMP, h, 0:HD], psq[0:SMP, P * h:P * h + P], ACT.Copy,
                                           scale=cols[0:SMP, T, 32 + h:33 + h])
            ins.then_inc(ie, 1)

        @block.vector
        def _(dve):
            V = nc.vector
            link = Link(dve, rchain)
            for x in (ke, ze, ptd, nd, cd):
                dve.sem_inc(x, 1)
            dve.sem_inc(yd, 2)
            dve.wait_ge(par_in, 32)
            V.tensor_scalar(li[:, :], c.gates[0:NH, :], bias[0:NH, 0:1], None, ALU.add)
            link(V.tensor_scalar(lf[:, :], c.gates[32:32 + NH, :], bias[32:32 + NH, 0:1], None, ALU.add))
            V.scalar_tensor_tensor(f[:, :], lf[:, :], -1.0, lf[:, :], ALU.mult, ALU.max).then_inc(e1, 1)
            link(V.memset(R[:, :], 0.0))
            link(V.memset(keep[:, :], 1.0))
            link(V.memset(chunks(keep)[:, :, 0:1], 0.0))
            link(V.tensor_scalar(lf[:, :], lf[:, :], 0.0, None, ALU.min))
            dve.wait_ge(e2, 2)
            link(V.tensor_tensor(lf[:, :], lf[:, :], f[:, :], ALU.subtract))
            link(V.tensor_tensor_scan(m[:, ALL], lf[:, ALL], li[:, ALL], 0.0, ALU.add, ALU.max))
            link(V.tensor_tensor_scan(b[:, ALL], keep[:, :], lf[:, ALL], 0.0, ALU.mult, ALU.add))
            dve.wait_ge(m0_in, 16)
            for t in range(NT):
                mp = smp(m)[:, :, t - 1] if t else before[:, NB:2 * NB]
                link(V.tensor_tensor(smp(m)[:, :, t], mp, smp(lf)[:, :, t], ALU.add))
                link(V.tensor_tensor(smp(m)[:, :, t], smp(m)[:, :, t], smp(li)[:, :, t], ALU.max))
                if t:
                    link(V.tensor_tensor(smp(b)[:, :, t], smp(b)[:, :, t - 1], smp(lf)[:, :, t], ALU.add))
                else:
                    link(V.tensor_copy(smp(b)[:, :, 0], smp(lf)[:, :, 0]))
            link(V.tensor_tensor(M[:, :], m[:, :], b[:, :], ALU.subtract))
            link(V.tensor_tensor(av[:, :], li[:, :], b[:, :], ALU.subtract))
            link(V.tensor_scalar(negM[:, :], M[:, :], -1.0, None, ALU.mult))
            link(V.memset(before[:, 0:1], 0.0))
            link(V.tensor_copy(before[:, 1:TILES], chunks(m)[:, 0:TILES - 1, P - 1]))
            link(V.tensor_copy(last[:, 0:TILES], chunks(M)[:, :, P - 1]))
            link(V.tensor_copy(last[:, NB:2 * NB], smp(M)[:, :, NT - 1]))
            for lo, view, n in ((0, chunks, P), (NB, smp, NT)):
                e = slice(lo, lo + 8)
                link(V.tensor_tensor(view(R[32:32 + NH, :]), bc(before[:, e], 2, n), view(M), ALU.subtract))
                link(V.tensor_tensor(view(R[96:96 + NH, :]), view(av), bc(last[:, e], 2, n), ALU.subtract))
            link(V.tensor_copy(R[0:NH, :], av[:, :]))
            V.tensor_tensor(fade[:, :], before[:, :], last[:, :], ALU.subtract).then_inc(made, 1)
            dve.wait_ge(e3, 4)
            V.tensor_scalar(R[96:96 + NH, :], R[96:96 + NH, :], HD ** -0.5, None, ALU.mult).then_inc(rows, 1)
            dve.wait_ge(trr, 1)
            for j, ps in enumerate((psq, psk)):
                link(V.tensor_copy(cols[:, 4 * j:4 * j + 4, :], heads(ps[:, :])))
            link(V.tensor_copy(cols[0:SMP, 8, :], psS[0:SMP, 0:P]))
            dve.wait_ge(n0t, 1)
            dve.wait_ge(C0_in, 16)
            V.tensor_copy(C0[:, :, HD], psN[:, 0:32]).then_inc(n0c, 1)
            dve.wait_ge(frd, 1)
            dve.wait_ge(n0c, 1)
            dve.wait_ge(pch, 1)
            dve.sem_inc(trc, 1)
            link = Link(dve, dch)

            def col(t, at, rows, h):
                if rows == SMP:
                    return cols[0:SMP, T, at + h:at + h + 1]
                return cols[:, bass.ds(t, 1), at + h:at + h + 1].rearrange("p a b -> p (a b)")

            def col4(t, at, rows):
                if rows == SMP:
                    return cols[0:SMP, T, at:at + NH]
                return cols[:, bass.ds(t, 1), at:at + NH].rearrange("p a b -> p (a b)")

            def front(t, u, n, rows=P):
                dve.wait_ge(tr, t + 1)
                V.tensor_scalar(heads(kT[u][:, :])[:, :, 0:rows], heads(psk[:, :])[:, :, 0:rows], HD ** -0.5, None,
                                ALU.mult).then_inc(ke, 1)
                dve.wait_ge(sc, t + 1)
                mask = c.neg_sj if rows == P else c.neg_smp
                for h in range(NH):
                    e = slice(P * h, P * h + rows)
                    ins = V.scalar_tensor_tensor(Z[u][0:rows, e], psZ[0:rows, e], col(t, 0, rows, h), mask[:, :],
                                                 ALU.add, ALU.add)
                ins.then_inc(zz, 1)
                dve.wait_ge(zz, t + 1)
                dve.sem_inc(ze, 1)
                dve.wait_ge(zex, t + 1)
                e = lambda x: heads(x[0:rows, :])[:, :, 0:rows]
                V.tensor_tensor(e(Pt[u]), e(Z[u]), e(psS), ALU.mult).then_inc(ptd, 1)

            def gated(t, u, n, rows):
                link.at(t * 5)
                d = num[0:rows, :, HD]
                link(V.scalar_tensor_tensor(den[0:rows, :], d, -1.0, d, ALU.mult, ALU.max))
                link(V.tensor_tensor(den[0:rows, :], den[0:rows, :], col4(t, 64, rows), ALU.max))
                link(V.reciprocal(den[0:rows, :], den[0:rows, :]))
                h4 = heads(hh[0:rows, :])
                V.tensor_tensor(h4, num[0:rows, :, 0:HD], bc(den[0:rows, :], 2, HD), ALU.mult).then_inc(hd_, 1)
                dve.wait_ge(sqd, t + 1)
                link(V.tensor_reduce(ssq[0:rows, :], heads(sq[0:rows, :]), AX.X, ALU.add))
                V.tensor_scalar(ssq[0:rows, :], ssq[0:rows, :], 1.0 / HD, EPS, ALU.mult, ALU.add).then_inc(ssd, 1)
                dve.wait_ge(rs, t + 1)
                link(V.tensor_tensor(h4, h4, bc(ssq[0:rows, :], 2, HD), ALU.mult))
                dve.wait_ge(gt, t + 1)
                dve.wait_ge(stored[u], n * 16)
                V.tensor_tensor(yb[u][0:rows, :], hh[0:rows, :], ga[u][0:rows, :], ALU.mult).then_inc(yd, 1)
                dve.wait_ge(yd, t + 3)

            def back(t, u, n):
                V.tensor_tensor(vw[:, :, :], v[u][:, :, :], bc(col4(t, 96, P), 2, HD + 1), ALU.mult).then_inc(vwd, 1)
                dve.wait_ge(ie, t + 1)
                V.tensor_tensor(by2(num[:, :, :]), by2(inter[:, :, :]), pair(psN), ALU.add).then_inc(nd, 1)
                dve.wait_ge(nd, t + 2)
                dve.wait_ge(up, t + 1)
                for h in range(NH):
                    ins = V.scalar_tensor_tensor(C[:, h, :], C[:, h, :],
                                                 fades[:, h, bass.ds(t, 1)], psI[:, of(psI, h)],
                                                 ALU.mult, ALU.add)
                ins.then_inc(cd, 1)
                gated(t, u, n, P)
            two_ahead(dve, front, back)

            front(T, 0, 5, SMP)
            dve.wait_ge(it2, 1)
            qn = psI[0:SMP, 512:512 + NH * NB].rearrange("p (h b) -> p h b", h=NH)
            s4 = sq[0:SMP, 0:NH * NB].rearrange("p (h b) -> p h b", h=NH)
            V.tensor_tensor(s4, qn, bc(c.of_seq[0:SMP, :], 1, NH), ALU.mult).then_inc(qnm, 1)
            dve.wait_ge(qnm, 1)
            V.tensor_reduce(ssq[0:SMP, :], s4, AX.X, ALU.add).then_inc(lqt, 1)
            dve.wait_ge(lqt, 1)
            V.tensor_tensor(inter[0:SMP, :, HD], ssq[0:SMP, :], col4(T, 32, SMP), ALU.mult).then_inc(lqt, 1)
            for h in range(NH):
                V.tensor_scalar(vw[0:SMP, h, :], v[0][0:SMP, h, :], col(T, 96, SMP, h), None, ALU.mult).then_inc(vwd, 1)
                dve.wait_ge(vwd, T + h + 1)
                V.tensor_tensor((vwm, vwm2)[h % 2][:, :, :], bc(vw[0:SMP, h, :], 1, NB),
                                bc(c.of_seq[0:SMP, :], 2, HD + 1), ALU.mult).then_inc(mk, 1)
                dve.wait_ge(up2, h + 1)
                for b_ in range(NB):
                    bank = (psk, psS, psZ)[b_ // 3]
                    at = (b_ % 3) * (HD + 1)
                    e = NH * b_ + h
                    ins = V.scalar_tensor_tensor(C0[:, e, :], C0[:, e, :], fades[:, h, NB + b_:NB + b_ + 1],
                                                 bank[:, at:at + HD + 1], ALU.mult, ALU.add)
                ins.then_inc(c2, 1)
            dve.wait_ge(ie, T + 1)
            dve.wait_ge(lqt, 2)
            V.tensor_tensor(by2(num[0:SMP, :, :]), by2(inter[0:SMP, :, :]), pair(psN)[0:SMP], ALU.add).then_inc(nd, 1)
            dve.wait_ge(nd, T + 2)
            gated(T, 0, 5, SMP)
            dve.wait_ge(fin, 1)
            V.tensor_copy(n0[:, :], psI[0:NB * NH, 0:HD]).then_inc(fint, 1)


def gmlp(nc, c, a, o):
    T = TILES
    with Stage(nc, "gmlp") as s:
        w = s.sb("w", [P, NH, P])
        wT = s.sb("wT", [P, NH, P])
        ws = s.sb("ws", [SMP, NH, SMP])
        bs = s.sb("bs", [P, NH])
        bss = s.sb("bss", [SMP, NH])
        lg, lb = s.sb("ln_g", [P, CW]), s.sb("ln_b", [P, CW])
        x, u_, g = ([s.sb(f"{n}{u}", [P, CW]) for u in range(2)] for n in ("v", "u", "gate"))
        vn = [s.sb(f"vn{u}", [P, CW]) for u in range(2)]
        yb = [s.sb(f"y{u}", [P, CW]) for u in range(2)]
        st = [s.sb(f"stats{u}", [P, 6]) for u in range(2)]
        mv = [s.sb(f"mv{u}", [P, 2]) for u in range(2)]
        psW = s.ps("wT_ps")
        psM = [s.ps(f"mix{u}") for u in range(2)]
        w_in, ws_in, v_in, ug_in, stored, vout = (s.sem("w_in"), s.sem("ws_in"), s.sem("v_in", 2), s.sem("ug_in", 2),
                                                   s.sem("stored", 2), s.sem("v_stored"))
        cleared, wt, wr, va, rs, cen, sc, vd, mm, um, yd, dch, pch = (s.sem(n) for n in (
            "cleared", "w_transposed", "w_ready", "variance", "rstd", "centred", "scaled", "v_normed", "mixed",
            "u_mixed", "y", "dve_chain", "pool_chain"))
        block = s.block()

        @block.sync
        def _(sp):
            for r in stored:
                sp.sem_inc(r, 16)
            sp.dma_start(w[:, :, :], a["gmlp_w"][0].rearrange("g t s -> t g s")).then_inc(w_in, 16)
            sp.dma_start(bs[:, :], a["gmlp_b"][0].rearrange("g t -> t g")).then_inc(w_in, 16)
            sp.dma_start(lg[:, :], a["gmlp_ln_g"].broadcast_to([P, CW])).then_inc(w_in, 16)
            sp.dma_start(lb[:, :], a["gmlp_ln_b"].broadcast_to([P, CW])).then_inc(w_in, 16)
            sp.wait_ge(cleared, 1)
            for b in range(NB):
                e = slice(NT * b, NT * b + NT)
                for q in range(NH):
                    sp.dma_start(ws[e, q, e], a["gmlp_w"][0, q, 0:NT, 0:NT].rearrange("t s -> s t")).then_inc(ws_in, 16)
                sp.dma_start(bss[e, :], a["gmlp_b"][0, :, 0:NT].rearrange("g t -> t g")).then_inc(ws_in, 16)

            def load(t, u, n, rows):
                sp.wait_ge(yd, t + 1)
                r = rows_of(t, rows)
                sp.dma_start(x[u][0:rows, :], c.h_even[r, E_VB:E_VB + CW]).then_inc(v_in[u], 16)
                sp.dma_start(u_[u][0:rows, :], c.h_even[r, E_U:E_U + CW]).then_inc(ug_in[u], 16)
                sp.dma_start(g[u][0:rows, :], c.h_even[r, E_GB:E_GB + CW]).then_inc(ug_in[u], 16)
            each_tile(sp, load)

        @block.scalar
        def _(act):
            def store(t, u, n, rows):
                act.wait_ge(yd, t + 3)
                act.dma_start(c.y_even[rows_of(t, rows), CW:2 * CW], yb[u][0:rows, :]).then_inc(stored[u], 16)
            each_tile(act, store)
            act.wait_ge(vd, T + 1)
            act.dma_start(o[8][0].rearrange("b t d -> (b t) d"), vn[0][0:SMP, :]).then_inc(vout, 16)
            act.wait_ge(vout, 16)
            act.wait_ge(stored[0], 6 * 16)
            act.wait_ge(stored[1], 5 * 16)

        @block.gpsimd
        def _(pool):
            pool.sem_inc(yd, 2)
            pool.wait_ge(w_in, 64)

            def norm(t, u, n, rows):
                link = Link(pool, pch)
                link.at(t * 2)
                pool.wait_ge(va, t + 1)
                v = mv[u][0:rows, 1:2]
                link(nc.gpsimd.tensor_tensor(v, v, c.eps[0:rows, 0:1], ALU.add))
                nc.gpsimd.tensor_tensor(v, v, c.half[0:rows, 0:1], ALU.pow).then_inc(rs, 1)
                pool.wait_ge(cen, t + 1)
                y = vn[u][0:rows, :]
                link(nc.gpsimd.tensor_tensor(y, y, lg[0:rows, :], ALU.mult))
                nc.gpsimd.tensor_tensor(y, y, lb[0:rows, :], ALU.add).then_inc(vd, 1)

            def gate(t, u, n, rows):
                pool.wait_ge(um, t + 1)
                nc.gpsimd.tensor_tensor(yb[u][0:rows, :], yb[u][0:rows, :], g[u][0:rows, :], ALU.mult).then_inc(yd, 1)
            two_ahead(pool, lambda t, u, n: norm(t, u, n, P), lambda t, u, n: gate(t, u, n, P))
            norm(T, 0, 5, SMP)
            gate(T, 0, 5, SMP)

        @block.vector
        def _(dve):
            V = nc.vector
            V.memset(ws[:, :, :], 0.0).then_inc(cleared, 1)
            dve.wait_ge(w_in, 64)
            dve.wait_ge(wt, 1)
            V.tensor_tensor(wT[:, :, :], heads(psW[:, :]), bc(c.causal[:, :], 1, NH), ALU.mult).then_inc(wr, 1)
            dve.wait_ge(ws_in, 40 * 16)
            V.tensor_tensor(ws[:, :, :], ws[:, :, :], bc(c.causal[0:SMP, 0:SMP], 1, NH), ALU.mult).then_inc(wr, 1)

            def norm(t, u, n, rows):
                dve.wait_ge(v_in[u], n * 16)
                V.bn_stats(st[u][0:rows, :], x[u][0:rows, :]).then_inc(dch, 1)
                dve.wait_ge(dch, t + 1)
                V.bn_aggr(mv[u][0:rows, :], st[u][0:rows, :]).then_inc(va, 1)
                dve.wait_ge(rs, t + 1)
                V.tensor_scalar(vn[u][0:rows, :], x[u][0:rows, :], mv[u][0:rows, 0:1], mv[u][0:rows, 1:2],
                                ALU.subtract, ALU.mult).then_inc(cen, 1)

            def mix(t, u, n, rows):
                dve.wait_ge(mm, t + 1)
                dve.wait_ge(ug_in[u], n * 32)
                dve.wait_ge(stored[u], n * 16)
                for q in range(NH):
                    e = slice(P * q, P * q + P)
                    ins = V.scalar_tensor_tensor(yb[u][0:rows, e], psM[u][0:rows, e], (bs if rows == P else bss)[0:rows, q:q + 1],
                                                 u_[u][0:rows, e], ALU.add, ALU.mult)
                ins.then_inc(um, 1)
            norm(0, 0, 1, P)
            for t in range(1, T):
                norm(t, t % 2, t // 2 + 1, P)
                mix(t - 1, (t - 1) % 2, (t - 1) // 2 + 1, P)
            mix(T - 1, (T - 1) % 2, T // 2, P)
            norm(T, 0, 5, SMP)
            mix(T, 0, 5, SMP)

        @block.tensor
        def _(pe):
            pe.wait_ge(w_in, 64)
            for q in range(NH):
                ins = nc.tensor.transpose(psW[:, P * q:P * q + P], w[:, q, :], c.ident[:, :])
            ins.then_inc(wt, 1)
            pe.wait_ge(wr, 2)

            def mix(t, u, n, rows):
                pe.wait_ge(vd, t + 1)
                for q in range(NH):
                    e = slice(P * q, P * q + P)
                    ins = nc.tensor.matmul(psM[u][0:rows, e], (wT if rows == P else ws)[0:rows, q, 0:rows],
                                           vn[u][0:rows, e], start=True, stop=True)
                ins.then_inc(mm, 1)
            each_tile(pe, mix)


def out_memory(c, L, w_out):
    c.w_out, c.wo = w_out, [L.sb(f"w{u}", [P, OUT_ROWS, D]) for u in range(2)]
    c.wo_in = L.pool_sem("w_in", 2)


def load_out(pool, c, j):
    pool.dma_start(c.wo[j % 2][:, :, :], c.w_out[:, OUT_ROWS * j:OUT_ROWS * (j + 1), :]).then_inc(c.wo_in[j % 2], 16)


def out_project(nc, c, name, y, x_of, to_of):
    T, YC, H = TILES, OUT_CHUNKS, 2
    with Stage(nc, name) as s:
        wh, wl = (s.sb(n, [P, YC, D], F32R) for n in ("w_hi", "w_lo"))
        yb = [s.sb(f"y{u}", [P, YC * P]) for u in range(2)]
        yh = [s.sb(f"yT_hi{u}", [P, YC, P], F32R) for u in range(2)]
        yl = [s.sb(f"yT_lo{u}", [P, YC, P], F32R) for u in range(2)]
        x = [s.sb(f"x{u}", [P, D]) for u in range(2)]
        psT = s.ps("yT_ps", 512 * 3)
        psO = [s.ps(f"acc{u}", D) for u in range(2)]
        y_in, x_in, stored = s.sem("y_in", 2), s.sem("x_in", 2), s.sem("stored", 2)
        tr, hi, lo, mm, add = (s.sem(n) for n in ("transposed", "upper", "lower", "products", "sums"))
        pieces, chain = s.sem("weights_split"), s.sem("dve_chain")
        block = s.block()

        @block.gpsimd
        def _(pool):
            for j in range(2, OUT_PIECES):
                pool.wait_ge(pieces, j - 1)
                load_out(pool, c, j)

        @block.sync
        def _(sp):
            for r in stored:
                sp.sem_inc(r, 16)

            def load(t, u, n, rows):
                sp.wait_ge(add, t + 1)
                sp.wait_ge(stored[u], n * 16)
                sp.dma_start(yb[u][0:rows, :], y[rows_of(t, rows), :]).then_inc(y_in[u], 16)
                sp.dma_start(x[u][0:rows, :], x_of(t, rows)).then_inc(x_in[u], 16)
            each_tile(sp, load)

        @block.tensor
        def _(pe):
            def front(t, u, n, rows=P):
                pe.wait_ge(y_in[u], n * 16)
                pe.wait_ge(lo, 3 * t + 3)
                for k in range(YC):
                    ins = nc.tensor.transpose(psT[:, P * k:P * k + rows], yb[u][0:rows, P * k:P * k + P],
                                              c.ident[0:rows, 0:rows])
                ins.then_inc(tr, 1)

            def back(t, u, n, rows=P, pieces_first=False):
                pe.wait_ge(lo, 3 * t + 6)
                pe.wait_ge(add, t + 1)
                for k in range(YC):
                    if pieces_first and k % OUT_ROWS == 0:
                        pe.wait_ge(pieces, k // OUT_ROWS + 1)
                    for j in range(H):
                        n5 = slice(512 * j, 512 * j + 512)
                        for i, (yx, wx) in enumerate(((yh, wh), (yh, wl), (yl, wh))):
                            ins = nc.tensor.matmul(psO[u][0:rows, n5], yx[u][:, k, 0:rows], wx[:, k, n5],
                                                   start=(k == 0 and i == 0), stop=(k == YC - 1 and i == 2),
                                                   skip_group_check=True)
                ins.then_inc(mm, 1)
            front(0, 0, 1)
            front(1, 1, 1)
            back(0, 0, 1, pieces_first=True)
            with pe.Fori(0, T // 2 - 1) as i:
                front(i * 2 + 2, 0, i + 2)
                back(i * 2 + 1, 1, i + 1)
                front(i * 2 + 3, 1, i + 2)
                back(i * 2 + 2, 0, i + 2)
            front(T, 0, 5, SMP)
            back(T - 1, 1, 4)
            back(T, 0, 5, SMP)

        @block.scalar
        def _(act):
            def upper(t, u, n, rows=P):
                act.wait_ge(tr, t + 1)
                act.wait_ge(mm, t + 1)
                for j in range(3):
                    nc.scalar.activation(yh[u][:, 4 * j:4 * j + 4, 0:rows],
                                         heads(psT[:, 512 * j:512 * j + 512])[:, :, 0:rows], ACT.Copy).then_inc(hi, 1)

            def store(t, u, n, rows=P):
                act.wait_ge(add, t + 3)
                act.dma_start(to_of(t, rows), x[u][0:rows, :]).then_inc(stored[u], 16)
            act.sem_inc(mm, 2)
            upper(0, 0, 1)
            upper(1, 1, 1)
            with act.Fori(0, T // 2 - 1) as i:
                store(i * 2, 0, i + 1)
                upper(i * 2 + 2, 0, i + 2)
                store(i * 2 + 1, 1, i + 1)
                upper(i * 2 + 3, 1, i + 2)
            store(T - 2, 0, 4)
            upper(T, 0, 5, SMP)
            store(T - 1, 1, 4)
            store(T, 0, 5, SMP)
            act.wait_ge(stored[0], 6 * 16)
            act.wait_ge(stored[1], 5 * 16)

        @block.vector
        def _(dve):
            dve.sem_inc(lo, 3)
            dve.sem_inc(add, 2)
            link = Link(dve, chain)

            def lower(t, u, n, rows=P):
                for j in range(3):
                    dve.wait_ge(hi, 3 * t + j + 1)
                    nc.vector.tensor_tensor(yl[u][:, 4 * j:4 * j + 4, 0:rows],
                                            heads(psT[:, 512 * j:512 * j + 512])[:, :, 0:rows],
                                            yh[u][:, 4 * j:4 * j + 4, 0:rows], ALU.subtract).then_inc(lo, 1)

            def sums(t, u, n, rows=P):
                dve.wait_ge(mm, t + 3)
                dve.wait_ge(x_in[u], n * 16)
                nc.vector.tensor_tensor(x[u][0:rows, :], psO[u][0:rows, :], x[u][0:rows, :], ALU.add).then_inc(add, 1)
            for j in range(OUT_PIECES):
                dve.wait_ge(c.wo_in[j % 2], (j // 2 + 1) * 16)
                rows3 = slice(OUT_ROWS * j, OUT_ROWS * (j + 1))
                split(nc.vector, link, c.wo[j % 2][:, :, :], wh[:, rows3, :], wl[:, rows3, :]).then_inc(pieces, 1)
                if j < 2:
                    lower(j, j, 1)
            with dve.Fori(0, T // 2 - 1) as i:
                sums(i * 2, 0, i + 1)
                lower(i * 2 + 2, 0, i + 2)
                sums(i * 2 + 1, 1, i + 1)
                lower(i * 2 + 3, 1, i + 2)
            sums(T - 2, 0, 4)
            lower(T, 0, 5, SMP)
            sums(T - 1, 1, 4)
            sums(T, 0, 5, SMP)


def project_indexer(nc, c, a):
    N, T = IH + ID, TILES
    with Stage(nc, "projidx") as s:
        w = s.sb("w", [P, KC, N])
        wh, wl = (s.sb(n, [P, KC, N], F32R) for n in ("w_hi", "w_lo"))
        st = [s.sb(f"st{u}", [P, N]) for u in range(2)]
        ps = [s.ps(f"acc{u}") for u in range(2)]
        w_in, mm, ev, stored = s.sem("w_in"), s.sem("products"), s.sem("evacuated"), s.sem("stored", 2)
        chain, halves = s.sem("dve_chain"), s.sem("weights_split")
        block = s.block()

        @block.sync
        def _(sp):
            sp.dma_start(w[:, :, :], a["w_wk"]).then_inc(w_in, 16)
            for r in stored:
                sp.sem_inc(r, 16)

            def store(t, u, n, rows):
                sp.wait_ge(ev, t + 3)
                sp.dma_start(c.h_odd[rows_of(t, rows), O_WK:O_WK + N], st[u][0:rows, :]).then_inc(stored[u], 16)
            each_tile(sp, store)
            sp.wait_ge(stored[0], 6 * 16)
            sp.wait_ge(stored[1], 5 * 16)

        @block.tensor
        def _(pe):
            pe.wait_ge(halves, 1)
            for t in range(T + 1):
                rows, u = (P, t % 2) if t < T else (SMP, 0)
                pe.wait_ge(ev, t + 1)
                to = slice(P * t, P * t + rows)
                products(nc.tensor, ps[u][0:rows, 0:N],
                         [((c.xh[:, k, to], c.xl[:, k, to]), (wh[:, k, :], wl[:, k, :]))
                          for k in range(KC)]).then_inc(mm, 1)

        @block.vector
        def _(dve):
            dve.sem_inc(ev, 2)
            dve.wait_ge(w_in, 16)
            split(nc.vector, Link(dve, chain), w[:, :, :], wh[:, :, :], wl[:, :, :]).then_inc(halves, 1)

            def copy(t, u, n, rows):
                dve.wait_ge(mm, t + 1)
                dve.wait_ge(stored[u], n * 16)
                nc.vector.tensor_copy(st[u][0:rows, :], ps[u][0:rows, 0:N]).then_inc(ev, 1)
            each_tile(dve, copy)


def sparse_memory(c, L):
    c.qT = L.sb("qT", [P, QH, TOK])
    c.kT = L.sb("kT", [P, KVH, TOK])
    c.qiT = L.sb("qiT", [P, IH // 2, TOK])
    c.kiT = L.sb("kiT", [P, TOK])
    c.v = L.sb("v", [P, TILES + 1, KVH * HD])
    c.wi = L.sb("wi", [P, TILES + 1, IH])


def sparse_prepare(nc, c, a, o):
    T, QK, H10 = TILES, (QH + KVH) * HD, QH + KVH
    with Stage(nc, "prep") as s:
        qk = [s.sb(f"qk{u}", [P, QK]) for u in range(2)]
        ik = [s.sb(f"ik{u}", [P, (IH + 2) * ID]) for u in range(2)]
        rt = [s.sb(f"rope{u}", [P, 2, HD // 8]) for u in range(2)]
        ri = [s.sb(f"ropei{u}", [P, 2, ID // 8]) for u in range(2)]
        sq = s.sb("sq", [P, QK])
        gam = s.sb("gam", [P, H10, HD])
        ssq = [s.sb(f"ssq{u}", [P, H10]) for u in range(2)]
        tmp = s.sb("tmp", [P, 4, H10, HD // 8])
        tmi = s.sb("tmi", [P, 4, IH + 1, ID // 8])
        ps = [s.ps(f"t{u}", 2048) for u in range(2)]
        qk_in, ik_in, rt_in, v_in, gam_in, stored = (s.sem("qk_in", 2), s.sem("ik_in", 2), s.sem("rope_in", 2),
                                                      s.sem("v_in", 2), s.sem("gamma_in"), s.sem("stored", 2))
        squ, red, rs, sc, gd, rq, ri_d, tr, ev, wd, dch, pch = (s.sem(n) for n in (
            "squares", "sums", "rstd", "scaled", "weighted", "rotated", "index_rotated", "transposed",
            "copied", "wi", "dve_chain", "pool_chain"))
        block = s.block()

        @block.sync
        def _(sp):
            for r in stored:
                sp.sem_inc(r, 48)
            sp.dma_start(gam[:, 0:QH, :], a["attn_qn"].unsqueeze(0).broadcast_to([P, QH, HD])).then_inc(gam_in, 16)
            sp.dma_start(gam[:, QH:H10, :], a["attn_kn"].unsqueeze(0).broadcast_to([P, KVH, HD])).then_inc(gam_in, 16)

            def load(t, u, n, rows):
                sp.wait_ge(tr, t + 1)
                sp.wait_ge(stored[u], n * 48)
                r = rows_of(t, rows)
                tt = bass.ds(t, 1)
                sp.dma_start(qk[u][0:rows, :], c.h_odd[r, 0:QK]).then_inc(qk_in[u], 16)
                sp.dma_start(ik[u][0:rows, 0:IH * ID], c.h_odd[r, O_QI:O_QI + IH * ID]).then_inc(ik_in[u], 16)
                sp.dma_start(ik[u][0:rows, IH * ID:(IH + 1) * ID], c.h_odd[r, O_WK + IH:O_WK + IH + ID])\
                    .then_inc(ik_in[u], 16)
                sp.dma_start(rt[u][0:rows], a["rope"][r]).then_inc(rt_in[u], 16)
                sp.dma_start(ri[u][0:rows], a["rope_idx"][r]).then_inc(rt_in[u], 16)
                sp.dma_start(c.v[0:rows, tt, :].rearrange("p o d -> p (o d)"), c.h_odd[r, O_KV + KVH * HD:O_KV + 2 * KVH * HD])\
                    .then_inc(v_in[u], 16)
                sp.dma_start(c.wi[0:rows, tt, :].rearrange("p o d -> p (o d)"), c.h_odd[r, O_WK:O_WK + IH])\
                    .then_inc(v_in[u], 16)
            each_tile(sp, load)

        @block.scalar
        def _(act):
            act.sem_inc(ev, 2 * 5)
            n_out = KVH * HD

            def copies(t, u, n, rows):
                r = rows_of(t, rows)
                if rows == P:
                    ko, vo, io = (o[x][0, 0, r] for x in (9, 10, 11))
                    ko, vo = (x.rearrange("t h d -> t (h d)") for x in (ko, vo))
                else:
                    ko, vo = (o[x][0].rearrange("b t h d -> (b t) (h d)") for x in (12, 13))
                    io = o[14][0].rearrange("b t d -> (b t) d")
                act.wait_ge(rq, t + 1)
                act.dma_start(ko, qk[u][0:rows, QH * HD:QK]).then_inc(stored[u], 16)
                act.wait_ge(ri_d, t + 1)
                act.dma_start(io, ik[u][0:rows, IH * ID:(IH + 1) * ID]).then_inc(stored[u], 16)
                act.wait_ge(v_in[u], n * 32)
                act.dma_start(vo, c.v[0:rows, bass.ds(t, 1), :].rearrange("p o d -> p (o d)")).then_inc(stored[u], 16)
                act.wait_ge(tr, t + 3)
                to = slice(SEQ, TOK) if rows == SMP else bass.ts(t, P)
                for j, dst in enumerate((c.qT[:, 0:4, to], c.qT[:, 4:8, to], c.qiT[:, :, to])):
                    nc.scalar.activation(dst, heads(ps[u][:, 512 * j:512 * j + 512])[:, :, 0:rows], ACT.Copy).then_inc(ev, 1)
                nc.scalar.activation(c.kT[:, :, to], heads(ps[u][:, 1536:1792], 2)[:, :, 0:rows], ACT.Copy).then_inc(ev, 1)
                nc.scalar.activation(c.kiT[:, to], ps[u][:, 1792:1792 + rows], ACT.Copy).then_inc(ev, 1)
            each_tile(act, copies)
            act.wait_ge(stored[0], 6 * 48)
            act.wait_ge(stored[1], 5 * 48)

        @block.gpsimd
        def _(pool):
            link = Link(pool, pch)
            G = nc.gpsimd

            def work(t, u, n, rows):
                link.at(t * 2)
                x = qk[u][0:rows, :]
                pool.wait_ge(qk_in[u], n * 16)
                pool.wait_ge(red, t + 1)
                G.tensor_tensor(sq[0:rows, :], x, x, ALU.mult).then_inc(squ, 1)
                pool.wait_ge(ik_in[u], n * 32)
                pool.wait_ge(rt_in[u], n * 32)
                v = ik[u][0:rows, 0:(IH + 1) * ID].rearrange("p (h d) -> p h d", d=ID)
                rotate(G, link, v, ID // 8, ri[u], tmi, rows, IH + 1)
                k = ik[u][0:rows, IH * ID:(IH + 1) * ID]
                G.tensor_tensor(ik[u][0:rows, (IH + 1) * ID:], k, c.one[0:rows, :].broadcast_to([rows, ID]), ALU.mult).then_inc(ri_d, 1)
                pool.wait_ge(red, t + 2)
                q = ssq[u][0:rows, :]
                G.tensor_tensor(q, q, c.half[0:rows, 0:H10], ALU.pow).then_inc(rs, 1)
                pool.wait_ge(gam_in, 32)
                pool.wait_ge(sc, t + 1)
                G.tensor_tensor(heads(x, H10), heads(x, H10), gam[0:rows], ALU.mult).then_inc(gd, 1)
            each_tile(pool, work)

        @block.vector
        def _(dve):
            link = Link(dve, dch)
            V = nc.vector
            dve.sem_inc(red, 1)

            def work(t, u, n, rows):
                link.at(t * 3)
                x = heads(qk[u][0:rows, :], H10)
                dve.wait_ge(v_in[u], n * 32)
                w = c.wi[0:rows, bass.ds(t, 1), :]
                V.tensor_scalar(w, w, IH ** -0.5, None, ALU.mult).then_inc(wd, 1)
                dve.wait_ge(squ, t + 1)
                link(V.tensor_reduce(ssq[u][0:rows, :], heads(sq[0:rows, :], H10), AX.X, ALU.add))
                V.tensor_scalar(ssq[u][0:rows, :], ssq[u][0:rows, :], 1.0 / HD, EPS, ALU.mult, ALU.add).then_inc(red, 1)
                dve.wait_ge(rs, t + 1)
                V.tensor_tensor(x, x, bc(ssq[u][0:rows, :], 2, HD), ALU.mult).then_inc(sc, 1)
                dve.wait_ge(gd, t + 1)
                dve.wait_ge(rt_in[u], n * 32)
                rotate(V, link, x, HD // 8, rt[u], tmp, rows, H10)
                dve.sem_inc(rq, 1)
            each_tile(dve, work)

        @block.tensor
        def _(pe):
            pe.sem_inc(tr, 2)

            def transposes(t, u, n, rows):
                pe.wait_ge(rq, t + 1)
                pe.wait_ge(ri_d, t + 1)
                pe.wait_ge(ev, t * 5 + 5)
                I = c.ident[0:rows, 0:rows]
                for h in range(QH):
                    nc.tensor.transpose(ps[u][:, P * h:P * h + rows], qk[u][0:rows, P * h:P * h + P], I)
                for h in range(IH // 2):
                    nc.tensor.transpose(ps[u][:, 1024 + P * h:1024 + P * h + rows], ik[u][0:rows, P * h:P * h + P], I)
                for h in range(KVH):
                    nc.tensor.transpose(ps[u][:, 1536 + P * h:1536 + P * h + rows],
                                        qk[u][0:rows, P * (QH + h):P * (QH + h + 1)], I)
                nc.tensor.transpose(ps[u][:, 1792:1792 + rows], ik[u][0:rows, IH * ID:(IH + 2) * ID], I).then_inc(tr, 1)
            each_tile(pe, transposes)


def rotate(eng, link, x, half, table, tmp, rows, n):
    cos, sin = (bc(table[0:rows, j, :], 1, n) for j in range(2))
    x1, x2 = x[:, :, 0:half], x[:, :, half:2 * half]
    t = [tmp[0:rows, j] for j in range(4)]
    eng.tensor_tensor(t[0], x1, cos, ALU.mult)
    eng.tensor_tensor(t[1], x2, sin, ALU.mult)
    eng.tensor_tensor(t[2], x2, cos, ALU.mult)
    link(eng.tensor_tensor(t[3], x1, sin, ALU.mult))
    eng.tensor_tensor(x1, t[0], t[1], ALU.subtract)
    link(eng.tensor_tensor(x2, t[2], t[3], ALU.add))


def pick_top(dve, link, scores, best):
    for _ in range(TOPK // 8):
        link(dve.max(best, scores))
        link(dve.match_replace(scores, best, scores, TAKEN))


def sparse_prompt(nc, c):
    B, FIRST = TILES, TOPK // P
    SC = HD ** -0.5
    with Stage(nc, "sparse_p") as s:
        relu = [s.sb(f"relu{u}", [P, SEQ]) for u in range(2)]
        acc = s.sb("scores", [P, SEQ])
        best = s.sb("best", [P, 8])
        bias = [s.sb(f"bias{u}", [P, SEQ]) for u in range(2)]
        sm = [s.sb(f"masked{u}", [P, SEQ]) for u in range(2)]
        pr = [s.sb(f"p{u}", [P, SEQ]) for u in range(2)]
        pT = [s.sb(f"pT{u}", [P, B, P]) for u in range(2)]
        mx, neg, tot, rec = ([s.sb(f"{n}{u}", [P, 1]) for u in range(2)] for n in ("max", "neg", "total", "rec"))
        gc = [s.sb(f"gate{u}", [P, QH * HD]) for u in range(2)]
        yb = [s.sb(f"y{u}", [P, QH * HD]) for u in range(2)]
        psS = [s.ps(f"s{u}", 1024) for u in range(2)]
        psT = s.ps("t", 1024)
        psO = [s.ps(f"o{u}") for u in range(2)]
        g_in, stored = s.sem("gate_in", 2), s.sem("stored", 2)
        xs, xr, xa, bd, ss, md, ng, ex, tr, te, od, rc, yd, dch = (s.sem(n) for n in (
            "index_scores", "relus", "added", "bias", "scores", "masked", "neg_max", "exps", "transposed", "pT_copied",
            "mixed", "reciprocal", "y", "dve_chain"))
        block = s.block()
        job = lambda i, h: QH * i + h
        idx = lambda i, h: IH * (i - FIRST) + h

        def blocks(index, attend):
            for i in range(B):
                if FIRST <= i + 1 < B:
                    index(i + 1, (i + 2) * P)
                attend(i, (i + 1) * P)

        @block.sync
        def _(sp):
            for i in range(B):
                if i >= 2:
                    sp.wait_ge(yd, job(i - 2, QH - 1) + 1)
                sp.dma_start(gc[i % 2][:, :], c.h_odd[P * i:P * i + P, O_GC:O_GC + QH * HD]).then_inc(g_in[i % 2], 16)
                if i >= 1:
                    j = i - 1
                    sp.wait_ge(yd, job(j, QH - 1) + 1)
                    sp.dma_start(c.y_odd[P * j:P * j + P, 0:QH * HD], yb[j % 2][:, :]).then_inc(stored[j % 2], 16)
            j = B - 1
            sp.wait_ge(yd, job(j, QH - 1) + 1)
            sp.dma_start(c.y_odd[P * j:P * j + P, 0:QH * HD], yb[j % 2][:, :]).then_inc(stored[j % 2], 16)
            sp.wait_ge(stored[0], B // 2 * 16)
            sp.wait_ge(stored[1], B // 2 * 16)

        @block.tensor
        def _(pe):
            def keys(n):
                return [(k, min(512, n - k)) for k in range(0, n, 512)]

            def index(i, n):
                for h in range(IH):
                    u, at = h % 2, ID * (h % 2)
                    if h < 2 and i > FIRST:
                        pe.wait_ge(md, job(i - 1, 0))
                    if h >= 2:
                        pe.wait_ge(xr, idx(i, h) - 1)
                    for k, m in keys(n):
                        ins = nc.tensor.matmul(psS[u][:, k:k + m], c.qiT[at:at + ID, h // 2, P * i:P * i + P],
                                               c.kiT[at:at + ID, k:k + m], start=True, stop=True)
                    ins.then_inc(xs, 1)

            def scores(i, h, n):
                g = job(i, h)
                if h < 2:
                    if i + 1 >= FIRST:
                        pe.wait_ge(xr, idx(min(i + 1, B - 1), IH))
                    if i >= 1:
                        pe.wait_ge(md, job(i, 0))
                else:
                    pe.wait_ge(md, g - 1)
                for k, m in keys(n):
                    ins = nc.tensor.matmul(psS[g % 2][:, k:k + m], c.qT[:, h, P * i:P * i + P],
                                           c.kT[:, h // 4, k:k + m], start=True, stop=True)
                ins.then_inc(ss, 1)

            def attend(i, n):
                scores(i, 0, n)
                for h in range(QH):
                    g = job(i, h)
                    if h + 1 < QH:
                        scores(i, h + 1, n)
                    pe.wait_ge(ex, g + 1)
                    if g:
                        pe.wait_ge(te, g)
                    for k in range(i + 1):
                        ins = nc.tensor.transpose(psT[:, P * k:P * k + P], pr[g % 2][:, P * k:P * k + P], c.ident[:, :])
                    ins.then_inc(tr, 1)
                    pe.wait_ge(te, g + 1)
                    if g >= 2:
                        pe.wait_ge(yd, g - 1)
                    for k in range(i + 1):
                        ins = nc.tensor.matmul(psO[g % 2][:, 0:P], pT[g % 2][:, k, :],
                                               c.v[:, k, HD * (h // 4):HD * (h // 4) + HD], start=(k == 0), stop=(k == i))
                    ins.then_inc(od, 1)
            blocks(index, attend)

        @block.scalar
        def _(act):
            def index(i, n):
                for h in range(IH):
                    act.wait_ge(xs, idx(i, h) + 1)
                    if idx(i, h) >= 2:
                        act.wait_ge(xa, idx(i, h) - 1)
                    nc.scalar.activation(relu[h % 2][:, 0:n], psS[h % 2][:, 0:n], ACT.Relu, scale=ID ** -0.5)\
                        .then_inc(xr, 1)

            def attend(i, n):
                for h in range(QH):
                    g = job(i, h)
                    act.wait_ge(ng, g + 1)
                    nc.scalar.activation(pr[g % 2][:, 0:n], sm[g % 2][:, 0:n], ACT.Exp, bias=neg[g % 2][:, :],
                                         scale=SC, accum_out=tot[g % 2][:, :]).then_inc(ex, 1)
                    act.wait_ge(tr, g + 1)
                    nc.scalar.activation(pT[g % 2][:, 0:i + 1, :], psT[:, 0:n].rearrange("p (k q) -> p k q", q=P),
                                         ACT.Copy).then_inc(te, 1)
            blocks(index, attend)

        @block.vector
        def _(dve):
            V = nc.vector
            link = Link(dve, dch)
            base = 0

            def index(i, n):
                for h in range(IH):
                    w = c.wi[:, i, h:h + 1]
                    dve.wait_ge(xr, idx(i, h) + 1)
                    if h == 0:
                        ins = V.tensor_scalar(acc[:, 0:n], relu[0][:, 0:n], w, None, ALU.mult)
                    else:
                        ins = V.scalar_tensor_tensor(acc[:, 0:n], relu[h % 2][:, 0:n], w, acc[:, 0:n], ALU.mult, ALU.add)
                    ins.then_inc(xa, 1)
                    dve.wait_ge(xa, idx(i, h) + 1)
                link(V.tensor_tensor(acc[:, n - P:n], acc[:, n - P:n], c.lid_qk[:, :], ALU.min))
                pick_top(dve, link, acc[:, 0:n], best[:, :])
                link(V.tensor_scalar(bias[i % 2][:, 0:n], acc[:, 0:n], -3.2e38, NEG, ALU.is_gt, ALU.mult))

            def masked(i, h, n):
                g = job(i, h)
                dve.wait_ge(ss, g + 1)
                if g >= 2:
                    dve.wait_ge(ex, g - 1)
                V.tensor_tensor_reduce(sm[g % 2][:, 0:n], psS[g % 2][:, 0:n], bias[i % 2][:, 0:n], 1.0, -3.4e38,
                                       ALU.add, ALU.max, mx[g % 2][:, :]).then_inc(md, 1)
                dve.wait_ge(md, g + 1)
                V.tensor_scalar(neg[g % 2][:, :], mx[g % 2][:, :], -SC, None, ALU.mult).then_inc(ng, 1)

            def attend(i, n):
                if i < FIRST:
                    if i:
                        link(V.memset(bias[i][:, 0:n - P], 0.0))
                    link(V.tensor_copy(bias[i][:, n - P:n], c.neg_qk[:, :]))
                masked(i, 0, n)
                dve.wait_ge(g_in[i % 2], 16 * (i // 2 + 1))
                if i >= 2:
                    dve.wait_ge(stored[i % 2], 16 * (i // 2))
                for h in range(QH):
                    g = job(i, h)
                    if h + 1 < QH:
                        masked(i, h + 1, n)
                    dve.wait_ge(ex, g + 1)
                    V.reciprocal(rec[g % 2][:, :], tot[g % 2][:, :]).then_inc(rc, 1)
                    dve.wait_ge(rc, g + 1)
                    dve.wait_ge(od, g + 1)
                    e = slice(P * h, P * h + P)
                    V.scalar_tensor_tensor(yb[i % 2][:, e], psO[g % 2][:, 0:P], rec[g % 2][:, :], gc[i % 2][:, e],
                                           ALU.mult, ALU.mult).then_inc(yd, 1)
            blocks(index, attend)


def sparse_sample(nc, c, a):
    SC = HD ** -0.5
    N = PAST + NT
    with Stage(nc, "sparse_s") as s:
        pt_sb = s.sb("pages", [1, NB * PAGES], mybir.dt.int32)
        ip = [s.sb(f"ip{u}", [P, PAGES, 2 * ID]) for u in range(2)]
        kp = [s.sb(f"kp{u}", [P, PAGES, KVH * HD]) for u in range(2)]
        vp = [s.sb(f"vp{u}", [P, PAGES, KVH * HD]) for u in range(2)]
        kT = [s.sb(f"kT{u}", [P, 1024]) for u in range(2)]
        qiT, qT = s.sb("qiT", [P, P]), s.sb("qT", [P, KVH, P])
        qim, qm = s.sb("qim", [P, NB, P]), s.sb("qm", [P, KVH, NB, P])
        wr = s.sb("w_rows", [P, 2])
        ok, okr = s.sb("ok", [SMP, NT]), s.sb("ok_rows", [P, NT])
        xr = s.sb("relus", [P, 2, N])
        tmp = s.sb("tmp", [P, KVH, NB * NT])
        acc = s.sb("scores", [SMP, N])
        best = s.sb("best", [SMP, 8])
        new = s.sb("new", [P, KVH, NT])
        mxa, mxb, neg, tot, totb = (s.sb(n, [P, KVH]) for n in ("mxa", "mxb", "neg", "tot", "totb"))
        pr = s.sb("p", [P, KVH, N])
        pn = s.sb("p_new", [P, KVH, NB * NT])
        pT = s.sb("pT", [P, KVH, PAGES, P])
        pnT = s.sb("p_newT", [NB * NT, KVH, P])
        oT = s.sb("oT", [P, KVH, P])
        gc, y = s.sb("gate", [SMP, QH * HD]), s.sb("y", [SMP, QH * HD])
        psX = [s.ps(f"x{u}", 1024) for u in range(2)]
        psT = [s.ps(f"t{u}", 1024) for u in range(2)]
        t_in, ip_in, kp_in, vp_in, g_in, out = (s.sem("table_in"), s.sem("ip_in", 2), s.sem("kp_in", 2),
                                                s.sem("vp_in", 2), s.sem("gate_in"), s.sem("stored"))
        (qd, itr, ica, icd, ixs, inw, xrd, xsum, sel, ktr, kca, ssd, biased, nw, nwr, ngd, exd, pnd, ptr, pte, pnt,
         od, oe, otr, yd, dch, ach) = (s.sem(n) for n in (
            "queries", "ip_transposed", "ipT_by_act", "ipT_by_dve", "index_scores", "index_new", "relus", "index_sums",
            "selected", "k_transposed", "kT_copied", "scores", "bias", "new_scores", "new_read", "neg_max", "exps",
            "p_normed", "p_transposed", "pT_copied", "p_new_transposed", "mixed", "oT_copied", "o_transposed", "y",
            "dve_chain", "act_chain"))
        xsr, xsr2 = s.sem("relus_read"), s.sem("index_sums_read")
        block = s.block()

        @block.sync
        def _(sp):
            sp.dma_start(pt_sb[:, :], a["page_table"].rearrange("b p -> (b p)").unsqueeze(0)).then_inc(t_in, 16)
            sp.dma_start(gc[:, :], c.h_odd[SEQ:TOK, O_GC:O_GC + QH * HD]).then_inc(g_in, 16)
            sp.wait_ge(t_in, 16)
            n_pool = a["cache_attn_k"].shape[1]

            def pages(b, body):
                for p in range(PAGES):
                    page = sp.value_load(pt_sb[0:1, PAGES * b + p:PAGES * b + p + 1], min_val=0, max_val=n_pool - 1)
                    body(p, bass.ds(page, 1))
            for b in range(NB):
                u = b % 2
                if b >= 2:
                    sp.wait_ge(itr, b - 1)

                def load(p, page):
                    src = a["cache_idx_k"][0, page].rearrange("o s d -> (o s) d")
                    for j in range(2):
                        sp.dma_start(ip[u][:, p, ID * j:ID * j + ID], src).then_inc(ip_in[u], 16)
                pages(b, load)
            for b in range(NB):
                u = b % 2
                if b >= 2:
                    sp.wait_ge(ktr, KVH * (b - 1))

                def load(p, page):
                    sp.dma_start(kp[u][:, p, :], a["cache_attn_k"][0, page].rearrange("o s h d -> (o s) (h d)"))\
                        .then_inc(kp_in[u], 16)
                pages(b, load)
            for b in range(NB):
                u = b % 2
                if b >= 2:
                    sp.wait_ge(od, b - 1)

                def load(p, page):
                    sp.dma_start(vp[u][:, p, :], a["cache_attn_v"][0, page].rearrange("o s h d -> (o s) (h d)"))\
                        .then_inc(vp_in[u], 16)
                pages(b, load)
            sp.wait_ge(yd, 1)
            sp.dma_start(c.y_odd[SEQ:TOK, 0:QH * HD], y[:, :]).then_inc(out, 16)
            sp.wait_ge(out, 16)

        @block.tensor
        def _(pe):
            T = nc.tensor
            pe.wait_ge(qd, 1)
            for b in range(NB):
                u = b % 2
                pe.wait_ge(ip_in[u], (b // 2 + 1) * 2 * PAGES * 16)
                if b >= 2:
                    pe.wait_ge(ica, b - 1)
                    pe.wait_ge(icd, b - 1)
                for p in range(PAGES):
                    ins = T.transpose(psT[u][:, P * p:P * p + P], ip[u][:, p, :], c.ident[:, :])
                ins.then_inc(itr, 1)
                pe.wait_ge(ica, b + 1)
                pe.wait_ge(icd, b + 1)
                for j in range(2):
                    e = slice(ID * j, ID * j + ID)
                    for k in range(2):
                        ins = T.matmul(psX[j][:, 512 * k:512 * k + 512], qim[e, b, :], kT[u][e, 512 * k:512 * k + 512],
                                       start=(b == 0), stop=(b == NB - 1), skip_group_check=True)
                ins.then_inc(ixs, 1)
            for j in range(2):
                e = slice(ID * j, ID * j + ID)
                ins = T.matmul(psT[j][:, 0:SMP], qiT[e, :], c.kiT[e, SEQ:TOK], start=True, stop=True)
            ins.then_inc(inw, 1)
            pe.wait_ge(xrd, 6)
            for k, m in ((0, 512), (512, 512)):
                for j in range(2):
                    T.matmul(psX[0][0:SMP, k:k + m], c.tok_of[:, :], xr[:, j, k:k + m], start=(j == 0), stop=(j == 1))
            for j in range(2):
                ins = T.matmul(psX[1][0:SMP, 0:NT], c.tok_of[:, :], xr[:, j, PAST:N], start=(j == 0), stop=(j == 1))
            ins.then_inc(xsum, 1)
            pe.wait_ge(xsr2, 2)
            for b in range(NB):
                u = b % 2
                pe.wait_ge(kp_in[u], (b // 2 + 1) * PAGES * 16)
                for n in range(KVH):
                    g = KVH * b + n
                    if g >= 2:
                        pe.wait_ge(kca, 2 * (g - 1))
                    for p in range(PAGES):
                        ins = T.transpose(psT[n][:, P * p:P * p + P], kp[u][:, p, HD * n:HD * n + HD], c.ident[:, :])
                    ins.then_inc(ktr, 1)
                    pe.wait_ge(kca, 2 * (g + 1))
                    for k in range(2):
                        ins = T.matmul(psX[n][:, 512 * k:512 * k + 512], qm[:, n, b, :], kT[n][:, 512 * k:512 * k + 512],
                                       start=(b == 0), stop=False, skip_group_check=True)
                    ins.then_inc(ssd, 1)
            pe.wait_ge(sel, 1)
            for n in range(KVH):
                for k in range(2):
                    T.matmul(psX[n][:, 512 * k:512 * k + 512], c.tok_to[:, :], acc[:, 512 * k:512 * k + 512],
                             start=False, stop=True, skip_group_check=True)
                T.matmul(psT[0][:, SMP * n:SMP * n + SMP], qT[:, n, :], c.kT[:, n, SEQ:TOK], start=True, stop=True)
            T.matmul(psT[0][:, 64:64 + NT], c.tok_to[:, :], acc[:, PAST:N], start=True, stop=True).then_inc(biased, 1)
            pe.wait_ge(pnd, 2)
            for n in range(KVH):
                if n:
                    pe.wait_ge(pte, 1)
                for p in range(PAGES):
                    ins = T.transpose(psT[n][:, P * p:P * p + P], pr[:, n, P * p:P * p + P], c.ident[:, :])
                ins.then_inc(ptr, 1)
            pe.wait_ge(pte, 2)
            for n in range(KVH):
                ins = T.transpose(psT[0][0:SMP, P * n:P * n + P], pn[:, n, :], c.ident[:, :])
            ins.then_inc(pnt, 1)
            pe.wait_ge(pte, 3)
            for b in range(NB):
                u = b % 2
                pe.wait_ge(vp_in[u], (b // 2 + 1) * PAGES * 16)
                for n in range(KVH):
                    def own(t):
                        return t.rearrange("p (g b t) -> p g b t", g=4, b=NB)[:, :, b, :]
                    for p in range(PAGES):
                        T.matmul(own(psT[1][:, P * n:P * n + P]), vp[u][:, p, HD * n:HD * n + HD], own(pT[:, n, p, :]),
                                 start=(p == 0), stop=False)
                    ins = T.matmul(own(psT[1][:, P * n:P * n + P]), c.v[0:SMP, TILES, HD * n:HD * n + HD],
                                   own(pnT[:, n, :]), start=False, stop=True)
                ins.then_inc(od, 1)
            pe.wait_ge(oe, 1)
            for n in range(KVH):
                for g in range(4):
                    ins = T.transpose(psX[0][0:SMP, P * (4 * n + g):P * (4 * n + g) + P],
                                      oT[:, n, SMP * g:SMP * g + SMP], c.ident[:, :])
            ins.then_inc(otr, 1)

        @block.scalar
        def _(act):
            A = nc.scalar.activation
            link = Link(act, ach)
            for b in range(NB):
                u = b % 2
                act.wait_ge(itr, b + 1)
                if b >= 2:
                    act.wait_ge(ixs, b - 1)
                A(kT[u][:, 0:512], psT[u][:, 0:512], ACT.Copy).then_inc(ica, 1)
            act.wait_ge(ixs, NB)
            for j in range(2):
                A(xr[:, j, 0:PAST], psX[j][:, :], ACT.Relu, scale=ID ** -0.5).then_inc(xsr, 1)
            act.wait_ge(inw, 1)
            for j in range(2):
                A(tmp[:, j, :], psT[j][:, 0:SMP], ACT.Relu, scale=ID ** -0.5).then_inc(xsr, 1)
            for g in range(KVH * NB):
                n = g % 2
                act.wait_ge(ktr, g + 1)
                if g >= 2:
                    act.wait_ge(ssd, g - 1)
                for k in range(2):
                    A(kT[n][:, 512 * k:512 * k + 512], psT[n][:, 512 * k:512 * k + 512], ACT.Copy).then_inc(kca, 1)
            act.wait_ge(ngd, 1)
            for n in range(KVH):
                A(pr[:, n, 0:PAST], psX[n][:, :], ACT.Exp, bias=neg[:, n:n + 1], scale=SC,
                  accum_out=tot[:, n:n + 1]).then_inc(exd, 1)
                A(pr[:, n, PAST:N], new[:, n, :], ACT.Exp, bias=neg[:, n:n + 1], scale=SC,
                  accum_out=totb[:, n:n + 1]).then_inc(exd, 1)
            for n in range(KVH):
                act.wait_ge(ptr, n + 1)
                A(pT[:, n, :, :], psT[n][:, :].rearrange("p (k q) -> p k q", q=P), ACT.Copy).then_inc(pte, 1)
            act.wait_ge(pnt, 1)
            A(pnT[:, :, :], heads(psT[0][0:SMP, 0:KVH * P], KVH), ACT.Copy).then_inc(pte, 1)
            act.wait_ge(od, NB)
            A(oT[:, :, :], heads(psT[1][:, 0:KVH * P], KVH), ACT.Copy).then_inc(oe, 1)

        @block.vector
        def _(dve):
            V = nc.vector
            link = Link(dve, dch)
            own = c.of_seq
            link(V.tensor_copy(qiT[:, :].rearrange("p (g t) -> p g t", g=4), c.qiT[:, :, SEQ:TOK]))
            link(V.tensor_copy(qT[:, :, :].rearrange("p n (g t) -> p (n g) t", g=4), c.qT[:, :, SEQ:TOK]))
            for b in range(NB):
                col = bc(c.seq_cols[:, b, :], 1, 4)
                V.tensor_tensor(qim[:, b, :].rearrange("p (g t) -> p g t", g=4),
                                qiT[:, :].rearrange("p (g t) -> p g t", g=4), col, ALU.mult)
                for n in range(KVH):
                    ins = V.tensor_tensor(qm[:, n, b, :].rearrange("p (g t) -> p g t", g=4),
                                          qT[:, n, :].rearrange("p (g t) -> p g t", g=4), col, ALU.mult)
            ins.then_inc(qd, 1)
            for g in range(4):
                link(V.tensor_copy(wr[SMP * g:SMP * g + SMP, :], c.wi[0:SMP, TILES, 2 * g:2 * g + 2]))
            link(V.tensor_reduce(ok[:, :], c.causal_smp[:, :].rearrange("p (b j) -> p j b", j=NT), AX.X, ALU.add))
            for g in range(4):
                link(V.tensor_copy(okr[SMP * g:SMP * g + SMP, :], ok[:, :]))
            for b in range(NB):
                u = b % 2
                dve.wait_ge(itr, b + 1)
                if b >= 2:
                    dve.wait_ge(ixs, b - 1)
                V.tensor_copy(kT[u][:, 512:1024], psT[u][:, 512:1024]).then_inc(icd, 1)
            dve.wait_ge(xsr, 4)
            for j in range(2):
                V.tensor_scalar(xr[:, j, 0:PAST], xr[:, j, 0:PAST], wr[:, j:j + 1], None, ALU.mult).then_inc(xrd, 1)
                link(V.tensor_scalar(tmp[:, j, :], tmp[:, j, :], wr[:, j:j + 1], None, ALU.mult))
                t = tmp[:, j, :].rearrange("p (b j) -> p b j", j=NT)
                V.tensor_tensor(t, t, bc(own[:, :], 2, NT), ALU.mult).then_inc(xrd, 1)
                dve.wait_ge(xrd, 3 * j + 2)
                V.tensor_reduce(xr[:, j, PAST:N], tmp[:, j, :].rearrange("p (b j) -> p j b", j=NT), AX.X, ALU.add)\
                    .then_inc(xrd, 1)
            dve.wait_ge(xsum, 1)
            V.tensor_copy(acc[:, 0:PAST], psX[0][0:SMP, :]).then_inc(xsr2, 1)
            V.tensor_copy(acc[:, PAST:N], psX[1][0:SMP, 0:NT]).then_inc(xsr2, 1)
            dve.wait_ge(xsr2, 2)
            link(V.tensor_tensor(acc[:, PAST:N], acc[:, PAST:N], ok[:, :], ALU.mult))
            link(V.tensor_scalar(ok[:, :], ok[:, :], 1.0, 3.0e38, ALU.subtract, ALU.mult))
            link(V.tensor_tensor(acc[:, PAST:N], acc[:, PAST:N], ok[:, :], ALU.add))
            pick_top(dve, link, acc[:, :], best[:, :])
            V.tensor_scalar(acc[:, :], acc[:, :], -3.2e38, NEG, ALU.is_gt, ALU.mult).then_inc(sel, 1)
            dve.wait_ge(biased, 1)
            for n in range(KVH):
                link(V.tensor_reduce(mxa[:, n:n + 1], psX[n][:, :], AX.X, ALU.max))
            t = tmp[:, :, :].rearrange("p n (b j) -> p n b j", j=NT)
            for n in range(KVH):
                link(V.tensor_tensor(t[:, n], psT[0][:, SMP * n:SMP * n + SMP].rearrange("p (b j) -> p b j", j=NT),
                                     bc(own[:, :], 2, NT), ALU.mult))
                link(V.tensor_reduce(new[:, n, :], tmp[:, n, :].rearrange("p (b j) -> p j b", j=NT), AX.X, ALU.add))
                link(V.tensor_tensor(new[:, n, :], new[:, n, :], psT[0][:, 64:64 + NT], ALU.add))
            link(V.tensor_reduce(mxb[:, :], new[:, :, :], AX.X, ALU.max))
            link(V.tensor_tensor(mxa[:, :], mxa[:, :], mxb[:, :], ALU.max))
            V.tensor_scalar(neg[:, :], mxa[:, :], -SC, None, ALU.mult).then_inc(ngd, 1)
            dve.wait_ge(exd, 4)
            link(V.tensor_tensor(tot[:, :], tot[:, :], totb[:, :], ALU.add))
            link(V.reciprocal(tot[:, :], tot[:, :]))
            V.tensor_tensor(pr[:, :, :], pr[:, :, :], bc(tot[:, :], 2, N), ALU.mult).then_inc(pnd, 1)
            dve.wait_ge(pnd, 1)
            for n in range(KVH):
                ins = V.tensor_tensor(pn[:, n, :].rearrange("p (b j) -> p b j", j=NT), bc(pr[:, n, PAST:N], 1, NB),
                                      bc(own[:, :], 2, NT), ALU.mult)
            ins.then_inc(pnd, 1)
            dve.wait_ge(otr, 1)
            dve.wait_ge(g_in, 16)
            V.tensor_tensor(y[:, :], psX[0][0:SMP, :], gc[:, :], ALU.mult).then_inc(yd, 1)


OUTS = [(1, SEQ, D), (NB, NT, D), (1, 1, NH, HD, HD), (1, 1, NH, HD), (1, 1, NH), (1, NB, NH, HD, HD),
        (1, NB, NH, HD), (1, NB, NH), (1, NB, NT, NH * HD), (1, 1, SEQ, KVH, HD), (1, 1, SEQ, KVH, HD),
        (1, 1, SEQ, ID), (1, NB, NT, KVH, HD), (1, NB, NT, KVH, HD), (1, NB, NT, ID),
        (2, 1, MEM, NH, HD), (2, 1, MEM, NH, HD)]


class Names:
    pass


def decoder(nc, a, o, stop=99):
    c = Names()
    with Stage(nc, "all") as st, nc.allow_non_contiguous_dma(reason="columns of a few hundred elements"):
        c.ident = st.sb("ident", [P, P])
        c.neg_sj = st.sb("neg_sj", [P, P])
        c.neg_qk = st.sb("neg_qk", [P, P])
        c.lid_qk = st.sb("lid_qk", [P, P])
        c.neg_smp = st.sb("neg_smp", [SMP, SMP])
        c.causal_smp = st.sb("causal_smp", [SMP, SMP])
        c.of_seq = st.sb("of_seq", [P, NB])
        c.seq_cols = st.sb("seq_cols", [P, NB, SMP])
        c.head_row = st.sb("head_row", [NH, NH, P])
        c.tok_of = st.sb("tok_of", [P, SMP])
        c.tok_to = st.sb("tok_to", [SMP, P])
        c.causal = st.sb("causal", [P, P])
        c.half = st.sb("half", [P, 16])
        c.eps = st.sb("eps", [P, 16])
        c.inv_d = st.sb("inv_d", [P, 1])
        c.one = st.sb("one", [P, 1])
        c.inv_hd = st.sb("inv_hd", [P, 16])
        c.keysT = st.sb("mem_keysT", [P, 2, NH, MEM])
        c.vals = st.sb("mem_vals", [P, 2, MC, NH * HD])
        c.gates = st.sb("gates", [P, TOK])
        c.h_even = nc.dram_tensor("h_even", [TOK, W_EVEN], F32).ap()
        c.h_odd = nc.dram_tensor("h_odd", [TOK, W_ODD], F32).ap()
        c.y_even = nc.dram_tensor("y_even", [TOK, 1536], F32).ap()
        c.y_odd = nc.dram_tensor("y_odd", [TOK, 1536], F32).ap()
        c.x1 = nc.dram_tensor("x1", [TOK, D], F32).ap()

        def x0(t, rows):
            if rows == SMP:
                return a["x_sample"].rearrange("b t d -> (b t) d")
            return a["x_prompt"][0, bass.ts(t, P), :]

        def x1(t, rows):
            return c.x1[rows_of(t, rows), :]

        def y_out(t, rows):
            if rows == SMP:
                return o[1].rearrange("b t d -> (b t) d")
            return o[0][0, bass.ts(t, P), :]

        constants(nc, c, st)
        with Stage(nc, "layer0") as L:
            projection_memory(c, L, a["w_even"])
            normed_transpose(nc, c, "norm0", x0, a["norm_even"])
            if stop < 1: return
            project(nc, c, "proj0", c.h_even,
                    [(3, (ACT.Copy, ACT.Copy)), (1, (ACT.Silu, ACT.Silu)), (1, (ACT.Silu, ACT.Sigmoid))])
            project_gates(nc, c, a)
        if stop < 2: return
        memory_keys(nc, c, a, o)
        if stop < 3: return
        mlstm(nc, c, a, o)
        if stop < 4: return
        gmlp(nc, c, a, o)
        if stop < 5: return
        with Stage(nc, "end0") as L:
            out_memory(c, L, a["w_out_even"])
            memory_attention(nc, c, a, 0, c.h_even, E_XQ, E_GX, c.y_even, 1024)
            if stop < 6: return
            out_project(nc, c, "out0", c.y_even, x0, x1)
        if stop < 7: return
        with Stage(nc, "layer1") as L:
            projection_memory(c, L, a["w_odd"])
            normed_transpose(nc, c, "norm1", x1, a["norm_odd"])
            project(nc, c, "proj1", c.h_odd,
                    [(2, (ACT.Copy, ACT.Copy)), (1, (ACT.Copy, ACT.Silu)), (1, (ACT.Silu, ACT.Silu))])
            project_indexer(nc, c, a)
        if stop < 8: return
        with Stage(nc, "sparse") as L:
            sparse_memory(c, L)
            sparse_prepare(nc, c, a, o)
            if stop < 9: return
            sparse_prompt(nc, c)
            if stop < 10: return
            sparse_sample(nc, c, a)
        if stop < 11: return
        with Stage(nc, "end1") as L:
            out_memory(c, L, a["w_out_odd"])
            memory_attention(nc, c, a, 1, c.h_odd, O_XQ, O_GX, c.y_odd, 1024)
            out_project(nc, c, "out1", c.y_odd, x1, y_out)


def laid_out(inputs):
    f = {n: np.ascontiguousarray(v) for n, v in inputs.items()}

    def chunks(w, columns):
        k = w.reshape(KC, P, -1).transpose(1, 0, 2)
        return np.ascontiguousarray(np.stack([k[:, :, q:q + CW] for q in columns]).reshape(len(columns), P, KC * CW))

    def small(w, columns):
        k = w.reshape(KC, P, -1).transpose(1, 0, 2)
        return np.ascontiguousarray(np.concatenate([k[:, :, q:q + n] for q, n in columns], axis=2))

    we, wo = f["w_in_even"][0], f["w_in_odd"][0]
    r = {n: f[n] for n in ("x_prompt", "x_sample", "state_mlstm_C", "state_mlstm_n", "state_mlstm_m",
                           "cache_attn_k", "cache_attn_v", "cache_idx_k", "cache_mem_k", "cache_mem_v",
                           "page_table", "mem_prompt", "norm_even", "b_if_even", "mlstm_hnorm", "gmlp_ln_g",
                           "gmlp_ln_b", "gmlp_w", "gmlp_b", "norm_odd", "attn_qn", "attn_kn", "mem_qn",
                           "mem_kn")}
    r["w_even"] = chunks(we, [0, 512, 1024, 2568, 3080, 4104, 2056, 3592, 4616, 1536])
    r["w_if"] = small(we, [(2048, 8)])
    r["w_odd"] = chunks(wo, [0, 512, 1024, 2560, 3144, 1536, 2048, 3656])
    r["w_wk"] = small(wo, [(3072, 72)])
    r["w_mem"] = np.stack([chunks(f["w_mem_kv"][l], [0, 512]) for l in range(2)])
    for n in ("even", "odd"):
        r[f"w_out_{n}"] = np.ascontiguousarray(f[f"w_out_{n}"][0].reshape(12, P, D).transpose(1, 0, 2))
    pos = np.arange(TOK, dtype=np.float32)
    pos[SEQ:] = PAST + np.arange(SMP) % NT
    for n, half in (("rope", HD // 8), ("rope_idx", ID // 8)):
        inv = np.float32(500000.0) ** (-np.arange(half, dtype=np.float32) / np.float32(half))
        ang = (pos[:, None] * inv[None, :].astype(np.float32)).astype(np.float32)
        r[n] = np.stack([np.cos(ang), np.sin(ang)], axis=1).astype(np.float32)
    return r


def kernel(**inputs):
    import numpy as _np
    import concourse.bacc as _bacc
    from concourse import mybir as _mybir
    from concourse.bass_utils import run_bass_kernel_spmd as _run

    nc = _bacc.Bacc("TRN2", target_bir_lowering=False, num_devices=1)
    arrays, a = {}, {}
    for name, v in laid_out(inputs).items():
        arrays[f"in_{name}"] = v
        a[name] = nc.dram_tensor(f"in_{name}", v.shape, _mybir.dt.from_np(v.dtype), kind="ExternalInput").ap()
    o = [nc.dram_tensor(f"out_{i}", s, F32, kind="ExternalOutput").ap() for i, s in enumerate(OUTS)]
    decoder(nc, a, o)
    r = _run(nc, [arrays], core_ids=[0])
    return tuple(r.results[0][f"out_{i}"] for i in range(len(OUTS)))
```

```python
import concourse.bass as bass
from concourse import mybir
from contextlib import ExitStack
import numpy as np

F32 = mybir.dt.float32
F32R = mybir.dt.float32r
ALU = mybir.AluOpType
ACT = mybir.ActivationFunctionType
AX = mybir.AxisListType

P = 128
D = 1024
KC = D // P
SEQ = 1024
NB, NT = 8, 4
SMP = NB * NT
TOK = SEQ + SMP
TILES = SEQ // P
HD = 128
NH = 4
MEM = 256
MC = MEM // P
QH, KVH = 8, 2
IH, ID = 8, 64
PAGES = 8
PAST = PAGES * P
TOPK = 256
EPS = 1e-6
NEG = -1e30
CUT = -3.0e38
TAKEN = -3.4e38
CW = 512
OUT_CHUNKS = 12
OUT_PIECES = 4
OUT_ROWS = OUT_CHUNKS // OUT_PIECES
W_EVEN = 10 * CW
W_ODD = 8 * CW + 72

E_Q, E_K, E_V, E_U, E_VB, E_XQ, E_GA, E_GB, E_GX, E_O = (CW * n for n in range(10))
O_Q, O_KV, O_QI, O_XQ, O_GC, O_GX, O_WK = 0, 1024, 1536, 2048, 2560, 3584, 4096


class Stage:

    def __init__(self, nc, name):
        self.nc, self.name, self.ctx, self.nums = nc, name, ExitStack(), []

    def __enter__(self):
        return self

    def __exit__(self, *e):
        return self.ctx.__exit__(*e)

    def sb(self, name, shape, dt=F32):
        return self.ctx.enter_context(self.nc.sbuf_tensor(f"{self.name}_{name}", shape, dt))

    def ps(self, name, cols=512):
        return self.ctx.enter_context(self.nc.psum_tensor(f"{self.name}_{name}", [P, cols], F32))

    def sem(self, name, n=None):
        if n is not None:
            return [self.sem(f"{name}{i}") for i in range(n)]
        sem = self.ctx.enter_context(self.nc.semaphore(f"{self.name}_{name}"))
        self.nums.append(sem.num)
        return sem

    def pool_sem(self, name, n=None):
        if n is not None:
            return [self.pool_sem(f"{name}{i}") for i in range(n)]
        return self.nc.alloc_semaphore(f"{self.name}_{name}")

    def clear(self):
        runs = []
        for n in sorted(self.nums):
            if runs and runs[-1][1] == n:
                runs[-1][1] = n + 1
            else:
                runs.append([n, n + 1])
        for lo, hi in runs:
            self.nc.all_engine_barrier(sems_to_clear=range(lo, hi))

    def block(self):
        self.ctx.callback(self.clear)
        return self.ctx.enter_context(self.nc.Block())


def each_tile(eng, body, buffers=2):
    with eng.Fori(0, TILES // buffers) as i:
        for u in range(buffers):
            body(i * buffers + u, u, i + 1, P)
    body(TILES, 0, TILES // buffers + 1, SMP)


def rows_of(t, rows):
    return slice(SEQ, TOK) if rows == SMP else bass.ts(t, P)


class Link:

    def __init__(self, eng, sem):
        self.eng, self.sem, self.base, self.n, self.per = eng, sem, 0, 0, 0

    def __call__(self, ins):
        self.n += 1
        ins.then_inc(self.sem, 1)
        self.eng.wait_ge(self.sem, self.base + self.n)

    def at(self, base):
        self.base, self.n = base, 0


def split(dve, link, x, hi, lo):
    link(dve.tensor_copy(hi, x))
    return dve.tensor_tensor(lo, x, hi, ALU.subtract)


def products(pe, out, terms):
    last = len(terms) - 1
    for k, ((xh, xl), (wh, wl)) in enumerate(terms):
        pe.matmul(out, xh, wh, start=(k == 0), stop=False)
        pe.matmul(out, xh, wl, start=False, stop=False)
        ins = pe.matmul(out, xl, wh, start=False, stop=(k == last))
    return ins


def constants(nc, c, st):
    done = st.sem("made")
    with Stage(nc, "const") as s:
        block = s.block()

        @block.gpsimd
        def _(pool):
            n = [0]

            def link(ins):
                n[0] += 1
                ins.then_inc(done, 1)
                pool.wait_ge(done, n[0])

            def select(t, pattern, base, mult, op, fill):
                link(nc.gpsimd.affine_select(out=t, in_=t, compare_op=op, fill=fill, base=base,
                                             pattern=pattern, channel_multiplier=mult))

            link(nc.gpsimd.memset(c.ident[:, :], 0.0))
            select(c.ident[:, :], [[-1, P]], 0, 1, ALU.not_equal, 1.0)
            link(nc.gpsimd.memset(c.neg_sj[:, :], 0.0))
            select(c.neg_sj[:, :], [[1, P]], 0, -1, ALU.is_ge, NEG)
            link(nc.gpsimd.memset(c.causal[:, :], 1.0))
            select(c.causal[:, :], [[1, P]], 0, -1, ALU.is_ge, 0.0)
            link(nc.gpsimd.memset(c.neg_qk[:, :], 0.0))
            select(c.neg_qk[:, :], [[-1, P]], 0, 1, ALU.is_ge, NEG)
            link(nc.gpsimd.memset(c.lid_qk[:, :], 3.0e38))
            select(c.lid_qk[:, :], [[-1, P]], 0, 1, ALU.is_ge, CUT)
            link(nc.gpsimd.memset(c.neg_smp[:, :], 0.0))
            select(c.neg_smp[:, :], [[1, SMP]], 0, -1, ALU.is_ge, NEG)
            v = c.neg_smp[:, :].rearrange("p (b t) -> p b t", t=NT)
            select(v, [[-NT, NB], [0, NT]], 0, 1, ALU.is_ge, NEG)
            link(nc.gpsimd.memset(c.causal_smp[:, :], 1.0))
            select(c.causal_smp[:, :], [[-1, SMP]], 0, 1, ALU.is_ge, 0.0)
            v = c.causal_smp[:, :].rearrange("p (b t) -> p b t", t=NT)
            select(v, [[NT, NB], [0, NT]], NT - 1, -1, ALU.is_ge, 0.0)
            link(nc.gpsimd.memset(c.of_seq[0:SMP, :], 1.0))
            select(c.of_seq[0:SMP, :], [[-NT, NB]], 0, 1, ALU.is_ge, 0.0)
            select(c.of_seq[0:SMP, :], [[NT, NB]], NT - 1, -1, ALU.is_ge, 0.0)
            for g in range(1, 4):
                link(nc.gpsimd.tensor_copy(c.of_seq[32 * g:32 * g + 32, :], c.of_seq[0:SMP, :]))
            link(nc.gpsimd.memset(c.seq_cols[:, :, :], 1.0))
            select(c.seq_cols[:, :, :], [[-NT, NB], [1, SMP]], 0, 0, ALU.is_ge, 0.0)
            select(c.seq_cols[:, :, :], [[NT, NB], [-1, SMP]], NT - 1, 0, ALU.is_ge, 0.0)
            link(nc.gpsimd.memset(c.head_row[:, :, :], 1.0))
            select(c.head_row[:, :, :], [[1, NH], [0, P]], 0, -1, ALU.is_equal, 0.0)
            for g in range(4):
                link(nc.gpsimd.tensor_copy(c.tok_of[32 * g:32 * g + 32, :],
                                           c.ident[32 * g:32 * g + 32, 32 * g:32 * g + 32]))
                link(nc.gpsimd.tensor_copy(c.tok_to[:, 32 * g:32 * g + 32], c.ident[0:32, 0:32]))
            link(nc.gpsimd.memset(c.half[:, :], -0.5))
            link(nc.gpsimd.memset(c.eps[:, :], EPS))
            link(nc.gpsimd.memset(c.one[:, :], 1.0))
            link(nc.gpsimd.memset(c.inv_d[:, :], 1.0 / D))
            link(nc.gpsimd.memset(c.inv_hd[:, :], 1.0 / HD))


def normed_transpose(nc, c, name, x_of, gamma):
    with Stage(nc, name) as s:
        x = [s.sb(f"x{u}", [P, D]) for u in range(2)]
        gam = s.sb("gamma", [P, D])
        junk = s.sb("squares", [P, D])
        ssq = s.sb("ssq", [P, 2])
        rstd = s.sb("rstd", [P, 2])
        ps = [s.ps(f"t{u}", 1024) for u in range(2)]
        x_in, gam_in = s.sem("x_in", 2), s.sem("gamma_in")
        sq, var, rs, xn = (s.sem(n) for n in ("ssq", "var", "rstd", "xn"))
        xt, ev, dc = s.sem("transposed"), s.sem("evacuated"), s.sem("dve_chain")
        block = s.block()

        @block.sync
        def _(sp):
            sp.dma_start(gam[:, :], gamma.to_broadcast([P, D])).then_inc(gam_in, 16)

            def load(t, u, n, rows):
                sp.wait_ge(xt, t + 1)
                sp.dma_start(x[u][0:rows, :], x_of(t, rows)).then_inc(x_in[u], 16)
            each_tile(sp, load)

        @block.scalar
        def _(act):
            def squares(t, u, n, rows):
                act.wait_ge(x_in[u], n * 16)
                nc.scalar.activation(junk[0:rows, :], x[u][0:rows, :], ACT.Square,
                                     accum_out=ssq[0:rows, u:u + 1]).then_inc(sq, 1)
                act.wait_ge(sq, t + 1)
            each_tile(act, squares)

        @block.gpsimd
        def _(pool):
            link = Link(pool, var)
            for u in range(2):
                load_weights(pool, c, u, u)
            pool.dma_start(c.w_small[:, :, :], c.w_small_from).then_inc(c.small_in, 16)

            def rstds(t, u, n, rows):
                v, r = ssq[0:rows, u:u + 1], rstd[0:rows, u:u + 1]
                pool.wait_ge(sq, t + 1)
                link.at(t * 2)
                link(nc.gpsimd.tensor_tensor(v, v, c.inv_d[0:rows, 0:1], ALU.mult))
                link(nc.gpsimd.tensor_tensor(v, v, c.eps[0:rows, 0:1], ALU.add))
                nc.gpsimd.tensor_tensor(r, v, c.half[0:rows, 0:1], ALU.pow).then_inc(rs, 1)
            each_tile(pool, rstds)

        @block.vector
        def _(dve):
            dve.sem_inc(ev, 4)
            dve.wait_ge(gam_in, 16)
            link = Link(dve, dc)

            def scale(t, u, n, rows=P):
                dve.wait_ge(rs, t + 1)
                nc.vector.scalar_tensor_tensor(x[u][0:rows, :], x[u][0:rows, :], rstd[0:rows, u:u + 1],
                                               gam[0:rows, :], ALU.mult, ALU.mult).then_inc(xn, 1)

            def keep(t, u, n, rows=P):
                dve.wait_ge(xt, t + 3)
                to = slice(SEQ, TOK) if rows == SMP else bass.ts(t, P)
                link.at(t * 2)
                for h in range(2):
                    k4 = slice(4 * h, 4 * h + 4)
                    split(nc.vector, link,
                          ps[u][:, 512 * h:512 * h + 512].rearrange("p (k t) -> p k t", k=4)[:, :, 0:rows],
                          c.xh[:, k4, to], c.xl[:, k4, to]).then_inc(ev, 1)
            two_ahead(dve, scale, keep)
            scale(TILES, 0, TILES // 2 + 1, SMP)
            keep(TILES, 0, TILES // 2 + 1, SMP)

        @block.tensor
        def _(pe):
            pe.sem_inc(xt, 2)

            def transposes(t, u, n, rows):
                pe.wait_ge(xn, t + 1)
                pe.wait_ge(ev, t * 2 + 2)
                for k in range(KC):
                    ins = nc.tensor.transpose(ps[u][:, P * k:P * k + rows], x[u][0:rows, P * k:P * k + P],
                                              c.ident[0:rows, 0:rows])
                ins.then_inc(xt, 1)
            each_tile(pe, transposes)


def projection_memory(c, L, w, small):
    c.xh, c.xl = (L.sb(n, [P, KC, TOK], F32R) for n in ("xT_hi", "xT_lo"))
    c.w_small, c.small_in = L.sb("w_small", [P, KC, small.shape[-1]]), L.pool_sem("small_in")
    c.w_small_from = small
    c.w, c.wraw, c.w_in = w, [L.sb(f"w{u}", [P, KC, CW]) for u in range(2)], L.pool_sem("w_in", 2)


def load_weights(pool, c, u, chunk):
    pool.dma_start(c.wraw[u][:, :, :].rearrange("p k n -> p (k n)"),
                   c.w[bass.ds(chunk, 1), :, :].rearrange("o p n -> (o p) n")).then_inc(c.w_in[u], 16)


def project(nc, c, name, h, runs):
    RING, PER = 6, 2 * (TILES + 1)
    with Stage(nc, name) as s:
        wh = [s.sb(f"w_hi{u}", [P, KC, CW], F32R) for u in range(2)]
        wl = [s.sb(f"w_lo{u}", [P, KC, CW], F32R) for u in range(2)]
        st = [s.sb(f"st{r}", [P, CW]) for r in range(RING)]
        ps = [s.ps(f"acc{r}") for r in range(RING)]
        mm, ev = s.sem("products"), s.sem("evacuated")
        halves, chain = s.sem("weights_split"), s.sem("dve_chain")
        stored = s.sem("stored", RING)
        block = s.block()
        CHUNKS = 2 * sum(n for n, _ in runs)

        def pairs(eng, body):
            at = 0
            for n, funcs in runs:
                with eng.Fori(at, at + n) as i:
                    body(i, funcs)
                at += n

        def order():
            for u in range(2):
                for t in range(TILES + 1):
                    r = u * (TILES + 1) + t
                    yield u, t, r, r % RING, P if t < TILES else SMP

        @block.gpsimd
        def _(pool):
            with pool.Fori(0, CHUNKS // 2 - 1) as i:
                for u in range(2):
                    pool.wait_ge(halves, i * 4 + 2 * u + 2)
                    load_weights(pool, c, u, i * 2 + 2 + u)

        @block.vector
        def _(dve):
            link = Link(dve, chain)
            with dve.Fori(0, CHUNKS // 2) as i:
                for u in range(2):
                    dve.wait_ge(c.w_in[u], i * 16 + 16)
                    dve.wait_ge(mm, i * PER + (u + 1) * (TILES + 1))
                    link.at(i * 4 + u * 2)
                    for k in (0, KC // 2):
                        k4 = slice(k, k + KC // 2)
                        split(nc.vector, link, c.wraw[u][:, k4, :], wh[u][:, k4, :], wl[u][:, k4, :])\
                            .then_inc(halves, 1)

        @block.tensor
        def _(pe):
            pe.sem_inc(mm, PER)

            def tiles(i, funcs):
                for u, t, r, b, rows in order():
                    if t == 0:
                        pe.wait_ge(halves, i * 4 + 2 * u + 2)
                    pe.wait_ge(ev, i * PER + r + 1)
                    to = slice(P * t, P * t + rows)
                    products(nc.tensor, ps[b][0:rows, :],
                             [((c.xh[:, k, to], c.xl[:, k, to]), (wh[u][:, k, :], wl[u][:, k, :]))
                              for k in range(KC)]).then_inc(mm, 1)
            pairs(pe, tiles)

        @block.scalar
        def _(act):
            act.sem_inc(ev, RING)
            for r in range(RING):
                act.sem_inc(stored[r], 16)

            def evacuate(i, funcs):
                for u, t, r, b, rows in order():
                    act.wait_ge(mm, i * PER + PER + r + 1)
                    act.wait_ge(stored[b], (i * (PER // RING) + r // RING + 1) * 16)
                    nc.scalar.activation(st[b][0:rows, :], ps[b][0:rows, :], funcs[u]).then_inc(ev, 1)
            pairs(act, evacuate)

        @block.sync
        def _(sp):
            def store(i, funcs):
                for u, t, r, b, rows in order():
                    sp.wait_ge(ev, i * PER + RING + r + 1)
                    sp.dma_start(h[P * t:P * t + rows, bass.ds(i * (2 * CW) + u * CW, CW)],
                                 st[b][0:rows, :]).then_inc(stored[b], 16)
            pairs(sp, store)
            for r in range(RING):
                sp.wait_ge(stored[r], (sum(n for n, _ in runs) * (PER // RING) + 1) * 16)


def project_gates(nc, c):
    with Stage(nc, "gates") as s:
        w = s.sb("w", [P, KC, 36])
        wh, wl = (s.sb(n, [P, KC, 36], F32R) for n in ("w_hi", "w_lo"))
        ps = [s.ps(f"acc{j}") for j in range(3)]
        N = TOK // 3
        laid, mm, ev = s.sem("laid"), s.sem("products"), s.sem("evacuated")
        chain = s.sem("dve_chain")
        block = s.block()

        @block.vector
        def _(dve):
            nc.vector.memset(w[:, :, :], 0.0).then_inc(laid, 1)
            dve.wait_ge(laid, 1)
            dve.wait_ge(c.small_in, 16)
            nc.vector.tensor_copy(w[:, :, 0:NH], c.w_small[:, :, 0:NH]).then_inc(laid, 1)
            nc.vector.tensor_copy(w[:, :, 32:32 + NH], c.w_small[:, :, NH:2 * NH]).then_inc(laid, 1)
            dve.wait_ge(laid, 3)
            split(nc.vector, Link(dve, chain), w[:, :, :], wh[:, :, :], wl[:, :, :]).then_inc(laid, 1)
            for j in range(3):
                dve.wait_ge(mm, j + 1)
                nc.vector.tensor_copy(c.gates[0:36, j * N:j * N + N], ps[j][0:36, 0:N]).then_inc(ev, 1)
            dve.wait_ge(ev, 3)

        @block.tensor
        def _(pe):
            pe.wait_ge(laid, 4)
            for j in range(3):
                to = slice(j * N, j * N + N)
                products(nc.tensor, ps[j][0:36, 0:N],
                         [((wh[:, k, :], wl[:, k, :]), (c.xh[:, k, to], c.xl[:, k, to]))
                          for k in range(KC)]).then_inc(mm, 1)


def bc(ap, axis, n):
    ap = ap.unsqueeze(axis)
    return ap.broadcast_to([n if i == axis else x for i, x in enumerate(ap.shape)])


def heads(ap, n=NH):
    return ap.rearrange("p (h d) -> p h d", h=n)


def two_ahead(eng, first, second, buffers=2):
    def both(t, u, n):
        first(t + 1, (u + 1) % buffers, n + (u + 1) // buffers)
        second(t, u, n)
    first(0, 0, 1)
    with eng.Fori(0, TILES // buffers - 1) as i:
        for u in range(buffers):
            both(i * buffers + u, u, i + 1)
    for u in range(buffers - 1):
        both(TILES - buffers + u, u, TILES // buffers)
    second(TILES - 1, buffers - 1, TILES // buffers)


def pipelined(eng, *steps):
    def once(t, u, n):
        for f, ahead in steps:
            if ahead:
                f(t + 1, 1 - u, n + u)
            else:
                f(t, u, n)
    for f, ahead in steps:
        if ahead:
            f(0, 0, 1)
    with eng.Fori(0, TILES // 2 - 1) as i:
        for u in range(2):
            once(i * 2 + u, u, i + 1)
    once(TILES - 2, 0, TILES // 2)
    for f, ahead in steps:
        if not ahead:
            f(TILES - 1, 1, TILES // 2)


def memory_keys(nc, c, a, o):
    with Stage(nc, "memkv") as s:
        mem = s.sb("mem", [P, MC, D])
        memT = s.sb("memT", [P, KC, MEM])
        w = [s.sb(f"w{j}", [P, KC, CW]) for j in range(4)]
        kn = s.sb("kn", [P, 2, HD])
        qn = s.sb("qn", [P, 2])
        k = [s.sb(f"k{j}", [P, CW]) for j in range(4)]
        sq = [s.sb(f"sq{j}", [P, CW]) for j in range(4)]
        ssq = s.sb("ssq", [P, 4, NH])
        pt = [s.ps(f"t{j}") for j in range(4)]
        pm = [s.ps(f"m{j}") for j in range(4)]
        mem_in, gam_in, w_in = s.sem("mem_in"), s.sem("gamma_in"), s.sem("w_in", 4)
        mt, mte, kmm, vmm, kraw, vcp, squ, red, rs, kno, kt, kte, chain = (s.sem(n) for n in (
            "memT", "memT_copied", "key_products", "value_products", "keys_copied", "values_copied",
            "squares", "sums", "rstd", "keys_normed", "keys_transposed", "keysT_copied", "pool_chain"))
        dchain, out = s.sem("dve_chain"), s.sem("stored")
        block = s.block()

        @block.sync
        def _(sp):
            sp.dma_start(mem[:, :, :], a["mem_prompt"][0].rearrange("(m p) d -> p m d", p=P)).then_inc(mem_in, 16)
            for j in range(4):
                sp.dma_start(w[j][:, :, :].rearrange("p k n -> p (k n)"), a["w_mem"][j // 2, j % 2])\
                    .then_inc(w_in[j], 16)
            sp.dma_start(kn[:, :, :], a["mem_kn"].unsqueeze(0).broadcast_to([P, 2, HD])).then_inc(gam_in, 16)
            sp.dma_start(qn[:, :], a["mem_qn"].rearrange("l d -> d l")).then_inc(gam_in, 16)
            for l in range(2):
                for m in range(MC):
                    sp.wait_ge(kno, 2 * l + m + 1)
                    sp.dma_start(o[15][l, 0, P * m:P * m + P].rearrange("m h d -> m (h d)"), k[2 * l + m][:, :])\
                        .then_inc(out, 16)
                    sp.wait_ge(vcp, 2 * l + m + 1)
                    sp.dma_start(o[16][l, 0, P * m:P * m + P].rearrange("m h d -> m (h d)"), c.vals[:, l, m, :])\
                        .then_inc(out, 16)
            sp.wait_ge(out, 8 * 16)

        @block.tensor
        def _(pe):
            pe.wait_ge(mem_in, 16)
            for j in range(4):
                for i in range(4):
                    m, kk = j // 2, (j % 2) * 4 + i
                    ins = nc.tensor.transpose(pt[j][:, P * i:P * i + P], mem[:, m, P * kk:P * kk + P], c.ident[:, :])
                ins.then_inc(mt, 1)
            pe.wait_ge(mte, 4)
            for l in range(2):
                for m in range(MC):
                    for v in range(2):
                        pe.wait_ge(w_in[2 * l + v], 16)
                        if l:
                            pe.wait_ge(vcp if v else kraw, m + 1)
                        for kk in range(KC):
                            ins = nc.tensor.matmul(pm[2 * m + v][:, :], memT[:, kk, P * m:P * m + P],
                                                   w[2 * l + v][:, kk, :], start=(kk == 0), stop=(kk == KC - 1))
                        ins.then_inc(vmm if v else kmm, 1)
            for j in range(4):
                pe.wait_ge(kno, j + 1)
                for h in range(NH):
                    ins = nc.tensor.transpose(pt[j][:, P * h:P * h + P], k[j][:, P * h:P * h + P], c.ident[:, :])
                ins.then_inc(kt, 1)

        @block.scalar
        def _(act):
            for j in range(4):
                act.wait_ge(mt, j + 1)
                m, half = j // 2, j % 2
                nc.scalar.activation(memT[:, 4 * half:4 * half + 4, P * m:P * m + P],
                                     heads(pt[j][:, :]), ACT.Copy).then_inc(mte, 1)
            for l in range(2):
                for m in range(MC):
                    act.wait_ge(kmm, 2 * l + m + 1)
                    nc.scalar.activation(k[2 * l + m][:, :], pm[2 * m][:, :], ACT.Copy).then_inc(kraw, 1)
                    act.wait_ge(vmm, 2 * l + m + 1)
                    nc.scalar.activation(c.vals[:, l, m, :], pm[2 * m + 1][:, :], ACT.Copy).then_inc(vcp, 1)
            act.wait_ge(gam_in, 32)
            for j in range(4):
                l, m = j // 2, j % 2
                act.wait_ge(kt, j + 1)
                nc.scalar.activation(c.keysT[:, l, :, P * m:P * m + P], heads(pt[j][:, :]), ACT.Copy,
                                     scale=qn[:, l:l + 1]).then_inc(kte, 1)
            act.wait_ge(kte, 4)

        @block.gpsimd
        def _(pool):
            link = Link(pool, chain)
            for j in range(4):
                pool.wait_ge(kraw, j + 1)
                nc.gpsimd.tensor_tensor(sq[j][:, :], k[j][:, :], k[j][:, :], ALU.mult).then_inc(squ, 1)
            for j in range(4):
                pool.wait_ge(red, j + 1)
                v = ssq[:, j, :]
                link(nc.gpsimd.tensor_tensor(v, v, c.inv_hd[:, 0:NH], ALU.mult))
                link(nc.gpsimd.tensor_tensor(v, v, c.eps[:, 0:NH], ALU.add))
                nc.gpsimd.tensor_tensor(v, v, c.half[:, 0:NH], ALU.pow).then_inc(rs, 1)

        @block.vector
        def _(dve):
            link = Link(dve, dchain)
            for j in range(4):
                dve.wait_ge(squ, j + 1)
                nc.vector.tensor_reduce(ssq[:, j, :], heads(sq[j][:, :]), AX.X, ALU.add).then_inc(red, 1)
            dve.wait_ge(gam_in, 32)
            for j in range(4):
                dve.wait_ge(rs, j + 1)
                kh = heads(k[j][:, :])
                link(nc.vector.tensor_tensor(kh, kh, bc(ssq[:, j, :], 2, HD), ALU.mult))
                nc.vector.tensor_tensor(kh, kh, bc(kn[:, j // 2, :], 1, NH), ALU.mult).then_inc(kno, 1)


def memory_attention(nc, c, a, layer, h, cq, cg, y, cy):
    with Stage(nc, f"memattn{layer}") as s:
        xq = [s.sb(f"q{u}", [P, CW]) for u in range(2)]
        gx = [s.sb(f"gate{u}", [P, CW]) for u in range(2)]
        sq = s.sb("squares", [P, CW])
        qT = [s.sb(f"qT{u}", [P, NH, P]) for u in range(2)]
        pr = [s.sb(f"p{u}", [P, NH * MEM]) for u in range(2)]
        prT = [s.sb(f"pT{u}", [P, NH * MC, P]) for u in range(2)]
        yb = [s.sb(f"y{u}", [P, CW]) for u in range(2)]
        ssq = [s.sb(f"rstd{u}", [P, NH]) for u in range(2)]
        mx = [s.sb(f"max{u}", [P, NH]) for u in range(2)]
        tot = [s.sb(f"total{u}", [P, NH]) for u in range(2)]
        ck = s.sb("ck", [P, NB, MC, CW])
        cv = s.sb("cv", [P, NB, MC, CW])
        ckT = s.sb("ckT", [P, NB, NH, MEM])
        qn = s.sb("qn", [P, 1])
        eps = s.sb("eps", [P, NH])
        qTm = s.sb("qTm", [P, NH, NB, SMP])
        oT = s.sb("oT", [P, NH, SMP])
        psT = s.ps("qT_ps")
        psS = [s.ps(f"s{u}", 1024) for u in range(2)]
        psP = s.ps("pT_ps", 1024)
        psO = s.ps("o_ps")
        q_in, g_in, stored = s.sem("q_in", 2), s.sem("gate_in", 2), s.sem("stored", 2)
        k_in, v_in, n_in = s.pool_sem("ck_in"), s.pool_sem("cv_in"), s.pool_sem("qn_in")
        squ, red, rs, qt, qe, sc, nm, ex, pt, pa, pd, od, yd = (s.sem(n) for n in (
            "squares", "sums", "rstd", "queries_transposed", "queriesT_copied", "scores", "neg_max",
            "exps", "p_transposed", "pT_by_act", "pT_by_dve", "mixed", "y"))
        pc, dc, rcp = s.sem("pool_chain"), s.sem("dve_chain"), s.sem("reciprocals")
        ktr, kca, kcd, masked, pn, oc, ot = (s.sem(n) for n in (
            "ck_transposed", "ckT_by_act", "ckT_by_dve", "masked", "p_normed", "oT_copied", "o_transposed"))
        block = s.block()
        L = TILES

        @block.sync
        def _(sp):
            for r in stored:
                sp.sem_inc(r, 16)

            def load_q(t, u, n, rows=P, first=False):
                if not first:
                    sp.wait_ge(squ, t - 1)
                    sp.wait_ge(qt, t - 1)
                sp.dma_start(xq[u][0:rows, :], h[rows_of(t, rows), cq:cq + CW]).then_inc(q_in[u], 16)

            def load_g(t, u, n, rows=P):
                sp.wait_ge(yd, t + 1)
                sp.dma_start(gx[u][0:rows, :], h[rows_of(t, rows), cg:cg + CW]).then_inc(g_in[u], 16)

            def store(t, u, n, rows=P):
                sp.wait_ge(yd, t + 3)
                sp.dma_start(y[rows_of(t, rows), cy:cy + CW], yb[u][0:rows, :]).then_inc(stored[u], 16)
            for t in range(2):
                load_q(t, t, 1, first=True)
                load_g(t, t, 1)
            with sp.Fori(0, TILES // 2 - 1) as i:
                load_q(i * 2 + 2, 0, i + 2)
                store(i * 2, 0, i + 1)
                load_g(i * 2 + 2, 0, i + 2)
                load_q(i * 2 + 3, 1, i + 2)
                store(i * 2 + 1, 1, i + 1)
                load_g(i * 2 + 3, 1, i + 2)
            load_q(L, 0, 5, SMP)
            store(L - 2, 0, 4)
            load_g(L, 0, 5, SMP)
            store(L - 1, 1, 4)
            store(L, 0, 5, SMP)
            sp.wait_ge(stored[0], 16 * 6)
            sp.wait_ge(stored[1], 16 * 5)

        @block.gpsimd
        def _(pool):
            pool.dma_start(qn[:, :], a["mem_qn"][layer].unsqueeze(1)).then_inc(n_in, 16)
            link = Link(pool, pc)
            nc.gpsimd.memset(eps[:, :], EPS * HD)

            def rstds(t, u, n, rows=P):
                link.at(t)
                pool.wait_ge(q_in[u], n * 16)
                pool.wait_ge(red, t + 1)
                nc.gpsimd.tensor_tensor(sq[0:rows, :], xq[u][0:rows, :], xq[u][0:rows, :], ALU.mult)\
                    .then_inc(squ, 1)
                pool.wait_ge(red, t + 2)
                v = ssq[u][0:rows, :]
                link(nc.gpsimd.tensor_tensor(v, v, eps[0:rows, :], ALU.add))
                nc.gpsimd.tensor_tensor(v, v, c.half[0:rows, 0:NH], ALU.pow).then_inc(rs, 1)

            def cached(b):
                for to, cache, sem in ((ck, "cache_mem_k", k_in), (cv, "cache_mem_v", v_in)):
                    src = a[cache][layer, bass.ds(b, 1)].rearrange("o (m p) h d -> p (o m) (h d)", p=P)
                    pool.dma_start(to[:, bass.ds(b, 1)].rearrange("p o m n -> p (o m) n"), src).then_inc(sem, 16)
            with pool.Fori(0, TILES // 2) as i:
                for u in range(2):
                    rstds(i * 2 + u, u, i + 1)
                    cached(i * 2 + u)
            for j in range(2):
                load_out(pool, c, j)
            rstds(L, 0, 5, SMP)

        @block.tensor
        def _(pe):
            def queries(t, u, n):
                pe.wait_ge(q_in[u], n * 16)
                pe.wait_ge(qe, t + 1)
                for g in range(NH):
                    ins = nc.tensor.transpose(psT[:, P * g:P * g + P], xq[u][:, P * g:P * g + P], c.ident[:, :])
                ins.then_inc(qt, 1)

            def scores(t, u, n):
                pe.wait_ge(qe, t + 2)
                for g in range(NH):
                    ins = nc.tensor.matmul(psS[u][:, MEM * g:MEM * g + MEM], qT[u][:, g, :],
                                           c.keysT[:, layer, g, :], start=True, stop=True)
                ins.then_inc(sc, 1)

            def probabilities(t, u, n):
                pe.wait_ge(ex, t + 1)
                pe.wait_ge(pa, t + 1)
                pe.wait_ge(pd, t + 1)
                for j in range(NH * MC):
                    ins = nc.tensor.transpose(psP[:, P * j:P * j + P], pr[u][:, P * j:P * j + P], c.ident[:, :])
                ins.then_inc(pt, 1)

            def mix(t, u, n):
                pe.wait_ge(pa, t + 2)
                pe.wait_ge(pd, t + 2)
                pe.wait_ge(yd, t + 2)
                for g in range(NH):
                    for m in range(MC):
                        ins = nc.tensor.matmul(psO[:, P * g:P * g + P], prT[u][:, MC * g + m, :],
                                               c.vals[:, layer, m, P * g:P * g + P],
                                               start=(m == 0), stop=(m == MC - 1))
                ins.then_inc(od, 1)
            queries(0, 0, 1)
            scores(0, 0, 1)
            queries(1, 1, 1)
            with pe.Fori(0, TILES // 2 - 1) as i:
                for u in range(2):
                    scores(i * 2 + u + 1, 1 - u, i + 1 + u)
                    probabilities(i * 2 + u, u, i + 1)
                    queries(i * 2 + u + 2, u, i + 2)
                    mix(i * 2 + u, u, i + 1)
            scores(L - 1, 1, 4)
            for t in (L - 2, L - 1):
                probabilities(t, t % 2, 4)
                mix(t, t % 2, 4)

            pe.wait_ge(q_in[0], 5 * 16)
            pe.wait_ge(qe, L + 1)
            for g in range(NH):
                ins = nc.tensor.transpose(psT[:, SMP * g:SMP * g + SMP], xq[0][0:SMP, P * g:P * g + P],
                                          c.ident[0:SMP, 0:SMP])
            ins.then_inc(qt, 1)
            pe.wait_ge(k_in, NB * 16)
            for b in range(NB):
                for m in range(MC):
                    bank = psP[:, 512 * m:512 * m + 512]
                    pe.wait_ge(kcd if m else kca, b + 1)
                    if b == 0:
                        pe.wait_ge(pd if m else pa, L + 1)
                    for g in range(NH):
                        ins = nc.tensor.transpose(bank[:, P * g:P * g + P], ck[:, b, m, P * g:P * g + P], c.ident[:, :])
                    ins.then_inc(ktr, 1)
            pe.wait_ge(masked, 1)
            pe.wait_ge(kca, NB + 1)
            pe.wait_ge(kcd, NB + 1)
            for g in range(NH):
                for b in range(NB):
                    ins = nc.tensor.matmul(psS[0][0:SMP, MEM * g:MEM * g + MEM], qTm[:, g, b, :], ckT[:, b, g, :],
                                           start=(b == 0), stop=(b == NB - 1))
            ins.then_inc(sc, 1)
            pe.wait_ge(pn, 1)
            for j in range(NH * MC):
                ins = nc.tensor.transpose(psP[:, SMP * j:SMP * j + SMP], pr[0][0:SMP, P * j:P * j + P],
                                          c.ident[0:SMP, 0:SMP])
            ins.then_inc(pt, 1)
            pe.wait_ge(pa, L + 2)
            pe.wait_ge(v_in, NB * 16)
            pe.wait_ge(yd, L + 2)
            for b in range(NB):
                for g in range(NH):
                    for m in range(MC):
                        at = SMP * g + NT * b
                        ins = nc.tensor.matmul(psO[:, at:at + NT], cv[:, b, m, P * g:P * g + P],
                                               prT[0][:, MC * g + m, NT * b:NT * b + NT],
                                               start=(m == 0), stop=(m == MC - 1))
            ins.then_inc(od, 1)
            pe.wait_ge(oc, 1)
            for g in range(NH):
                ins = nc.tensor.transpose(psT[0:SMP, P * g:P * g + P], oT[:, g, :], c.ident[:, :])
            ins.then_inc(ot, 1)

        @block.scalar
        def _(act):
            act.sem_inc(qe, 1)
            act.sem_inc(pa, 1)
            act.sem_inc(kca, 1)

            def exps(t, u, rows):
                act.wait_ge(nm, t + 1)
                for g in range(NH):
                    ins = nc.scalar.activation(pr[u][0:rows, MEM * g:MEM * g + MEM], psS[u][0:rows, MEM * g:MEM * g + MEM],
                                               ACT.Exp, bias=mx[u][0:rows, g:g + 1], scale=ssq[u][0:rows, g:g + 1],
                                               accum_out=tot[u][0:rows, g:g + 1])
                ins.then_inc(ex, 1)

            def front(t, u, n):
                act.wait_ge(qt, t + 1)
                nc.scalar.activation(qT[u][:, :, :], heads(psT[:, :]), ACT.Copy).then_inc(qe, 1)

            def back(t, u, n):
                act.wait_ge(pt, t + 1)
                nc.scalar.activation(prT[u][:, 0:4, :], heads(psP[:, 0:512]), ACT.Copy).then_inc(pa, 1)
            front(0, 0, 1)
            exps(0, 0, P)
            front(1, 1, 1)
            with act.Fori(0, TILES // 2 - 1) as i:
                for u in range(2):
                    back(i * 2 + u, u, i + 1)
                    front(i * 2 + u + 2, u, i + 2)
                    exps(i * 2 + u + 1, 1 - u, P)
            back(L - 2, 0, 4)
            exps(L - 1, 1, P)
            back(L - 1, 1, 4)
            act.wait_ge(qt, L + 1)
            nc.scalar.activation(qT[0][:, :, 0:SMP], heads(psT[:, 0:NH * SMP]), ACT.Copy).then_inc(qe, 1)
            act.wait_ge(n_in, 16)
            for b in range(NB):
                act.wait_ge(ktr, 2 * b + 1)
                nc.scalar.activation(ckT[:, b, :, 0:P], heads(psP[:, 0:512]), ACT.Copy, scale=qn[:, 0:1]).then_inc(kca, 1)
            exps(L, 0, SMP)
            act.wait_ge(pt, L + 1)
            nc.scalar.activation(prT[0][:, :, 0:SMP], psP[:, 0:256].rearrange("p (j t) -> p j t", j=8), ACT.Copy)\
                .then_inc(pa, 1)
            act.wait_ge(od, L + 1)
            nc.scalar.activation(oT[:, :, :], heads(psO[:, 0:NH * SMP]), ACT.Copy).then_inc(oc, 1)

        @block.vector
        def _(dve):
            link = Link(dve, dc)
            dve.sem_inc(red, 1)
            dve.sem_inc(pd, 1)
            dve.sem_inc(yd, 2)
            dve.sem_inc(kcd, 1)

            def front(t, u, n, rows=P):
                link.at(t)
                dve.wait_ge(squ, t + 1)
                nc.vector.tensor_reduce(ssq[u][0:rows, :], heads(sq[0:rows, :]), AX.X, ALU.add).then_inc(red, 1)
                dve.wait_ge(sc, t + 1)
                link(nc.vector.tensor_reduce(mx[u][0:rows, :], psS[u][0:rows, :].rearrange("p (h m) -> p h m", h=NH),
                                             AX.X, ALU.max))
                dve.wait_ge(rs, t + 1)
                nc.vector.scalar_tensor_tensor(mx[u][0:rows, :], mx[u][0:rows, :], -1.0, ssq[u][0:rows, :],
                                               ALU.mult, ALU.mult).then_inc(nm, 1)

            def back(t, u, n):
                dve.wait_ge(pt, t + 1)
                nc.vector.tensor_copy(prT[u][:, 4:8, :], heads(psP[:, 512:1024])).then_inc(pd, 1)
                dve.wait_ge(ex, t + 1)
                nc.vector.reciprocal(tot[u][:, :], tot[u][:, :]).then_inc(rcp, 1)
                dve.wait_ge(rcp, t + 1)
                dve.wait_ge(od, t + 1)
                dve.wait_ge(g_in[u], n * 16)
                dve.wait_ge(stored[u], n * 16)
                for g in range(NH):
                    v = slice(P * g, P * g + P)
                    ins = nc.vector.scalar_tensor_tensor(yb[u][:, v], psO[:, v], tot[u][:, g:g + 1], gx[u][:, v],
                                                         ALU.mult, ALU.mult)
                ins.then_inc(yd, 1)
            two_ahead(dve, front, back)
            dve.wait_ge(qe, L + 2)
            for g in range(NH):
                ins = nc.vector.tensor_tensor(qTm[:, g, :, :], bc(qT[0][:, g, 0:SMP], 1, NB), c.seq_cols[:, :, :], ALU.mult)
            ins.then_inc(masked, 1)
            dve.wait_ge(n_in, 16)
            for b in range(NB):
                dve.wait_ge(ktr, 2 * b + 2)
                nc.vector.tensor_scalar(ckT[:, b, :, P:2 * P], heads(psP[:, 512:1024]), qn[:, 0:1], None, ALU.mult)\
                    .then_inc(kcd, 1)
            front(L, 0, 5, SMP)
            dve.wait_ge(ex, L + 1)
            nc.vector.reciprocal(tot[0][0:SMP, :], tot[0][0:SMP, :]).then_inc(rcp, 1)
            dve.wait_ge(rcp, L + 1)
            p4 = pr[0][0:SMP, :].rearrange("p (h m) -> p h m", h=NH)
            nc.vector.tensor_tensor(p4, p4, bc(tot[0][0:SMP, :], 2, MEM), ALU.mult).then_inc(pn, 1)
            dve.wait_ge(ot, 1)
            dve.wait_ge(g_in[0], 5 * 16)
            dve.wait_ge(stored[0], 5 * 16)
            nc.vector.tensor_tensor(yb[0][0:SMP, :], psT[0:SMP, :], gx[0][0:SMP, :], ALU.mult).then_inc(yd, 1)


def mlstm(nc, c, a, o):
    T = TILES
    with Stage(nc, "mlstm") as s:
        li, lf, f, m, b, av, M, negM = (s.sb(n, [NH, TOK]) for n in ("li", "lf", "f", "m", "b", "a", "M", "negM"))
        keep = s.sb("keep", [NH, SEQ])
        bias = s.sb("bias", [P, 1])
        before, last, fade = (s.sb(n, [NH, 16]) for n in ("m_before", "M_last", "fade"))
        R = s.sb("rows", [P, TOK])
        cols = s.sb("cols", [P, T + 1, P])
        fades = s.sb("fades", [P, NH, 16])
        q, k, og, ga = ([s.sb(f"{n}{u}", [P, CW]) for u in range(2)] for n in ("q", "k", "og", "ga"))
        v = [s.sb(f"v{u}", [P, NH, HD + 1]) for u in range(2)]
        hg = s.sb("hg", [P, CW])
        qT, kT, Z, Pt = ([s.sb(f"{n}{u}", [P, CW]) for u in range(2)] for n in ("qT", "kT", "z", "pt"))
        vw = s.sb("vw", [P, NH, HD + 1])
        inter = s.sb("inter", [P, NH, HD + 1])
        num = s.sb("num", [P, NH, HD + 1])
        hh, sq = s.sb("h", [P, CW]), s.sb("sq", [P, CW])
        den, ssq = s.sb("den", [P, NH]), s.sb("ssq", [P, NH])
        yb = [s.sb(f"y{u}", [P, CW]) for u in range(2)]
        C = s.sb("C", [P, NH, HD + 1])
        C0 = s.sb("C0", [P, NB * NH, HD + 1])
        n0 = s.sb("n0", [NB * NH, HD])
        vwm = s.sb("vwm", [SMP, NB, HD + 1])
        vwm2 = s.sb("vwm2", [SMP, NB, HD + 1])
        psq, psk, psS, psZ = (s.ps(n) for n in ("psq", "psk", "pss", "psz"))
        psN, psI = s.ps("psn", 1024), s.ps("psi", 1024)

        def pair(ps):
            return ps[:, :].rearrange("p (b x) -> p b x", b=2)[:, :, 0:2 * (HD + 1)]\
                .rearrange("p b (h d) -> p b h d", h=2)

        def by2(t):
            return t.rearrange("p (b h) d -> p b h d", b=2)

        def of(ps, h):
            at = 512 * (h // 2) + (HD + 1) * (h % 2)
            return slice(at, at + HD + 1)

        par_in, m0_in, C0_in, hg_in, n0_in = (
            s.sem("bias_in"), s.sem("m0_in"), s.pool_sem("C0_in"), s.sem("hg_in"), s.pool_sem("n0_in"))
        made, zex, qnm = s.sem("rows_made"), s.sem("z_exponentials"), s.sem("smp_qn_masked")
        x_in, gt_in, stored, outs = s.sem("qkv_in", 2), s.sem("gates_in", 2), s.sem("stored", 2), s.sem("outs")
        (vones, rchain, e1, e2, e3, rows, trr, trc, frd, tr, qe, ke, sc, zz, ze, ptd, mm, ie, vwd, up, cd, nd, hd_,
         sqd, gt, ssd, rs, yd, dch, pch) = (s.sem(n) for n in (
            "v_ones", "row_chain", "log_f_exps", "rows_ready", "rows_exp", "rows_done", "rows_transposed",
            "cols_copied", "fades_copied", "qk_transposed", "qT_copied", "kT_copied", "scores", "z", "z_exp",
            "weighted", "num_inter", "inter_copied", "vw", "update", "C_updated", "num", "h", "squares", "gate",
            "sums", "rstd", "y", "dve_chain", "pool_chain"))
        n0t, n0c, lqt, mk, up2, c2, it2, itc, it3, fin, fint = (s.sem(n) for n in (
            "n0_transposed", "n0_copied", "smp_qn", "smp_masked", "smp_update", "smp_C", "smp_inter",
            "smp_inter_copied", "smp_inter_back", "n_final", "n_final_copied"))
        block = s.block()
        ALL = slice(0, SEQ)

        def smp(ap):
            return ap[:, SEQ:TOK].rearrange("p (b t) -> p b t", t=NT)

        def chunks(ap):
            return ap[:, 0:SEQ].rearrange("p (c t) -> p c t", t=P)

        @block.sync
        def _(sp):
            for r in stored:
                sp.sem_inc(r, 16)
            sp.dma_start(bias[0:NH, :], a["b_if_even"][0, 0:NH].unsqueeze(1)).then_inc(par_in, 16)
            sp.dma_start(bias[32:32 + NH, :], a["b_if_even"][0, NH:2 * NH].unsqueeze(1)).then_inc(par_in, 16)
            sp.dma_start(before[:, NB:2 * NB], a["state_mlstm_m"][0].rearrange("b h -> h b")).then_inc(m0_in, 16)
            sp.dma_start(hg[:, :], a["mlstm_hnorm"].broadcast_to([P, CW])).then_inc(hg_in, 16)

            def load(t, u, rows=P, first=False):
                if not first:
                    sp.wait_ge(up, t - 1)
                r = rows_of(t, rows)
                sp.dma_start(q[u][0:rows, :], c.h_even[r, E_Q:E_Q + CW]).then_inc(x_in[u], 16)
                sp.dma_start(k[u][0:rows, :], c.h_even[r, E_K:E_K + CW]).then_inc(x_in[u], 16)
                sp.dma_start(v[u][0:rows, :, 0:HD], heads(c.h_even[r, E_V:E_V + CW])).then_inc(x_in[u], 16)

            def load_gates(t, u, rows=P):
                sp.wait_ge(yd, t + 1)
                r = rows_of(t, rows)
                sp.dma_start(og[u][0:rows, :], c.h_even[r, E_O:E_O + CW]).then_inc(gt_in[u], 16)
                sp.dma_start(ga[u][0:rows, :], c.h_even[r, E_GA:E_GA + CW]).then_inc(gt_in[u], 16)

            def store(t, u, rows=P):
                sp.wait_ge(yd, t + 3)
                sp.dma_start(c.y_even[rows_of(t, rows), 0:CW], yb[u][0:rows, :]).then_inc(stored[u], 16)
            sp.wait_ge(vones, 2)
            for t in range(2):
                load(t, t, first=True)
                load_gates(t, t)
            with sp.Fori(0, T // 2 - 1) as i:
                for u in range(2):
                    load(i * 2 + u + 2, u)
                    store(i * 2 + u, u)
                    load_gates(i * 2 + u + 2, u)
            load(T, 0, SMP)
            store(T - 2, 0)
            load_gates(T, 0, SMP)
            store(T - 1, 1)
            store(T, 0, SMP)
            sp.wait_ge(rows, 1)
            sp.dma_start(o[4][0, 0].unsqueeze(1), m[:, SEQ - 1:SEQ]).then_inc(outs, 16)
            sp.dma_start(o[7][0].rearrange("b h -> h b"), smp(m)[:, :, NT - 1]).then_inc(outs, 16)
            sp.wait_ge(cd, T + 1)
            sp.dma_start(o[2][0, 0].rearrange("h k v -> k h v"), C[:, :, 0:HD]).then_inc(outs, 16)
            sp.dma_start(o[3][0, 0].rearrange("h k -> k h"), C[:, :, HD]).then_inc(outs, 16)
            sp.wait_ge(c2, NH)
            sp.dma_start(o[5][0].rearrange("b h k v -> k (b h) v"), C0[:, :, 0:HD]).then_inc(outs, 16)
            sp.wait_ge(fint, 1)
            sp.dma_start(o[6][0].rearrange("b h k -> (b h) k"), n0[:, :]).then_inc(outs, 16)
            sp.wait_ge(outs, 6 * 16)
            sp.wait_ge(stored[0], 6 * 16)
            sp.wait_ge(stored[1], 5 * 16)

        @block.gpsimd
        def _(pool):
            pool.dma_start(C0[:, :, 0:HD], a["state_mlstm_C"][0].rearrange("b h k v -> k (b h) v")).then_inc(C0_in, 16)
            pool.dma_start(n0[:, :], a["state_mlstm_n"][0].rearrange("b h k -> (b h) k")).then_inc(n0_in, 16)
            for u in range(2):
                nc.gpsimd.memset(v[u][:, :, HD:HD + 1], 1.0).then_inc(vones, 1)
            link = Link(pool, pch)
            link(nc.gpsimd.memset(C[:, :, :], 0.0))
            pool.wait_ge(hg_in, 16)

            def gates(t, u, n, rows=P):
                link.at(1 + t)
                pool.wait_ge(gt_in[u], n * 32)
                g = ga[u][0:rows, :]
                link(nc.gpsimd.tensor_tensor(g, g, og[u][0:rows, :], ALU.mult))
                nc.gpsimd.tensor_tensor(g, g, hg[0:rows, :], ALU.mult).then_inc(gt, 1)
                pool.wait_ge(hd_, t + 1)
                nc.gpsimd.tensor_tensor(sq[0:rows, :], hh[0:rows, :], hh[0:rows, :], ALU.mult).then_inc(sqd, 1)
                pool.wait_ge(ssd, t + 1)
                nc.gpsimd.tensor_tensor(ssq[0:rows, :], ssq[0:rows, :], c.half[0:rows, 0:NH], ALU.pow).then_inc(rs, 1)
            with pool.Fori(0, T // 2) as i:
                for u in range(2):
                    gates(i * 2 + u, u, i + 1)
            gates(T, 0, 5, SMP)

        @block.tensor
        def _(pe):
            pe.sem_inc(mm, 1)
            pe.wait_ge(rows, 1)
            for t in range(T + 1):
                w = P if t < T else SMP
                bank = (psq, psk, psS)[t // 4]
                ins = nc.tensor.transpose(bank[0:w, P * (t % 4):P * (t % 4) + P], R[:, P * t:P * t + w], c.ident[:, :])
            for h in range(NH):
                ins = nc.tensor.matmul(psZ[:, 16 * h:16 * h + 16], c.head_row[:, h, :], fade[:, :], start=True, stop=True)
            ins.then_inc(trr, 1)
            pe.wait_ge(n0_in, 16)
            nc.tensor.transpose(psN[:, 0:32], n0[:, :], c.ident[0:32, 0:32]).then_inc(n0t, 1)

            def turned(t, u, n, rows=P):
                pe.wait_ge(x_in[u], n * 48)
                pe.wait_ge(qe, t + 1)
                pe.wait_ge(ke, t + 1)
                for src, ps in ((q, psq), (k, psk)):
                    for h in range(NH):
                        ins = nc.tensor.transpose(ps[:, P * h:P * h + rows], src[u][0:rows, P * h:P * h + P],
                                                  c.ident[0:rows, 0:rows])
                ins.then_inc(tr, 1)

            def scores(t, u, n, rows=P):
                pe.wait_ge(ze, t + 1)
                for h in range(NH):
                    cut = slice(SEQ, TOK) if rows == SMP else bass.ts(t, P)
                    nc.tensor.matmul(psZ[0:rows, P * h:P * h + rows], c.head_row[:, h, 0:rows], negM[:, cut],
                                     start=True, stop=True)
                pe.wait_ge(qe, t + 2)
                pe.wait_ge(ke, t + 2)
                pe.wait_ge(ptd, t + 1)
                for h in range(NH):
                    ins = nc.tensor.matmul(psS[0:rows, P * h:P * h + rows], kT[u][:, P * h:P * h + rows],
                                           qT[u][:, P * h:P * h + rows], start=True, stop=True)
                ins.then_inc(sc, 1)

            def mix(t, u, n):
                pe.wait_ge(ptd, t + 2)
                pe.wait_ge(nd, t + 1)
                for h in range(NH):
                    nc.tensor.matmul(psN[:, of(psN, h)], Pt[u][:, P * h:P * h + P], v[u][:, h, :],
                                     start=True, stop=True)
                pe.wait_ge(cd, t + 1)
                for h in range(NH):
                    ins = nc.tensor.matmul(psI[:, of(psI, h)], qT[u][:, P * h:P * h + P], C[:, h, :],
                                           start=True, stop=True)
                ins.then_inc(mm, 1)

            def update(t, u, n):
                pe.wait_ge(ie, t + 1)
                pe.wait_ge(vwd, t + 1)
                for h in range(NH):
                    ins = nc.tensor.matmul(psI[:, of(psI, h)], k[u][:, P * h:P * h + P], vw[:, h, :],
                                           start=True, stop=True)
                ins.then_inc(up, 1)
            pe.wait_ge(trc, 1)
            pipelined(pe, (turned, 1), (mix, 0), (scores, 1), (update, 0))

            turned(T, 0, 5, SMP)
            scores(T, 0, 5, SMP)
            pe.wait_ge(ptd, T + 2)
            pe.wait_ge(nd, T + 1)
            pe.wait_ge(cd, T + 1)
            for h in range(NH):
                nc.tensor.matmul(psN[0:SMP, of(psN, h)], Pt[0][0:SMP, P * h:P * h + SMP], v[0][0:SMP, h, :],
                                 start=True, stop=True)
            pe.wait_ge(C0_in, 16)
            pe.wait_ge(n0c, 1)
            for h in range(NH):
                for b_ in range(NB):
                    at = SMP * h + NT * b_
                    nc.tensor.matmul(psI[:, at:at + NT], C0[:, NH * b_ + h, 0:HD],
                                     qT[0][:, P * h + NT * b_:P * h + NT * b_ + NT], start=True, stop=True)
            n_of = C0[:, :, HD].rearrange("p (b h) -> p b h", h=NH)
            for h in range(NH):
                ins = nc.tensor.matmul(psI[0:SMP, 512 + NB * h:512 + NB * h + NB], qT[0][:, P * h:P * h + SMP],
                                       n_of[:, :, h], start=True, stop=True)
            ins.then_inc(it2, 1)
            pe.wait_ge(itc, 1)
            for h in range(NH):
                ins = nc.tensor.transpose(psq[0:SMP, P * h:P * h + P], hh[:, SMP * h:SMP * h + SMP], c.ident[:, :])
            ins.then_inc(it3, 1)
            for h in range(NH):
                pe.wait_ge(mk, h + 1)
                if h >= 1:
                    pe.wait_ge(c2, h)
                for j, n in enumerate((3, 3, 2)):
                    bank = (psk, psS, psZ)[j]
                    ins = nc.tensor.matmul(bank[:, 0:n * (HD + 1)], k[0][0:SMP, P * h:P * h + P],
                                           (vwm, vwm2)[h % 2][:, 3 * j:3 * j + n, :].rearrange("p b d -> p (b d)"),
                                           start=True, stop=True)
                ins.then_inc(up2, 1)
            pe.wait_ge(c2, NH)
            nc.tensor.transpose(psI[0:NB * NH, 0:HD], C0[:, :, HD], c.ident[:, :]).then_inc(fin, 1)

        @block.scalar
        def _(act):
            act.sem_inc(qe, 1)
            act.wait_ge(e1, 1)
            nc.scalar.activation(f[:, :], f[:, :], ACT.Exp, scale=-1.0).then_inc(e2, 1)
            act.wait_ge(e2, 1)
            nc.scalar.activation(f[:, :], f[:, :], ACT.Ln, bias=1.0).then_inc(e2, 1)
            act.wait_ge(made, 1)
            nc.scalar.activation(R[32:32 + NH, :], R[32:32 + NH, :], ACT.Exp).then_inc(e3, 1)
            nc.scalar.activation(R[64:64 + NH, :], m[:, :], ACT.Exp, scale=-1.0).then_inc(e3, 1)
            nc.scalar.activation(R[96:96 + NH, :], R[96:96 + NH, :], ACT.Exp).then_inc(e3, 1)
            nc.scalar.activation(fade[:, :], fade[:, :], ACT.Exp).then_inc(e3, 1)
            act.wait_ge(trr, 1)
            nc.scalar.activation(fades[:, :, :], heads(psZ[:, 0:64]), ACT.Copy).then_inc(frd, 1)
            act.wait_ge(frd, 1)

            def front(t, u, n, rows=P):
                act.wait_ge(tr, t + 1)
                nc.scalar.activation(heads(qT[u][:, :])[:, :, 0:rows], heads(psq[:, :])[:, :, 0:rows], ACT.Copy)\
                    .then_inc(qe, 1)

            def exps(t, u, n, rows=P):
                act.wait_ge(zz, t + 1)
                z = heads(Z[u][0:rows, :])[:, :, 0:rows]
                nc.scalar.activation(z, z, ACT.Exp).then_inc(zex, 1)

            def back(t, u, n):
                act.wait_ge(mm, t + 2)
                act.wait_ge(nd, t + 1)
                for h in range(NH):
                    ins = nc.scalar.activation(inter[:, h, :], psI[:, of(psI, h)], ACT.Copy,
                                               scale=cols[:, bass.ds(t, 1), 32 + h:33 + h].rearrange("p a b -> p (a b)"))
                ins.then_inc(ie, 1)
            pipelined(act, (front, 1), (back, 0), (exps, 1))
            front(T, 0, 5, SMP)
            exps(T, 0, 5, SMP)
            act.wait_ge(it2, 1)
            nc.scalar.activation(hh[:, 0:NH * SMP], psI[:, 0:NH * SMP], ACT.Copy).then_inc(itc, 1)
            act.wait_ge(it3, 1)
            act.wait_ge(qnm, 1)
            for h in range(NH):
                ins = nc.scalar.activation(inter[0:SMP, h, 0:HD], psq[0:SMP, P * h:P * h + P], ACT.Copy,
                                           scale=cols[0:SMP, T, 32 + h:33 + h])
            ins.then_inc(ie, 1)

        @block.vector
        def _(dve):
            V = nc.vector
            link = Link(dve, rchain)
            for x in (ke, ze, ptd, nd, cd):
                dve.sem_inc(x, 1)
            dve.sem_inc(yd, 2)
            dve.wait_ge(par_in, 32)
            V.tensor_scalar(li[:, :], c.gates[0:NH, :], bias[0:NH, 0:1], None, ALU.add)
            link(V.tensor_scalar(lf[:, :], c.gates[32:32 + NH, :], bias[32:32 + NH, 0:1], None, ALU.add))
            V.scalar_tensor_tensor(f[:, :], lf[:, :], -1.0, lf[:, :], ALU.mult, ALU.max).then_inc(e1, 1)
            link(V.memset(R[:, :], 0.0))
            link(V.memset(keep[:, :], 1.0))
            link(V.memset(chunks(keep)[:, :, 0:1], 0.0))
            link(V.tensor_scalar(lf[:, :], lf[:, :], 0.0, None, ALU.min))
            dve.wait_ge(e2, 2)
            link(V.tensor_tensor(lf[:, :], lf[:, :], f[:, :], ALU.subtract))
            link(V.tensor_tensor_scan(m[:, ALL], lf[:, ALL], li[:, ALL], 0.0, ALU.add, ALU.max))
            link(V.tensor_tensor_scan(b[:, ALL], keep[:, :], lf[:, ALL], 0.0, ALU.mult, ALU.add))
            dve.wait_ge(m0_in, 16)
            for t in range(NT):
                mp = smp(m)[:, :, t - 1] if t else before[:, NB:2 * NB]
                link(V.tensor_tensor(smp(m)[:, :, t], mp, smp(lf)[:, :, t], ALU.add))
                link(V.tensor_tensor(smp(m)[:, :, t], smp(m)[:, :, t], smp(li)[:, :, t], ALU.max))
                if t:
                    link(V.tensor_tensor(smp(b)[:, :, t], smp(b)[:, :, t - 1], smp(lf)[:, :, t], ALU.add))
                else:
                    link(V.tensor_copy(smp(b)[:, :, 0], smp(lf)[:, :, 0]))
            link(V.tensor_tensor(M[:, :], m[:, :], b[:, :], ALU.subtract))
            link(V.tensor_tensor(av[:, :], li[:, :], b[:, :], ALU.subtract))
            link(V.tensor_scalar(negM[:, :], M[:, :], -1.0, None, ALU.mult))
            link(V.memset(before[:, 0:1], 0.0))
            link(V.tensor_copy(before[:, 1:TILES], chunks(m)[:, 0:TILES - 1, P - 1]))
            link(V.tensor_copy(last[:, 0:TILES], chunks(M)[:, :, P - 1]))
            link(V.tensor_copy(last[:, NB:2 * NB], smp(M)[:, :, NT - 1]))
            for lo, view, n in ((0, chunks, P), (NB, smp, NT)):
                e = slice(lo, lo + 8)
                link(V.tensor_tensor(view(R[32:32 + NH, :]), bc(before[:, e], 2, n), view(M), ALU.subtract))
                link(V.tensor_tensor(view(R[96:96 + NH, :]), view(av), bc(last[:, e], 2, n), ALU.subtract))
            link(V.tensor_copy(R[0:NH, :], av[:, :]))
            V.tensor_tensor(fade[:, :], before[:, :], last[:, :], ALU.subtract).then_inc(made, 1)
            dve.wait_ge(e3, 4)
            V.tensor_scalar(R[96:96 + NH, :], R[96:96 + NH, :], HD ** -0.5, None, ALU.mult).then_inc(rows, 1)
            dve.wait_ge(trr, 1)
            for j, ps in enumerate((psq, psk)):
                link(V.tensor_copy(cols[:, 4 * j:4 * j + 4, :], heads(ps[:, :])))
            link(V.tensor_copy(cols[0:SMP, 8, :], psS[0:SMP, 0:P]))
            dve.wait_ge(n0t, 1)
            dve.wait_ge(C0_in, 16)
            V.tensor_copy(C0[:, :, HD], psN[:, 0:32]).then_inc(n0c, 1)
            dve.wait_ge(frd, 1)
            dve.wait_ge(n0c, 1)
            dve.wait_ge(pch, 1)
            dve.sem_inc(trc, 1)
            link = Link(dve, dch)

            def col(t, at, rows, h):
                if rows == SMP:
                    return cols[0:SMP, T, at + h:at + h + 1]
                return cols[:, bass.ds(t, 1), at + h:at + h + 1].rearrange("p a b -> p (a b)")

            def col4(t, at, rows):
                if rows == SMP:
                    return cols[0:SMP, T, at:at + NH]
                return cols[:, bass.ds(t, 1), at:at + NH].rearrange("p a b -> p (a b)")

            def front(t, u, n, rows=P):
                dve.wait_ge(tr, t + 1)
                V.tensor_scalar(heads(kT[u][:, :])[:, :, 0:rows], heads(psk[:, :])[:, :, 0:rows], HD ** -0.5, None,
                                ALU.mult).then_inc(ke, 1)

            def exponents(t, u, n, rows=P):
                dve.wait_ge(sc, t + 1)
                mask = c.neg_sj if rows == P else c.neg_smp
                for h in range(NH):
                    e = slice(P * h, P * h + rows)
                    ins = V.scalar_tensor_tensor(Z[u][0:rows, e], psZ[0:rows, e], col(t, 0, rows, h), mask[:, :],
                                                 ALU.add, ALU.add)
                ins.then_inc(zz, 1)
                dve.wait_ge(zz, t + 1)
                dve.sem_inc(ze, 1)

            def weights(t, u, n, rows=P):
                dve.wait_ge(zex, t + 1)
                e = lambda x: heads(x[0:rows, :])[:, :, 0:rows]
                V.tensor_tensor(e(Pt[u]), e(Z[u]), e(psS), ALU.mult).then_inc(ptd, 1)

            def h_of(t, u, n, rows=P):
                link.at(t * 5)
                d = num[0:rows, :, HD]
                link(V.scalar_tensor_tensor(den[0:rows, :], d, -1.0, d, ALU.mult, ALU.max))
                link(V.tensor_tensor(den[0:rows, :], den[0:rows, :], col4(t, 64, rows), ALU.max))
                link(V.reciprocal(den[0:rows, :], den[0:rows, :]))
                h4 = heads(hh[0:rows, :])
                V.tensor_tensor(h4, num[0:rows, :, 0:HD], bc(den[0:rows, :], 2, HD), ALU.mult).then_inc(hd_, 1)

            def mean_squares(t, u, n, rows=P):
                link.at(t * 5 + 3)
                dve.wait_ge(sqd, t + 1)
                link(V.tensor_reduce(ssq[0:rows, :], heads(sq[0:rows, :]), AX.X, ALU.add))
                V.tensor_scalar(ssq[0:rows, :], ssq[0:rows, :], 1.0 / HD, EPS, ALU.mult, ALU.add).then_inc(ssd, 1)

            def y_of(t, u, n, rows=P):
                link.at(t * 5 + 4)
                h4 = heads(hh[0:rows, :])
                dve.wait_ge(rs, t + 1)
                link(V.tensor_tensor(h4, h4, bc(ssq[0:rows, :], 2, HD), ALU.mult))
                dve.wait_ge(gt, t + 1)
                dve.wait_ge(stored[u], n * 16)
                V.tensor_tensor(yb[u][0:rows, :], hh[0:rows, :], ga[u][0:rows, :], ALU.mult).then_inc(yd, 1)
                dve.wait_ge(yd, t + 3)

            def values(t, u, n):
                V.tensor_tensor(vw[:, :, :], v[u][:, :, :], bc(col4(t, 96, P), 2, HD + 1), ALU.mult).then_inc(vwd, 1)

            def total(t, u, n):
                dve.wait_ge(ie, t + 1)
                V.tensor_tensor(by2(num[:, :, :]), by2(inter[:, :, :]), pair(psN), ALU.add).then_inc(nd, 1)
                dve.wait_ge(nd, t + 2)

            def state(t, u, n):
                dve.wait_ge(up, t + 1)
                for h in range(NH):
                    ins = V.scalar_tensor_tensor(C[:, h, :], C[:, h, :],
                                                 fades[:, h, bass.ds(t, 1)], psI[:, of(psI, h)],
                                                 ALU.mult, ALU.add)
                ins.then_inc(cd, 1)
            pipelined(dve, (front, 1), (values, 0), (total, 0), (h_of, 0), (exponents, 1), (state, 0),
                      (mean_squares, 0), (weights, 1), (y_of, 0))

            for step in (front, exponents, weights):
                step(T, 0, 5, SMP)
            dve.wait_ge(it2, 1)
            qn = psI[0:SMP, 512:512 + NH * NB].rearrange("p (h b) -> p h b", h=NH)
            s4 = sq[0:SMP, 0:NH * NB].rearrange("p (h b) -> p h b", h=NH)
            V.tensor_tensor(s4, qn, bc(c.of_seq[0:SMP, :], 1, NH), ALU.mult).then_inc(qnm, 1)
            dve.wait_ge(qnm, 1)
            V.tensor_reduce(ssq[0:SMP, :], s4, AX.X, ALU.add).then_inc(lqt, 1)
            dve.wait_ge(lqt, 1)
            V.tensor_tensor(inter[0:SMP, :, HD], ssq[0:SMP, :], col4(T, 32, SMP), ALU.mult).then_inc(lqt, 1)
            for h in range(NH):
                V.tensor_scalar(vw[0:SMP, h, :], v[0][0:SMP, h, :], col(T, 96, SMP, h), None, ALU.mult).then_inc(vwd, 1)
                dve.wait_ge(vwd, T + h + 1)
                V.tensor_tensor((vwm, vwm2)[h % 2][:, :, :], bc(vw[0:SMP, h, :], 1, NB),
                                bc(c.of_seq[0:SMP, :], 2, HD + 1), ALU.mult).then_inc(mk, 1)
                dve.wait_ge(up2, h + 1)
                for b_ in range(NB):
                    bank = (psk, psS, psZ)[b_ // 3]
                    at = (b_ % 3) * (HD + 1)
                    e = NH * b_ + h
                    ins = V.scalar_tensor_tensor(C0[:, e, :], C0[:, e, :], fades[:, h, NB + b_:NB + b_ + 1],
                                                 bank[:, at:at + HD + 1], ALU.mult, ALU.add)
                ins.then_inc(c2, 1)
            dve.wait_ge(ie, T + 1)
            dve.wait_ge(lqt, 2)
            V.tensor_tensor(by2(num[0:SMP, :, :]), by2(inter[0:SMP, :, :]), pair(psN)[0:SMP], ALU.add).then_inc(nd, 1)
            dve.wait_ge(nd, T + 2)
            for step in (h_of, mean_squares, y_of):
                step(T, 0, 5, SMP)
            dve.wait_ge(fin, 1)
            V.tensor_copy(n0[:, :], psI[0:NB * NH, 0:HD]).then_inc(fint, 1)


def gmlp(nc, c, a, o):
    T = TILES
    with Stage(nc, "gmlp") as s:
        w = s.sb("w", [P, NH, P])
        wT = s.sb("wT", [P, NH, P])
        ws = s.sb("ws", [SMP, NH, SMP])
        bs = s.sb("bs", [P, NH])
        bss = s.sb("bss", [SMP, NH])
        lg, lb = s.sb("ln_g", [P, CW]), s.sb("ln_b", [P, CW])
        x, u_, g = ([s.sb(f"{n}{u}", [P, CW]) for u in range(2)] for n in ("v", "u", "gate"))
        vn = [s.sb(f"vn{u}", [P, CW]) for u in range(2)]
        yb = [s.sb(f"y{u}", [P, CW]) for u in range(2)]
        st = [s.sb(f"stats{u}", [P, 6]) for u in range(2)]
        mv = [s.sb(f"mv{u}", [P, 2]) for u in range(2)]
        psW = s.ps("wT_ps")
        psM = [s.ps(f"mix{u}") for u in range(2)]
        w_in, ws_in, v_in, ug_in, stored, vout = (s.sem("w_in"), s.sem("ws_in"), s.sem("v_in", 2), s.sem("ug_in", 2),
                                                   s.sem("stored", 2), s.sem("v_stored"))
        cleared, wt, wr, va, rs, cen, sc, vd, mm, um, yd, dch, pch = (s.sem(n) for n in (
            "cleared", "w_transposed", "w_ready", "variance", "rstd", "centred", "scaled", "v_normed", "mixed",
            "u_mixed", "y", "dve_chain", "pool_chain"))
        block = s.block()

        @block.sync
        def _(sp):
            for r in stored:
                sp.sem_inc(r, 16)
            sp.dma_start(w[:, :, :], a["gmlp_w"][0].rearrange("g t s -> t g s")).then_inc(w_in, 16)
            sp.dma_start(bs[:, :], a["gmlp_b"][0].rearrange("g t -> t g")).then_inc(w_in, 16)
            sp.dma_start(lg[:, :], a["gmlp_ln_g"].broadcast_to([P, CW])).then_inc(w_in, 16)
            sp.dma_start(lb[:, :], a["gmlp_ln_b"].broadcast_to([P, CW])).then_inc(w_in, 16)

            def load(t, u, n, rows):
                sp.wait_ge(yd, t + 1)
                r = rows_of(t, rows)
                sp.dma_start(x[u][0:rows, :], c.h_even[r, E_VB:E_VB + CW]).then_inc(v_in[u], 16)
                sp.dma_start(u_[u][0:rows, :], c.h_even[r, E_U:E_U + CW]).then_inc(ug_in[u], 16)
                sp.dma_start(g[u][0:rows, :], c.h_even[r, E_GB:E_GB + CW]).then_inc(ug_in[u], 16)
            each_tile(sp, load)

        @block.scalar
        def _(act):
            act.wait_ge(cleared, 1)
            for b in range(NB):
                e = slice(NT * b, NT * b + NT)
                for q in range(NH):
                    act.dma_start(ws[e, q, e], a["gmlp_w"][0, q, 0:NT, 0:NT].rearrange("t s -> s t")).then_inc(ws_in, 16)
                act.dma_start(bss[e, :], a["gmlp_b"][0, :, 0:NT].rearrange("g t -> t g")).then_inc(ws_in, 16)
            def store(t, u, n, rows):
                act.wait_ge(yd, t + 3)
                act.dma_start(c.y_even[rows_of(t, rows), CW:2 * CW], yb[u][0:rows, :]).then_inc(stored[u], 16)
            each_tile(act, store)
            act.wait_ge(vd, T + 1)
            act.dma_start(o[8][0].rearrange("b t d -> (b t) d"), vn[0][0:SMP, :]).then_inc(vout, 16)
            act.wait_ge(vout, 16)
            act.wait_ge(stored[0], 6 * 16)
            act.wait_ge(stored[1], 5 * 16)

        @block.gpsimd
        def _(pool):
            pool.sem_inc(yd, 2)
            pool.wait_ge(w_in, 64)

            def norm(t, u, n, rows):
                link = Link(pool, pch)
                link.at(t * 2)
                pool.wait_ge(va, t + 1)
                v = mv[u][0:rows, 1:2]
                link(nc.gpsimd.tensor_tensor(v, v, c.eps[0:rows, 0:1], ALU.add))
                nc.gpsimd.tensor_tensor(v, v, c.half[0:rows, 0:1], ALU.pow).then_inc(rs, 1)
                pool.wait_ge(cen, t + 1)
                y = vn[u][0:rows, :]
                link(nc.gpsimd.tensor_tensor(y, y, lg[0:rows, :], ALU.mult))
                nc.gpsimd.tensor_tensor(y, y, lb[0:rows, :], ALU.add).then_inc(vd, 1)

            each_tile(pool, norm)

        @block.vector
        def _(dve):
            V = nc.vector
            V.memset(ws[:, :, :], 0.0).then_inc(cleared, 1)
            dve.wait_ge(w_in, 64)
            dve.wait_ge(wt, 1)
            V.tensor_tensor(wT[:, :, :], heads(psW[:, :]), bc(c.causal[:, :], 1, NH), ALU.mult).then_inc(wr, 1)

            def norm(t, u, n, rows):
                dve.wait_ge(v_in[u], n * 16)
                V.bn_stats(st[u][0:rows, :], x[u][0:rows, :]).then_inc(dch, 1)
                dve.wait_ge(dch, t + 1)
                V.bn_aggr(mv[u][0:rows, :], st[u][0:rows, :]).then_inc(va, 1)
                dve.wait_ge(rs, t + 1)
                V.tensor_scalar(vn[u][0:rows, :], x[u][0:rows, :], mv[u][0:rows, 0:1], mv[u][0:rows, 1:2],
                                ALU.subtract, ALU.mult).then_inc(cen, 1)

            def mix(t, u, n, rows):
                dve.wait_ge(mm, t + 1)
                dve.wait_ge(ug_in[u], n * 32)
                dve.wait_ge(stored[u], n * 16)
                for q in range(NH):
                    e = slice(P * q, P * q + P)
                    ins = V.scalar_tensor_tensor(yb[u][0:rows, e], psM[u][0:rows, e], (bs if rows == P else bss)[0:rows, q:q + 1],
                                                 u_[u][0:rows, e], ALU.add, ALU.mult)
                ins.then_inc(um, 1)
                dve.wait_ge(um, t + 1)
                V.tensor_tensor(yb[u][0:rows, :], yb[u][0:rows, :], g[u][0:rows, :], ALU.mult).then_inc(yd, 1)
            norm(0, 0, 1, P)
            for t in range(1, T):
                norm(t, t % 2, t // 2 + 1, P)
                mix(t - 1, (t - 1) % 2, (t - 1) // 2 + 1, P)
            mix(T - 1, (T - 1) % 2, T // 2, P)
            dve.wait_ge(ws_in, 40 * 16)
            V.tensor_tensor(ws[:, :, :], ws[:, :, :], bc(c.causal[0:SMP, 0:SMP], 1, NH), ALU.mult).then_inc(wr, 1)
            norm(T, 0, 5, SMP)
            mix(T, 0, 5, SMP)

        @block.tensor
        def _(pe):
            pe.wait_ge(w_in, 64)
            for q in range(NH):
                ins = nc.tensor.transpose(psW[:, P * q:P * q + P], w[:, q, :], c.ident[:, :])
            ins.then_inc(wt, 1)
            pe.wait_ge(wr, 1)

            def mix(t, u, n, rows):
                pe.wait_ge(vd, t + 1)
                for q in range(NH):
                    e = slice(P * q, P * q + P)
                    ins = nc.tensor.matmul(psM[u][0:rows, e], (wT if rows == P else ws)[0:rows, q, 0:rows],
                                           vn[u][0:rows, e], start=True, stop=True)
                ins.then_inc(mm, 1)
            with pe.Fori(0, T // 2) as i:
                for u in range(2):
                    mix(i * 2 + u, u, i + 1, P)
            pe.wait_ge(wr, 2)
            mix(T, 0, 5, SMP)


def out_memory(c, L, w_out):
    c.w_out, c.wo = w_out, [L.sb(f"w{u}", [P, OUT_ROWS, D]) for u in range(2)]
    c.wo_in = L.pool_sem("w_in", 2)


def load_out(pool, c, j):
    pool.dma_start(c.wo[j % 2][:, :, :], c.w_out[:, OUT_ROWS * j:OUT_ROWS * (j + 1), :]).then_inc(c.wo_in[j % 2], 16)


def out_project(nc, c, name, y, x_of, to_of):
    T, YC, H = TILES, OUT_CHUNKS, 2
    with Stage(nc, name) as s:
        wh, wl = (s.sb(n, [P, YC, D], F32R) for n in ("w_hi", "w_lo"))
        yb = [s.sb(f"y{u}", [P, YC * P]) for u in range(2)]
        yh = [s.sb(f"yT_hi{u}", [P, YC, P], F32R) for u in range(2)]
        yl = [s.sb(f"yT_lo{u}", [P, YC, P], F32R) for u in range(2)]
        x = [s.sb(f"x{u}", [P, D]) for u in range(2)]
        psT = s.ps("yT_ps", 512 * 3)
        psO = [s.ps(f"acc{u}", D) for u in range(2)]
        y_in, x_in, stored = s.sem("y_in", 2), s.sem("x_in", 2), s.sem("stored", 2)
        tr, hi, lo, mm, add = (s.sem(n) for n in ("transposed", "upper", "lower", "products", "sums"))
        pieces, chain = s.sem("weights_split"), s.sem("dve_chain")
        block = s.block()

        @block.gpsimd
        def _(pool):
            for j in range(2, OUT_PIECES):
                pool.wait_ge(pieces, j - 1)
                load_out(pool, c, j)

        @block.sync
        def _(sp):
            for r in stored:
                sp.sem_inc(r, 16)

            def load(t, u, n, rows):
                sp.wait_ge(tr, t + 1)
                sp.dma_start(yb[u][0:rows, :], y[rows_of(t, rows), :]).then_inc(y_in[u], 16)
                sp.wait_ge(stored[u], n * 16)
                sp.dma_start(x[u][0:rows, :], x_of(t, rows)).then_inc(x_in[u], 16)
            each_tile(sp, load)

        @block.tensor
        def _(pe):
            pe.sem_inc(tr, 2)

            def front(t, u, n, rows=P):
                pe.wait_ge(y_in[u], n * 16)
                pe.wait_ge(lo, 3 * t + 3)
                for k in range(YC):
                    ins = nc.tensor.transpose(psT[:, P * k:P * k + rows], yb[u][0:rows, P * k:P * k + P],
                                              c.ident[0:rows, 0:rows])
                ins.then_inc(tr, 1)

            def back(t, u, n, rows=P, pieces_first=False):
                pe.wait_ge(lo, 3 * t + 6)
                pe.wait_ge(add, t + 1)
                for k in range(YC):
                    if pieces_first and k % OUT_ROWS == 0:
                        pe.wait_ge(pieces, k // OUT_ROWS + 1)
                    for j in range(H):
                        n5 = slice(512 * j, 512 * j + 512)
                        for i, (yx, wx) in enumerate(((yh, wh), (yh, wl), (yl, wh))):
                            ins = nc.tensor.matmul(psO[u][0:rows, n5], yx[u][:, k, 0:rows], wx[:, k, n5],
                                                   start=(k == 0 and i == 0), stop=(k == YC - 1 and i == 2),
                                                   skip_group_check=True)
                ins.then_inc(mm, 1)
            front(0, 0, 1)
            front(1, 1, 1)
            back(0, 0, 1, pieces_first=True)
            with pe.Fori(0, T // 2 - 1) as i:
                front(i * 2 + 2, 0, i + 2)
                back(i * 2 + 1, 1, i + 1)
                front(i * 2 + 3, 1, i + 2)
                back(i * 2 + 2, 0, i + 2)
            front(T, 0, 5, SMP)
            back(T - 1, 1, 4)
            back(T, 0, 5, SMP)

        @block.scalar
        def _(act):
            def upper(t, u, n, rows=P):
                act.wait_ge(tr, t + 3)
                act.wait_ge(mm, t + 1)
                for j in range(3):
                    nc.scalar.activation(yh[u][:, 4 * j:4 * j + 4, 0:rows],
                                         heads(psT[:, 512 * j:512 * j + 512])[:, :, 0:rows], ACT.Copy).then_inc(hi, 1)

            def store(t, u, n, rows=P):
                act.wait_ge(add, t + 3)
                act.dma_start(to_of(t, rows), x[u][0:rows, :]).then_inc(stored[u], 16)
            act.sem_inc(mm, 2)
            upper(0, 0, 1)
            upper(1, 1, 1)
            with act.Fori(0, T // 2 - 1) as i:
                store(i * 2, 0, i + 1)
                upper(i * 2 + 2, 0, i + 2)
                store(i * 2 + 1, 1, i + 1)
                upper(i * 2 + 3, 1, i + 2)
            store(T - 2, 0, 4)
            upper(T, 0, 5, SMP)
            store(T - 1, 1, 4)
            store(T, 0, 5, SMP)
            act.wait_ge(stored[0], 6 * 16)
            act.wait_ge(stored[1], 5 * 16)

        @block.vector
        def _(dve):
            dve.sem_inc(lo, 3)
            dve.sem_inc(add, 2)
            link = Link(dve, chain)

            def lower(t, u, n, rows=P):
                for j in range(3):
                    dve.wait_ge(hi, 3 * t + j + 1)
                    nc.vector.tensor_tensor(yl[u][:, 4 * j:4 * j + 4, 0:rows],
                                            heads(psT[:, 512 * j:512 * j + 512])[:, :, 0:rows],
                                            yh[u][:, 4 * j:4 * j + 4, 0:rows], ALU.subtract).then_inc(lo, 1)

            def sums(t, u, n, rows=P):
                dve.wait_ge(mm, t + 3)
                dve.wait_ge(x_in[u], n * 16)
                nc.vector.tensor_tensor(x[u][0:rows, :], psO[u][0:rows, :], x[u][0:rows, :], ALU.add).then_inc(add, 1)
            for j in range(OUT_PIECES):
                dve.wait_ge(c.wo_in[j % 2], (j // 2 + 1) * 16)
                rows3 = slice(OUT_ROWS * j, OUT_ROWS * (j + 1))
                split(nc.vector, link, c.wo[j % 2][:, :, :], wh[:, rows3, :], wl[:, rows3, :]).then_inc(pieces, 1)
                if j < 2:
                    lower(j, j, 1)
            with dve.Fori(0, T // 2 - 1) as i:
                sums(i * 2, 0, i + 1)
                lower(i * 2 + 2, 0, i + 2)
                sums(i * 2 + 1, 1, i + 1)
                lower(i * 2 + 3, 1, i + 2)
            sums(T - 2, 0, 4)
            lower(T, 0, 5, SMP)
            sums(T - 1, 1, 4)
            sums(T, 0, 5, SMP)


def project_indexer(nc, c):
    N, T, BANKS = IH + ID, TILES, 4
    with Stage(nc, "projidx") as s:
        w = s.sb("w_halves", [P, KC, 2, N], F32R)
        st = s.sb("st", [P, T + 1, N])
        ps = [s.ps(f"acc{u}") for u in range(BANKS)]
        mm, ev, stored = s.sem("products"), s.sem("evacuated"), s.sem("stored", 2)
        chain, halves = s.sem("dve_chain"), s.sem("weights_split")
        block = s.block()

        @block.sync
        def _(sp):
            sp.wait_ge(ev, T)
            sp.dma_start(c.h_odd[0:SEQ, O_WK:O_WK + N].rearrange("(t p) n -> p t n", p=P), st[:, 0:T, :])\
                .then_inc(stored[0], 16)
            sp.wait_ge(ev, T + 1)
            sp.dma_start(c.h_odd[SEQ:TOK, O_WK:O_WK + N], st[0:SMP, T, :]).then_inc(stored[1], 16)
            for r in stored:
                sp.wait_ge(r, 16)

        @block.tensor
        def _(pe):
            pe.wait_ge(halves, 1)
            for t in range(T + 1):
                rows = P if t < T else SMP
                if t >= BANKS:
                    pe.wait_ge(ev, t - BANKS + 1)
                to = slice(P * t, P * t + rows)
                out = ps[t % BANKS][0:rows, 0:2 * N]
                for k in range(KC):
                    nc.tensor.matmul(out, c.xh[:, k, to], w[:, k].rearrange("p j n -> p (j n)"),
                                     start=(k == 0), stop=False)
                    ins = nc.tensor.matmul(out[:, 0:N], c.xl[:, k, to], w[:, k, 0, :], start=False, stop=(k == KC - 1))
                ins.then_inc(mm, 1)

        @block.vector
        def _(dve):
            dve.wait_ge(c.small_in, 16)
            split(nc.vector, Link(dve, chain), c.w_small[:, :, :], w[:, :, 0, :], w[:, :, 1, :]).then_inc(halves, 1)
            for t in range(T + 1):
                rows = P if t < T else SMP
                dve.wait_ge(mm, t + 1)
                nc.vector.tensor_reduce(st[0:rows, t, :], ps[t % BANKS][0:rows, 0:2 * N].rearrange("p (j n) -> p n j", j=2),
                                        AX.X, ALU.add).then_inc(ev, 1)


def sparse_memory(c, L):
    c.qT = L.sb("qT", [P, QH, TOK])
    c.kT = L.sb("kT", [P, KVH, TOK])
    c.qiT = L.sb("qiT", [P, IH // 2, TOK])
    c.kiT = L.sb("kiT", [P, TOK])
    c.v = L.sb("v", [P, TILES + 1, KVH * HD])
    c.wi = L.sb("wi", [P, TILES + 1, IH])
    c.page_ids = L.sb("pages", [1, NB * PAGES], mybir.dt.int32)
    c.ip = L.sb("ip", [P, NB, PAGES, ID])
    c.kp, c.vp = ([L.sb(f"{n}{u}", [P, PAGES, KVH * HD]) for u in range(2)] for n in ("kp", "vp"))
    c.ids_in, c.ip_in = L.pool_sem("table_in"), L.pool_sem("ip_in")
    c.kp_in, c.vp_in = L.pool_sem("kp_in", 2), L.pool_sem("vp_in", 2)


def load_pages(sp, c, a, b, cache, to, sem):
    n_pool = a[cache].shape[1]
    for p in range(PAGES):
        at = PAGES * b + p
        page = sp.value_load(c.page_ids[0:1, at:at + 1], min_val=0, max_val=n_pool - 1)
        src = a[cache][0, bass.ds(page, 1)]
        src = src.rearrange("o s d -> (o s) d") if len(src.shape) == 3 else src.rearrange("o s h d -> (o s) (h d)")
        sp.dma_start(to[:, p, :], src).then_inc(sem, 16)


def sparse_prepare(nc, c, a, o):
    T, QK, H10 = TILES, (QH + KVH) * HD, QH + KVH
    B = 4
    with Stage(nc, "prep") as s:
        qk = [s.sb(f"qk{u}", [P, QK]) for u in range(B)]
        ik = [s.sb(f"ik{u}", [P, (IH + 2) * ID]) for u in range(B)]
        rt = [s.sb(f"rope{u}", [P, 2, HD // 8]) for u in range(B)]
        ri = [s.sb(f"ropei{u}", [P, 2, ID // 8]) for u in range(B)]
        sq = s.sb("sq", [P, QK])
        gam = s.sb("gam", [P, H10, HD])
        ssq = [s.sb(f"ssq{u}", [P, H10]) for u in range(B)]
        tmp = s.sb("tmp", [P, 4, H10, HD // 8])
        tmi = s.sb("tmi", [P, 4, IH + 1, ID // 8])
        ps = [s.ps(f"t{u}", 2048) for u in range(2)]
        qk_in, ik_in, rt_in, v_in, gam_in, stored = (s.sem("qk_in", B), s.sem("ik_in", B), s.sem("rope_in", B),
                                                      s.sem("v_in", B), s.sem("gamma_in"), s.sem("stored", B))
        squ, red, rs, sc, gd, rq, ri_d, tr, ev, wd, dch, pch = (s.sem(n) for n in (
            "squares", "sums", "rstd", "scaled", "weighted", "rotated", "index_rotated", "transposed",
            "copied", "wi", "dve_chain", "pool_chain"))
        dch2 = s.sem("dve_chain_rope")
        block = s.block()

        @block.sync
        def _(sp):
            for r in stored:
                sp.sem_inc(r, 48)
            sp.dma_start(gam[:, 0:QH, :], a["attn_qn"].unsqueeze(0).broadcast_to([P, QH, HD])).then_inc(gam_in, 16)
            sp.dma_start(gam[:, QH:H10, :], a["attn_kn"].unsqueeze(0).broadcast_to([P, KVH, HD])).then_inc(gam_in, 16)

            def load(t, u, n, rows):
                sp.wait_ge(tr, t + 1)
                sp.wait_ge(stored[u], n * 48)
                r = rows_of(t, rows)
                tt = bass.ds(t, 1)
                sp.dma_start(qk[u][0:rows, :], c.h_odd[r, 0:QK]).then_inc(qk_in[u], 16)
                sp.dma_start(ik[u][0:rows, 0:IH * ID], c.h_odd[r, O_QI:O_QI + IH * ID]).then_inc(ik_in[u], 16)
                sp.dma_start(ik[u][0:rows, IH * ID:(IH + 1) * ID], c.h_odd[r, O_WK + IH:O_WK + IH + ID])\
                    .then_inc(ik_in[u], 16)
                sp.dma_start(rt[u][0:rows], a["rope"][r]).then_inc(rt_in[u], 16)
                sp.dma_start(ri[u][0:rows], a["rope_idx"][r]).then_inc(rt_in[u], 16)
                sp.dma_start(c.v[0:rows, tt, :].rearrange("p o d -> p (o d)"), c.h_odd[r, O_KV + KVH * HD:O_KV + 2 * KVH * HD])\
                    .then_inc(v_in[u], 16)
                sp.dma_start(c.wi[0:rows, tt, :].rearrange("p o d -> p (o d)"), c.h_odd[r, O_WK:O_WK + IH])\
                    .then_inc(v_in[u], 16)
            each_tile(sp, load, B)

        @block.scalar
        def _(act):
            act.sem_inc(ev, 2 * 5)
            n_out = KVH * HD

            def squares(t, u, n, rows=P):
                act.wait_ge(qk_in[u], n * 16)
                act.wait_ge(red, t + 1)
                nc.scalar.activation(sq[0:rows, :], qk[u][0:rows, :], ACT.Square).then_inc(squ, 1)

            def copies(t, u, n, rows=P):
                r = rows_of(t, rows)
                if rows == P:
                    ko, vo, io = (o[x][0, 0, r] for x in (9, 10, 11))
                    ko, vo = (x.rearrange("t h d -> t (h d)") for x in (ko, vo))
                else:
                    ko, vo = (o[x][0].rearrange("b t h d -> (b t) (h d)") for x in (12, 13))
                    io = o[14][0].rearrange("b t d -> (b t) d")
                act.wait_ge(rq, t + 1)
                act.dma_start(ko, qk[u][0:rows, QH * HD:QK]).then_inc(stored[u], 16)
                act.wait_ge(ri_d, t + 1)
                act.dma_start(io, ik[u][0:rows, IH * ID:(IH + 1) * ID]).then_inc(stored[u], 16)
                act.wait_ge(v_in[u], n * 32)
                act.dma_start(vo, c.v[0:rows, bass.ds(t, 1), :].rearrange("p o d -> p (o d)")).then_inc(stored[u], 16)
                act.wait_ge(tr, t + 1 + B)
                to = slice(SEQ, TOK) if rows == SMP else bass.ts(t, P)
                for j, dst in enumerate((c.qT[:, 0:4, to], c.qT[:, 4:8, to], c.qiT[:, :, to])):
                    nc.scalar.activation(dst, heads(ps[u % 2][:, 512 * j:512 * j + 512])[:, :, 0:rows], ACT.Copy).then_inc(ev, 1)
                nc.scalar.activation(c.kT[:, :, to], heads(ps[u % 2][:, 1536:1792], 2)[:, :, 0:rows], ACT.Copy).then_inc(ev, 1)
                nc.scalar.activation(c.kiT[:, to], ps[u % 2][:, 1792:1792 + rows], ACT.Copy).then_inc(ev, 1)
            squares(0, 0, 1)
            squares(1, 1, 1)
            with act.Fori(0, T // B - 1) as i:
                for u in range(B):
                    squares(i * B + u + 2, (u + 2) % B, i + 1 + (u + 2) // B)
                    copies(i * B + u, u, i + 1)
            for u in range(B):
                t = T - B + u + 2
                if t <= T:
                    squares(t, t % B, t // B + 1, P if t < T else SMP)
                copies(T - B + u, u, T // B)
            copies(T, 0, T // B + 1, SMP)
            for u in range(B):
                act.wait_ge(stored[u], (T // B + 1 + (u == 0)) * 48)

        @block.gpsimd
        def _(pool):
            link = Link(pool, pch)
            G = nc.gpsimd

            def indexer(t, u, n, rows=P):
                link.at(t * 2)
                pool.wait_ge(ik_in[u], n * 32)
                pool.wait_ge(rt_in[u], n * 32)
                v = ik[u][0:rows, 0:(IH + 1) * ID].rearrange("p (h d) -> p h d", d=ID)
                rotate(G, link, v, ID // 8, ri[u], tmi, rows, IH + 1)
                k = ik[u][0:rows, IH * ID:(IH + 1) * ID]
                G.tensor_tensor(ik[u][0:rows, (IH + 1) * ID:], k, c.one[0:rows, :].broadcast_to([rows, ID]), ALU.mult).then_inc(ri_d, 1)
                pool.wait_ge(red, t + 2)
                q = ssq[u][0:rows, :]
                G.tensor_tensor(q, q, c.half[0:rows, 0:H10], ALU.pow).then_inc(rs, 1)

            def weigh(t, u, n, rows=P):
                x = qk[u][0:rows, :]
                pool.wait_ge(sc, t + 1)
                G.tensor_tensor(heads(x, H10), heads(x, H10), gam[0:rows], ALU.mult).then_inc(gd, 1)
            pool.wait_ge(gam_in, 32)

            two_ahead(pool, indexer, weigh, B)
            indexer(T, 0, T // B + 1, SMP)
            weigh(T, 0, T // B + 1, SMP)

        @block.vector
        def _(dve):
            link, link2 = Link(dve, dch), Link(dve, dch2)
            V = nc.vector
            dve.sem_inc(red, 1)

            def scale(t, u, n, rows=P):
                link.at(t)
                x = heads(qk[u][0:rows, :], H10)
                dve.wait_ge(v_in[u], n * 32)
                w = c.wi[0:rows, bass.ds(t, 1), :]
                V.tensor_scalar(w, w, IH ** -0.5, None, ALU.mult).then_inc(wd, 1)
                dve.wait_ge(squ, t + 1)
                link(V.tensor_reduce(ssq[u][0:rows, :], heads(sq[0:rows, :], H10), AX.X, ALU.add))
                V.tensor_scalar(ssq[u][0:rows, :], ssq[u][0:rows, :], 1.0 / HD, EPS, ALU.mult, ALU.add).then_inc(red, 1)
                dve.wait_ge(rs, t + 1)
                V.tensor_tensor(x, x, bc(ssq[u][0:rows, :], 2, HD), ALU.mult).then_inc(sc, 1)

            def turn(t, u, n, rows=P):
                link2.at(t * 2)
                x = heads(qk[u][0:rows, :], H10)
                dve.wait_ge(gd, t + 1)
                dve.wait_ge(rt_in[u], n * 32)
                rotate(V, link2, x, HD // 8, rt[u], tmp, rows, H10)
                dve.sem_inc(rq, 1)

            two_ahead(dve, scale, turn, B)
            scale(T, 0, T // B + 1, SMP)
            turn(T, 0, T // B + 1, SMP)

        @block.tensor
        def _(pe):
            pe.sem_inc(tr, B)

            def transposes(t, u, n, rows):
                pe.wait_ge(rq, t + 1)
                pe.wait_ge(ri_d, t + 1)
                pe.wait_ge(ev, t * 5 + 5)
                I = c.ident[0:rows, 0:rows]
                for h in range(QH):
                    nc.tensor.transpose(ps[u % 2][:, P * h:P * h + rows], qk[u][0:rows, P * h:P * h + P], I)
                for h in range(IH // 2):
                    nc.tensor.transpose(ps[u % 2][:, 1024 + P * h:1024 + P * h + rows], ik[u][0:rows, P * h:P * h + P], I)
                for h in range(KVH):
                    nc.tensor.transpose(ps[u % 2][:, 1536 + P * h:1536 + P * h + rows],
                                        qk[u][0:rows, P * (QH + h):P * (QH + h + 1)], I)
                nc.tensor.transpose(ps[u % 2][:, 1792:1792 + rows], ik[u][0:rows, IH * ID:(IH + 2) * ID], I).then_inc(tr, 1)
            each_tile(pe, transposes, B)


def rotate(eng, link, x, half, table, tmp, rows, n):
    cos, sin = (bc(table[0:rows, j, :], 1, n) for j in range(2))
    x1, x2 = x[:, :, 0:half], x[:, :, half:2 * half]
    t = [tmp[0:rows, j] for j in range(4)]
    eng.tensor_tensor(t[0], x1, cos, ALU.mult)
    eng.tensor_tensor(t[1], x2, sin, ALU.mult)
    eng.tensor_tensor(t[2], x2, cos, ALU.mult)
    link(eng.tensor_tensor(t[3], x1, sin, ALU.mult))
    eng.tensor_tensor(x1, t[0], t[1], ALU.subtract)
    link(eng.tensor_tensor(x2, t[2], t[3], ALU.add))


def pick_top(dve, link, scores, best, rounds=TOPK // 8):
    for _ in range(rounds):
        link(dve.max(best, scores))
        link(dve.match_replace(scores, best, scores, TAKEN))


def sparse_prompt(nc, c, a):
    B, FIRST = TILES, TOPK // P
    SC = HD ** -0.5
    with Stage(nc, "sparse_p") as s:
        relu = [s.sb(f"relu{u}", [P, SEQ]) for u in range(2)]
        acc = s.sb("scores", [P, SEQ])
        best = s.sb("best", [P, 8])
        bias = [s.sb(f"bias{u}", [P, SEQ]) for u in range(2)]
        sm = [s.sb(f"masked{u}", [P, SEQ]) for u in range(2)]
        pr = [s.sb(f"p{u}", [P, SEQ]) for u in range(2)]
        pT = [s.sb(f"pT{u}", [P, B, P]) for u in range(2)]
        mx, neg, tot, rec = ([s.sb(f"{n}{u}", [P, 1]) for u in range(2)] for n in ("max", "neg", "total", "rec"))
        gc = [s.sb(f"gate{u}", [P, QH * HD]) for u in range(2)]
        yb = [s.sb(f"y{u}", [P, QH * HD]) for u in range(2)]
        psS = [s.ps(f"s{u}", 1024) for u in range(2)]
        psT = s.ps("t", 1024)
        psO = [s.ps(f"o{u}") for u in range(2)]
        g_in, stored = s.sem("gate_in", 2), s.sem("stored", 2)
        xs, xr, xa, bd, ss, md, ng, ex, tr, te, od, rc, yd, dch = (s.sem(n) for n in (
            "index_scores", "relus", "added", "bias", "scores", "masked", "neg_max", "exps", "transposed", "pT_copied",
            "mixed", "reciprocal", "y", "dve_chain"))
        block = s.block()
        job = lambda i, h: QH * i + h
        idx = lambda i, h: IH * (i - FIRST) + h

        def blocks(index, attend):
            for i in range(B):
                if FIRST <= i + 1 < B:
                    index(i + 1, (i + 2) * P)
                attend(i, (i + 1) * P)

        @block.sync
        def _(sp):
            sp.dma_start(c.page_ids[:, :], a["page_table"].rearrange("b p -> (b p)").unsqueeze(0)).then_inc(c.ids_in, 16)
            for i in range(B):
                if i >= 2:
                    sp.wait_ge(yd, job(i - 2, QH - 1) + 1)
                sp.dma_start(gc[i % 2][:, :], c.h_odd[P * i:P * i + P, O_GC:O_GC + QH * HD]).then_inc(g_in[i % 2], 16)
                if i >= 1:
                    j = i - 1
                    sp.wait_ge(yd, job(j, QH - 1) + 1)
                    sp.dma_start(c.y_odd[P * j:P * j + P, 0:QH * HD], yb[j % 2][:, :]).then_inc(stored[j % 2], 16)
                if i == 1:
                    sp.wait_ge(c.ids_in, 16)
                if 1 <= i <= NB // 2:
                    for b in (2 * i - 2, 2 * i - 1):
                        load_pages(sp, c, a, b, "cache_idx_k", c.ip[:, b], c.ip_in)
                elif NB // 2 < i <= NB // 2 + 2:
                    b = i - NB // 2 - 1
                    load_pages(sp, c, a, b, "cache_attn_k", c.kp[b], c.kp_in[b])
                    load_pages(sp, c, a, b, "cache_attn_v", c.vp[b], c.vp_in[b])
            j = B - 1
            sp.wait_ge(yd, job(j, QH - 1) + 1)
            sp.dma_start(c.y_odd[P * j:P * j + P, 0:QH * HD], yb[j % 2][:, :]).then_inc(stored[j % 2], 16)
            sp.wait_ge(stored[0], B // 2 * 16)
            sp.wait_ge(stored[1], B // 2 * 16)

        @block.tensor
        def _(pe):
            def keys(n):
                return [(k, min(512, n - k)) for k in range(0, n, 512)]

            def index(i, n):
                for h in range(IH):
                    u, at = h % 2, ID * (h % 2)
                    if h < 2 and i > FIRST:
                        pe.wait_ge(md, job(i - 1, 0))
                    if h >= 2:
                        pe.wait_ge(xr, idx(i, h) - 1)
                    for k, m in keys(n):
                        ins = nc.tensor.matmul(psS[u][:, k:k + m], c.qiT[at:at + ID, h // 2, P * i:P * i + P],
                                               c.kiT[at:at + ID, k:k + m], start=True, stop=True)
                    ins.then_inc(xs, 1)

            def scores(i, h, n):
                g = job(i, h)
                if h < 2:
                    if i + 1 >= FIRST:
                        pe.wait_ge(xr, idx(min(i + 1, B - 1), IH))
                    if i >= 1:
                        pe.wait_ge(md, job(i, 0))
                else:
                    pe.wait_ge(md, g - 1)
                for k, m in keys(n):
                    ins = nc.tensor.matmul(psS[g % 2][:, k:k + m], c.qT[:, h, P * i:P * i + P],
                                           c.kT[:, h // 4, k:k + m], start=True, stop=True)
                ins.then_inc(ss, 1)

            def attend(i, n):
                scores(i, 0, n)
                for h in range(QH):
                    g = job(i, h)
                    if h + 1 < QH:
                        scores(i, h + 1, n)
                    pe.wait_ge(ex, g + 1)
                    if g:
                        pe.wait_ge(te, g)
                    for k in range(i + 1):
                        ins = nc.tensor.transpose(psT[:, P * k:P * k + P], pr[g % 2][:, P * k:P * k + P], c.ident[:, :])
                    ins.then_inc(tr, 1)
                    pe.wait_ge(te, g + 1)
                    if g >= 2:
                        pe.wait_ge(yd, g - 1)
                    for k in range(i + 1):
                        ins = nc.tensor.matmul(psO[g % 2][:, 0:P], pT[g % 2][:, k, :],
                                               c.v[:, k, HD * (h // 4):HD * (h // 4) + HD], start=(k == 0), stop=(k == i))
                    ins.then_inc(od, 1)
            blocks(index, attend)

        @block.scalar
        def _(act):
            def index(i, n):
                for h in range(IH):
                    act.wait_ge(xs, idx(i, h) + 1)
                    if idx(i, h) >= 2:
                        act.wait_ge(xa, idx(i, h) - 1)
                    nc.scalar.activation(relu[h % 2][:, 0:n], psS[h % 2][:, 0:n], ACT.Relu, scale=ID ** -0.5)\
                        .then_inc(xr, 1)

            def attend(i, n):
                for h in range(QH):
                    g = job(i, h)
                    act.wait_ge(ng, g + 1)
                    nc.scalar.activation(pr[g % 2][:, 0:n], sm[g % 2][:, 0:n], ACT.Exp, bias=neg[g % 2][:, :],
                                         scale=SC, accum_out=tot[g % 2][:, :]).then_inc(ex, 1)
                    act.wait_ge(tr, g + 1)
                    nc.scalar.activation(pT[g % 2][:, 0:i + 1, :], psT[:, 0:n].rearrange("p (k q) -> p k q", q=P),
                                         ACT.Copy).then_inc(te, 1)
            blocks(index, attend)

        @block.vector
        def _(dve):
            V = nc.vector
            link = Link(dve, dch)
            base = 0

            def index(i, n):
                for h in range(IH):
                    w = c.wi[:, i, h:h + 1]
                    dve.wait_ge(xr, idx(i, h) + 1)
                    if h == 0:
                        ins = V.tensor_scalar(acc[:, 0:n], relu[0][:, 0:n], w, None, ALU.mult)
                    else:
                        ins = V.scalar_tensor_tensor(acc[:, 0:n], relu[h % 2][:, 0:n], w, acc[:, 0:n], ALU.mult, ALU.add)
                    ins.then_inc(xa, 1)
                    dve.wait_ge(xa, idx(i, h) + 1)
                link(V.tensor_tensor(acc[:, n - P:n], acc[:, n - P:n], c.lid_qk[:, :], ALU.min))

            def top(i, n, rounds):
                if FIRST <= i < B:
                    pick_top(dve, link, acc[:, 0:n], best[:, :], rounds)

            def chosen(i, n):
                link(V.tensor_scalar(bias[i % 2][:, 0:n], acc[:, 0:n], -3.2e38, NEG, ALU.is_gt, ALU.mult))

            def masked(i, h, n):
                g = job(i, h)
                dve.wait_ge(ss, g + 1)
                if g >= 2:
                    dve.wait_ge(ex, g - 1)
                V.tensor_tensor_reduce(sm[g % 2][:, 0:n], psS[g % 2][:, 0:n], bias[i % 2][:, 0:n], 1.0, -3.4e38,
                                       ALU.add, ALU.max, mx[g % 2][:, :]).then_inc(md, 1)
                dve.wait_ge(md, g + 1)
                V.tensor_scalar(neg[g % 2][:, :], mx[g % 2][:, :], -SC, None, ALU.mult).then_inc(ng, 1)

            def attend(i, n):
                if i < FIRST:
                    if i:
                        link(V.memset(bias[i][:, 0:n - P], 0.0))
                    link(V.tensor_copy(bias[i][:, n - P:n], c.neg_qk[:, :]))
                masked(i, 0, n)
                dve.wait_ge(g_in[i % 2], 16 * (i // 2 + 1))
                if i >= 2:
                    dve.wait_ge(stored[i % 2], 16 * (i // 2))
                for h in range(QH):
                    g = job(i, h)
                    if h + 1 < QH:
                        masked(i, h + 1, n)
                    top(i + 1, n + P, TOPK // 8 // QH // 2)
                    dve.wait_ge(ex, g + 1)
                    V.reciprocal(rec[g % 2][:, :], tot[g % 2][:, :]).then_inc(rc, 1)
                    dve.wait_ge(rc, g + 1)
                    top(i + 1, n + P, TOPK // 8 // QH // 2)
                    dve.wait_ge(od, g + 1)
                    e = slice(P * h, P * h + P)
                    V.scalar_tensor_tensor(yb[i % 2][:, e], psO[g % 2][:, 0:P], rec[g % 2][:, :], gc[i % 2][:, e],
                                           ALU.mult, ALU.mult).then_inc(yd, 1)
                if FIRST <= i + 1 < B:
                    chosen(i + 1, n + P)
            blocks(index, attend)


def sparse_sample(nc, c, a):
    SC = HD ** -0.5
    N = PAST + NT
    with Stage(nc, "sparse_s") as s:
        ip = [s.sb(f"ip{u}", [P, PAGES, 2 * ID]) for u in range(2)]
        kp, kp_in = c.kp, c.kp_in
        own_place = c.ip[:, :, :, :].rearrange("p (j b) g d -> p j (b g d)", j=2)
        vp = c.vp + [own_place[:, j, :].rearrange("p (g n) -> p g n", g=PAGES) for j in range(2)] + kp
        vp_in = c.vp_in + s.sem("vp_in", 4)
        kT = [s.sb(f"kT{u}", [P, 1024]) for u in range(2)]
        qiT, qT = s.sb("qiT", [P, P]), s.sb("qT", [P, KVH, P])
        qim, qm = s.sb("qim", [P, NB, P]), s.sb("qm", [P, KVH, NB, P])
        wr = s.sb("w_rows", [P, 2])
        ok, okr = s.sb("ok", [SMP, NT]), s.sb("ok_rows", [P, NT])
        xr = s.sb("relus", [P, 2, N])
        tmp = s.sb("tmp", [P, KVH, NB * NT])
        acc = s.sb("scores", [SMP, N])
        best = s.sb("best", [SMP, 8])
        new = s.sb("new", [P, KVH, NT])
        mxa, mxb, neg, tot, totb = (s.sb(n, [P, KVH]) for n in ("mxa", "mxb", "neg", "tot", "totb"))
        pr = xr
        pn = s.sb("p_new", [P, KVH, NB * NT])
        pT = s.sb("pT", [P, KVH, PAGES, P])
        pnT = s.sb("p_newT", [NB * NT, KVH, P])
        gc = s.sb("gate", [4 * NT, KVH, NB, HD])
        y = gc
        psX = [s.ps(f"x{u}", 1024) for u in range(2)]
        psT = [s.ps(f"t{u}", 1024) for u in range(2)]
        twice, g_in, out = s.sem("ip_twice"), s.sem("gate_in"), s.sem("stored")
        (qd, itr, ica, icd, ixs, inw, xrd, xsum, sel, ktr, kca, ssd, biased, nw, nwr, ngd, exd, pnd, ptr, pte, pnt,
         od, yd, dch, ach) = (s.sem(n) for n in (
            "queries", "ip_transposed", "ipT_by_act", "ipT_by_dve", "index_scores", "index_new", "relus", "index_sums",
            "selected", "k_transposed", "kT_copied", "scores", "bias", "new_scores", "new_read", "neg_max", "exps",
            "p_normed", "p_transposed", "pT_copied", "p_new_transposed", "mixed", "y",
            "dve_chain", "act_chain"))

        def by_head(rows, at, n, g):
            at += HD * (4 * n + g)
            return rows[SEQ:TOK, at:at + HD].rearrange("(b t) d -> t b d", b=NB)

        def mixed(n):
            return psX[n][0:4 * NT, :].rearrange("p (b d) -> p b d", b=NB)
        xsr, xsr2 = s.sem("relus_read"), s.sem("index_sums_read")
        block = s.block()

        @block.sync
        def _(sp):
            for n in range(KVH):
                for g in range(4):
                    sp.dma_start(gc[NT * g:NT * g + NT, n], by_head(c.h_odd, O_GC, n, g)).then_inc(g_in, 16)
            sp.wait_ge(twice, NB)
            for b in (2, 3):
                load_pages(sp, c, a, b, "cache_attn_v", vp[b], vp_in[b])
            for b in range(2, NB):
                sp.wait_ge(ktr, KVH * (b - 1))
                load_pages(sp, c, a, b, "cache_attn_k", kp[b % 2], kp_in[b % 2])
            sp.wait_ge(ktr, KVH * NB)
            for b in (4, 5):
                load_pages(sp, c, a, b, "cache_attn_v", vp[b], vp_in[b])
            for b in (6, 7):
                sp.wait_ge(od, b - 5)
                load_pages(sp, c, a, b, "cache_attn_v", vp[b % 6], vp_in[b % 6])
            for n in range(KVH):
                sp.wait_ge(yd, n + 1)
                for g in range(4):
                    sp.dma_start(by_head(c.y_odd, 0, n, g), y[NT * g:NT * g + NT, n]).then_inc(out, 16)
            sp.wait_ge(out, 4 * KVH * 16)

        @block.gpsimd
        def _(pool):
            pool.wait_ge(c.ip_in, NB * PAGES * 16)
            for b in range(NB):
                if b >= 2:
                    pool.wait_ge(itr, b - 1)
                for j in range(2):
                    ins = nc.gpsimd.tensor_copy(ip[b % 2][:, :, ID * j:ID * j + ID], c.ip[:, b])
                ins.then_inc(twice, 1)

        @block.tensor
        def _(pe):
            T = nc.tensor
            pe.wait_ge(qd, 1)
            for b in range(NB):
                u = b % 2
                pe.wait_ge(twice, b + 1)
                if b >= 2:
                    pe.wait_ge(ica, b - 1)
                    pe.wait_ge(icd, b - 1)
                for p in range(PAGES):
                    ins = T.transpose(psT[u][:, P * p:P * p + P], ip[u][:, p, :], c.ident[:, :])
                ins.then_inc(itr, 1)
                pe.wait_ge(ica, b + 1)
                pe.wait_ge(icd, b + 1)
                for j in range(2):
                    e = slice(ID * j, ID * j + ID)
                    for k in range(2):
                        ins = T.matmul(psX[j][:, 512 * k:512 * k + 512], qim[e, b, :], kT[u][e, 512 * k:512 * k + 512],
                                       start=(b == 0), stop=(b == NB - 1), skip_group_check=True)
                ins.then_inc(ixs, 1)
            for j in range(2):
                e = slice(ID * j, ID * j + ID)
                ins = T.matmul(psT[j][:, 0:SMP], qiT[e, :], c.kiT[e, SEQ:TOK], start=True, stop=True)
            ins.then_inc(inw, 1)
            pe.wait_ge(xrd, 6)
            for k, m in ((0, 512), (512, 512)):
                for j in range(2):
                    T.matmul(psX[0][0:SMP, k:k + m], c.tok_of[:, :], xr[:, j, k:k + m], start=(j == 0), stop=(j == 1))
            for j in range(2):
                ins = T.matmul(psX[1][0:SMP, 0:NT], c.tok_of[:, :], xr[:, j, PAST:N], start=(j == 0), stop=(j == 1))
            ins.then_inc(xsum, 1)
            pe.wait_ge(xsr2, 2)
            for b in range(NB):
                u = b % 2
                pe.wait_ge(kp_in[u], (b // 2 + 1) * PAGES * 16)
                for n in range(KVH):
                    g = KVH * b + n
                    if g >= 2:
                        pe.wait_ge(kca, 2 * (g - 1))
                    for p in range(PAGES):
                        ins = T.transpose(psT[n][:, P * p:P * p + P], kp[u][:, p, HD * n:HD * n + HD], c.ident[:, :])
                    ins.then_inc(ktr, 1)
                    pe.wait_ge(kca, 2 * (g + 1))
                    for k in range(2):
                        ins = T.matmul(psX[n][:, 512 * k:512 * k + 512], qm[:, n, b, :], kT[n][:, 512 * k:512 * k + 512],
                                       start=(b == 0), stop=False, skip_group_check=True)
                    ins.then_inc(ssd, 1)
            pe.wait_ge(sel, 1)
            for n in range(KVH):
                for k in range(2):
                    T.matmul(psX[n][:, 512 * k:512 * k + 512], c.tok_to[:, :], acc[:, 512 * k:512 * k + 512],
                             start=False, stop=True, skip_group_check=True)
                T.matmul(psT[0][:, SMP * n:SMP * n + SMP], qT[:, n, :], c.kT[:, n, SEQ:TOK], start=True, stop=True)
            T.matmul(psT[0][:, 64:64 + NT], c.tok_to[:, :], acc[:, PAST:N], start=True, stop=True).then_inc(biased, 1)
            pe.wait_ge(pnd, 2)
            for n in range(KVH):
                if n:
                    pe.wait_ge(pte, 1)
                for p in range(PAGES):
                    ins = T.transpose(psT[n][:, P * p:P * p + P], pr[:, n, P * p:P * p + P], c.ident[:, :])
                ins.then_inc(ptr, 1)
            pe.wait_ge(pte, 2)
            for n in range(KVH):
                ins = T.transpose(psT[0][0:SMP, P * n:P * n + P], pn[:, n, :], c.ident[:, :])
            ins.then_inc(pnt, 1)
            pe.wait_ge(pte, 3)
            for b in range(NB):
                u = b % 6
                pe.wait_ge(vp_in[u], (b // 6 + 1) * PAGES * 16)
                for n in range(KVH):
                    def own(t):
                        return t[:, 4 * NT * b:4 * NT * (b + 1)]
                    out = mixed(n)[:, b, :]
                    for p in range(PAGES):
                        T.matmul(out, own(pT[:, n, p, :]), vp[u][:, p, HD * n:HD * n + HD], start=(p == 0), stop=False)
                    ins = T.matmul(out, own(pnT[:, n, :]), c.v[0:SMP, TILES, HD * n:HD * n + HD],
                                   start=False, stop=True)
                ins.then_inc(od, 1)

        @block.scalar
        def _(act):
            A = nc.scalar.activation
            link = Link(act, ach)
            for b in range(NB):
                u = b % 2
                act.wait_ge(itr, b + 1)
                if b >= 2:
                    act.wait_ge(ixs, b - 1)
                A(kT[u][:, 0:512], psT[u][:, 0:512], ACT.Copy).then_inc(ica, 1)
            act.wait_ge(ixs, NB)
            for j in range(2):
                A(xr[:, j, 0:PAST], psX[j][:, :], ACT.Relu, scale=ID ** -0.5).then_inc(xsr, 1)
            act.wait_ge(inw, 1)
            for j in range(2):
                A(tmp[:, j, :], psT[j][:, 0:SMP], ACT.Relu, scale=ID ** -0.5).then_inc(xsr, 1)
            for g in range(KVH * NB):
                n = g % 2
                act.wait_ge(ktr, g + 1)
                if g >= 2:
                    act.wait_ge(ssd, g - 1)
                for k in range(2):
                    A(kT[n][:, 512 * k:512 * k + 512], psT[n][:, 512 * k:512 * k + 512], ACT.Copy).then_inc(kca, 1)
            act.wait_ge(ngd, 1)
            for n in range(KVH):
                A(pr[:, n, 0:PAST], psX[n][:, :], ACT.Exp, bias=neg[:, n:n + 1], scale=SC,
                  accum_out=tot[:, n:n + 1]).then_inc(exd, 1)
                A(pr[:, n, PAST:N], new[:, n, :], ACT.Exp, bias=neg[:, n:n + 1], scale=SC,
                  accum_out=totb[:, n:n + 1]).then_inc(exd, 1)
            for n in range(KVH):
                act.wait_ge(ptr, n + 1)
                for g in range(4):
                    ins = A(pT[:, n, :, :].rearrange("p k (b g t) -> p k g b t", b=NB, g=4)[:, :, g],
                            psT[n][:, :].rearrange("p (k g b t) -> p k g b t", k=PAGES, g=4, b=NB)[:, :, g], ACT.Copy)
                ins.then_inc(pte, 1)
            act.wait_ge(pnt, 1)
            for n in range(KVH):
                ins = A(pnT[:, n, :].rearrange("p (b g t) -> p g b t", b=NB, g=4),
                        psT[0][0:SMP, P * n:P * n + P].rearrange("p (g b t) -> p g b t", g=4, b=NB), ACT.Copy)
            ins.then_inc(pte, 1)

        @block.vector
        def _(dve):
            V = nc.vector
            link = Link(dve, dch)
            own = c.of_seq
            link(V.tensor_copy(qiT[:, :].rearrange("p (g t) -> p g t", g=4), c.qiT[:, :, SEQ:TOK]))
            link(V.tensor_copy(qT[:, :, :].rearrange("p n (g t) -> p (n g) t", g=4), c.qT[:, :, SEQ:TOK]))
            for b in range(NB):
                col = bc(c.seq_cols[:, b, :], 1, 4)
                V.tensor_tensor(qim[:, b, :].rearrange("p (g t) -> p g t", g=4),
                                qiT[:, :].rearrange("p (g t) -> p g t", g=4), col, ALU.mult)
                for n in range(KVH):
                    ins = V.tensor_tensor(qm[:, n, b, :].rearrange("p (g t) -> p g t", g=4),
                                          qT[:, n, :].rearrange("p (g t) -> p g t", g=4), col, ALU.mult)
            ins.then_inc(qd, 1)
            for g in range(4):
                link(V.tensor_copy(wr[SMP * g:SMP * g + SMP, :], c.wi[0:SMP, TILES, 2 * g:2 * g + 2]))
            link(V.tensor_reduce(ok[:, :], c.causal_smp[:, :].rearrange("p (b j) -> p j b", j=NT), AX.X, ALU.add))
            for g in range(4):
                link(V.tensor_copy(okr[SMP * g:SMP * g + SMP, :], ok[:, :]))
            for b in range(NB):
                u = b % 2
                dve.wait_ge(itr, b + 1)
                if b >= 2:
                    dve.wait_ge(ixs, b - 1)
                V.tensor_copy(kT[u][:, 512:1024], psT[u][:, 512:1024]).then_inc(icd, 1)
            dve.wait_ge(xsr, 4)
            for j in range(2):
                V.tensor_scalar(xr[:, j, 0:PAST], xr[:, j, 0:PAST], wr[:, j:j + 1], None, ALU.mult).then_inc(xrd, 1)
                link(V.tensor_scalar(tmp[:, j, :], tmp[:, j, :], wr[:, j:j + 1], None, ALU.mult))
                t = tmp[:, j, :].rearrange("p (b j) -> p b j", j=NT)
                V.tensor_tensor(t, t, bc(own[:, :], 2, NT), ALU.mult).then_inc(xrd, 1)
                dve.wait_ge(xrd, 3 * j + 2)
                V.tensor_reduce(xr[:, j, PAST:N], tmp[:, j, :].rearrange("p (b j) -> p j b", j=NT), AX.X, ALU.add)\
                    .then_inc(xrd, 1)
            dve.wait_ge(xsum, 1)
            V.tensor_copy(acc[:, 0:PAST], psX[0][0:SMP, :]).then_inc(xsr2, 1)
            V.tensor_copy(acc[:, PAST:N], psX[1][0:SMP, 0:NT]).then_inc(xsr2, 1)
            dve.wait_ge(xsr2, 2)
            link(V.tensor_tensor(acc[:, PAST:N], acc[:, PAST:N], ok[:, :], ALU.mult))
            link(V.tensor_scalar(ok[:, :], ok[:, :], 1.0, 3.0e38, ALU.subtract, ALU.mult))
            link(V.tensor_tensor(acc[:, PAST:N], acc[:, PAST:N], ok[:, :], ALU.add))
            pick_top(dve, link, acc[:, :], best[:, :])
            V.tensor_scalar(acc[:, :], acc[:, :], -3.2e38, NEG, ALU.is_gt, ALU.mult).then_inc(sel, 1)
            dve.wait_ge(biased, 1)
            for n in range(KVH):
                link(V.tensor_reduce(mxa[:, n:n + 1], psX[n][:, :], AX.X, ALU.max))
            t = tmp[:, :, :].rearrange("p n (b j) -> p n b j", j=NT)
            for n in range(KVH):
                link(V.tensor_tensor(t[:, n], psT[0][:, SMP * n:SMP * n + SMP].rearrange("p (b j) -> p b j", j=NT),
                                     bc(own[:, :], 2, NT), ALU.mult))
                link(V.tensor_reduce(new[:, n, :], tmp[:, n, :].rearrange("p (b j) -> p j b", j=NT), AX.X, ALU.add))
                link(V.tensor_tensor(new[:, n, :], new[:, n, :], psT[0][:, 64:64 + NT], ALU.add))
            link(V.tensor_reduce(mxb[:, :], new[:, :, :], AX.X, ALU.max))
            link(V.tensor_tensor(mxa[:, :], mxa[:, :], mxb[:, :], ALU.max))
            V.tensor_scalar(neg[:, :], mxa[:, :], -SC, None, ALU.mult).then_inc(ngd, 1)
            dve.wait_ge(exd, 4)
            link(V.tensor_tensor(tot[:, :], tot[:, :], totb[:, :], ALU.add))
            link(V.reciprocal(tot[:, :], tot[:, :]))
            V.tensor_tensor(pr[:, :, :], pr[:, :, :], bc(tot[:, :], 2, N), ALU.mult).then_inc(pnd, 1)
            dve.wait_ge(pnd, 1)
            for n in range(KVH):
                ins = V.tensor_tensor(pn[:, n, :].rearrange("p (b j) -> p b j", j=NT), bc(pr[:, n, PAST:N], 1, NB),
                                      bc(own[:, :], 2, NT), ALU.mult)
            ins.then_inc(pnd, 1)
            dve.wait_ge(od, NB)
            dve.wait_ge(g_in, 4 * KVH * 16)
            for n in range(KVH):
                V.tensor_tensor(y[:, n], mixed(n), gc[:, n], ALU.mult).then_inc(yd, 1)


OUTS = [(1, SEQ, D), (NB, NT, D), (1, 1, NH, HD, HD), (1, 1, NH, HD), (1, 1, NH), (1, NB, NH, HD, HD),
        (1, NB, NH, HD), (1, NB, NH), (1, NB, NT, NH * HD), (1, 1, SEQ, KVH, HD), (1, 1, SEQ, KVH, HD),
        (1, 1, SEQ, ID), (1, NB, NT, KVH, HD), (1, NB, NT, KVH, HD), (1, NB, NT, ID),
        (2, 1, MEM, NH, HD), (2, 1, MEM, NH, HD)]


class Names:
    pass


def decoder(nc, a, o, stop=99):
    c = Names()
    with Stage(nc, "all") as st, nc.allow_non_contiguous_dma(reason="columns of a few hundred elements"):
        c.ident = st.sb("ident", [P, P])
        c.neg_sj = st.sb("neg_sj", [P, P])
        c.neg_qk = st.sb("neg_qk", [P, P])
        c.lid_qk = st.sb("lid_qk", [P, P])
        c.neg_smp = st.sb("neg_smp", [SMP, SMP])
        c.causal_smp = st.sb("causal_smp", [SMP, SMP])
        c.of_seq = st.sb("of_seq", [P, NB])
        c.seq_cols = st.sb("seq_cols", [P, NB, SMP])
        c.head_row = st.sb("head_row", [NH, NH, P])
        c.tok_of = st.sb("tok_of", [P, SMP])
        c.tok_to = st.sb("tok_to", [SMP, P])
        c.causal = st.sb("causal", [P, P])
        c.half = st.sb("half", [P, 16])
        c.eps = st.sb("eps", [P, 16])
        c.inv_d = st.sb("inv_d", [P, 1])
        c.one = st.sb("one", [P, 1])
        c.inv_hd = st.sb("inv_hd", [P, 16])
        c.keysT = st.sb("mem_keysT", [P, 2, NH, MEM])
        c.vals = st.sb("mem_vals", [P, 2, MC, NH * HD])
        c.gates = st.sb("gates", [P, TOK])
        c.h_even = nc.dram_tensor("h_even", [TOK, W_EVEN], F32).ap()
        c.h_odd = nc.dram_tensor("h_odd", [TOK, W_ODD], F32).ap()
        c.y_even = nc.dram_tensor("y_even", [TOK, 1536], F32).ap()
        c.y_odd = nc.dram_tensor("y_odd", [TOK, 1536], F32).ap()
        c.x1 = nc.dram_tensor("x1", [TOK, D], F32).ap()

        def x0(t, rows):
            if rows == SMP:
                return a["x_sample"].rearrange("b t d -> (b t) d")
            return a["x_prompt"][0, bass.ts(t, P), :]

        def x1(t, rows):
            return c.x1[rows_of(t, rows), :]

        def y_out(t, rows):
            if rows == SMP:
                return o[1].rearrange("b t d -> (b t) d")
            return o[0][0, bass.ts(t, P), :]

        constants(nc, c, st)
        with Stage(nc, "layer0") as L:
            projection_memory(c, L, a["w_even"], a["w_if"])
            normed_transpose(nc, c, "norm0", x0, a["norm_even"])
            if stop < 1: return
            project(nc, c, "proj0", c.h_even,
                    [(3, (ACT.Copy, ACT.Copy)), (1, (ACT.Silu, ACT.Silu)), (1, (ACT.Silu, ACT.Sigmoid))])
            project_gates(nc, c)
        if stop < 2: return
        memory_keys(nc, c, a, o)
        if stop < 3: return
        mlstm(nc, c, a, o)
        if stop < 4: return
        gmlp(nc, c, a, o)
        if stop < 5: return
        with Stage(nc, "end0") as L:
            out_memory(c, L, a["w_out_even"])
            memory_attention(nc, c, a, 0, c.h_even, E_XQ, E_GX, c.y_even, 1024)
            if stop < 6: return
            out_project(nc, c, "out0", c.y_even, x0, x1)
        if stop < 7: return
        with Stage(nc, "layer1") as L:
            projection_memory(c, L, a["w_odd"], a["w_wk"])
            normed_transpose(nc, c, "norm1", x1, a["norm_odd"])
            project(nc, c, "proj1", c.h_odd,
                    [(2, (ACT.Copy, ACT.Copy)), (1, (ACT.Copy, ACT.Silu)), (1, (ACT.Silu, ACT.Silu))])
            project_indexer(nc, c)
        if stop < 8: return
        with Stage(nc, "sparse") as L:
            sparse_memory(c, L)
            sparse_prepare(nc, c, a, o)
            if stop < 9: return
            sparse_prompt(nc, c, a)
            if stop < 10: return
            sparse_sample(nc, c, a)
        if stop < 11: return
        with Stage(nc, "end1") as L:
            out_memory(c, L, a["w_out_odd"])
            memory_attention(nc, c, a, 1, c.h_odd, O_XQ, O_GX, c.y_odd, 1024)
            out_project(nc, c, "out1", c.y_odd, x1, y_out)


def laid_out(inputs):
    f = {n: np.ascontiguousarray(v) for n, v in inputs.items()}

    def chunks(w, columns):
        k = w.reshape(KC, P, -1).transpose(1, 0, 2)
        return np.ascontiguousarray(np.stack([k[:, :, q:q + CW] for q in columns]).reshape(len(columns), P, KC * CW))

    def small(w, columns):
        k = w.reshape(KC, P, -1).transpose(1, 0, 2)
        return np.ascontiguousarray(np.concatenate([k[:, :, q:q + n] for q, n in columns], axis=2))

    we, wo = f["w_in_even"][0], f["w_in_odd"][0]
    r = {n: f[n] for n in ("x_prompt", "x_sample", "state_mlstm_C", "state_mlstm_n", "state_mlstm_m",
                           "cache_attn_k", "cache_attn_v", "cache_idx_k", "cache_mem_k", "cache_mem_v",
                           "page_table", "mem_prompt", "norm_even", "b_if_even", "mlstm_hnorm", "gmlp_ln_g",
                           "gmlp_ln_b", "gmlp_w", "gmlp_b", "norm_odd", "attn_qn", "attn_kn", "mem_qn",
                           "mem_kn")}
    r["w_even"] = chunks(we, [0, 512, 1024, 2568, 3080, 4104, 2056, 3592, 4616, 1536])
    r["w_if"] = small(we, [(2048, 8)])
    r["w_odd"] = chunks(wo, [0, 512, 1024, 2560, 3144, 1536, 2048, 3656])
    r["w_wk"] = small(wo, [(3072, 72)])
    r["w_mem"] = np.stack([chunks(f["w_mem_kv"][l], [0, 512]) for l in range(2)])
    for n in ("even", "odd"):
        r[f"w_out_{n}"] = np.ascontiguousarray(f[f"w_out_{n}"][0].reshape(12, P, D).transpose(1, 0, 2))
    pos = np.arange(TOK, dtype=np.float32)
    pos[SEQ:] = PAST + np.arange(SMP) % NT
    for n, half in (("rope", HD // 8), ("rope_idx", ID // 8)):
        inv = np.float32(500000.0) ** (-np.arange(half, dtype=np.float32) / np.float32(half))
        ang = (pos[:, None] * inv[None, :].astype(np.float32)).astype(np.float32)
        r[n] = np.stack([np.cos(ang), np.sin(ang)], axis=1).astype(np.float32)
    return r


def kernel(**inputs):
    import numpy as _np
    import concourse.bacc as _bacc
    from concourse import mybir as _mybir
    from concourse.bass_utils import run_bass_kernel_spmd as _run

    nc = _bacc.Bacc("TRN2", target_bir_lowering=False, num_devices=1)
    arrays, a = {}, {}
    for name, v in laid_out(inputs).items():
        arrays[f"in_{name}"] = v
        a[name] = nc.dram_tensor(f"in_{name}", v.shape, _mybir.dt.from_np(v.dtype), kind="ExternalInput").ap()
    o = [nc.dram_tensor(f"out_{i}", s, F32, kind="ExternalOutput").ap() for i, s in enumerate(OUTS)]
    decoder(nc, a, o)
    r = _run(nc, [arrays], core_ids=[0])
    return tuple(r.results[0][f"out_{i}"] for i in range(len(OUTS)))
```
